# Optimizing a Trainium2 kernel written in Bass

```python
import math
import jax
import jax.numpy as jnp
from jax import lax
import numpy as np

D_MODEL = 1024
BATCH = 1
SEQ = 512
DEPTH = 2

CTX_LEN = 256
GRID_W = 64
N_MIXERS = 3
N_A_LAYERS = len(range(0, DEPTH, N_MIXERS))
N_B_LAYERS = len(range(1, DEPTH, N_MIXERS))
N_C_LAYERS = len(range(2, DEPTH, N_MIXERS))
DN_ALPHA = (2 * DEPTH) ** 0.25
DN_BETA = (8 * DEPTH) ** -0.25
LN_EPS = 1e-5
NORM_EPS = 1e-6
ADA_CHUNKS = 6

DA_HEADS = 8
DA_HEAD_DIM = D_MODEL // DA_HEADS // 2
ROPE_BASE = 10000.0
Q_BLOCK = 128

GDN_K_HEADS = 8
GDN_V_HEADS = 16
GDN_HEAD_DIM = 128
GDN_KEY_DIM = GDN_K_HEADS * GDN_HEAD_DIM
GDN_VAL_DIM = GDN_V_HEADS * GDN_HEAD_DIM
GDN_CONV_W = 5
GDN_IN_DIM = 2 * GDN_KEY_DIM + 2 * GDN_VAL_DIM + 4 * GDN_V_HEADS
CHUNK = 64

GLA_HEADS = 4
GLA_KEY_DIM = D_MODEL // 2
GLA_VAL_DIM = D_MODEL
GLA_DK = GLA_KEY_DIM // GLA_HEADS
GLA_DV = GLA_VAL_DIM // GLA_HEADS
GLA_GATE_RANK = 16
GLA_TAU = 16.0
GLA_IN_DIM = 2 * GLA_KEY_DIM + 2 * GLA_VAL_DIM + 2 * GLA_GATE_RANK

N_EXPERTS = 64
TOP_K = 8
EXPERT_FF = 256
SHARED_FF = 256
ROUTE_SCALE = 2.5
MOE_BLOCK = 128

kernel_name = 'hybrid_diffattn_gdn_gla_moe_flow_backbone'

F32 = jnp.float32

def layer_norm(x, g, b):
    xf = x.astype(F32)
    mu = jnp.mean(xf, -1, keepdims=True)
    var = jnp.mean(jnp.square(xf - mu), -1, keepdims=True)
    return ((xf - mu) * lax.rsqrt(var + LN_EPS) * g + b).astype(x.dtype)

def rms_norm(x, g):
    xf = x.astype(F32)
    return (xf * lax.rsqrt(jnp.mean(xf * xf, -1, keepdims=True) + NORM_EPS) * g).astype(x.dtype)

def l2_norm(x):
    xf = x.astype(F32)
    return (xf * lax.rsqrt(jnp.sum(xf * xf, -1, keepdims=True) + NORM_EPS)).astype(x.dtype)

def post_norm(res, y, gate, g, b):
    return layer_norm(DN_ALPHA * res + gate * y, g, b)

def axial_rope(n_tok, dim):
    rows = n_tok // GRID_W
    row = jnp.repeat(jnp.arange(rows), GRID_W).astype(F32)
    col = jnp.tile(jnp.arange(GRID_W), rows).astype(F32)
    n_freq = dim // 4
    inv = 1.0 / (ROPE_BASE ** (jnp.arange(n_freq, dtype=F32) / n_freq))
    ang = jnp.concatenate([row[:, None] * inv, col[:, None] * inv], -1)
    return jnp.cos(ang), jnp.sin(ang)

def apply_rope(x, cos, sin):
    x1, x2 = jnp.split(x, 2, -1)
    cs = cos[:, None, None, :]
    sn = sin[:, None, None, :]
    return jnp.concatenate([x1 * cs - x2 * sn, x1 * sn + x2 * cs], -1).astype(x.dtype)

def short_conv(x, w):
    ch = x.shape[-1]
    pad = GDN_CONV_W // 2
    return lax.conv_general_dilated(x, w[:, None, :].astype(x.dtype), window_strides=(1,),
                                    padding=[(pad, pad)], dimension_numbers=('NWC', 'WIO', 'NWC'),
                                    feature_group_count=ch)

def to_chunks(t):
    b, l, h = t.shape[:3]
    t = jnp.moveaxis(t, 2, 1)
    return t.reshape(b, h, l // CHUNK, CHUNK, *t.shape[3:])

def from_chunks(t):
    b, h, n, c, d = t.shape
    return jnp.moveaxis(t.reshape(b, h, n * c, d), 1, 2)

def gdn_chunked(q, k, v, g, beta, s0):
    out_dtype = v.dtype
    q, k, v = (to_chunks(t.astype(F32)) for t in (q, k, v))
    g, beta = to_chunks(g.astype(F32)), to_chunks(beta.astype(F32))
    tril = jnp.tril(jnp.ones((CHUNK, CHUNK), bool))
    strict = jnp.tril(jnp.ones((CHUNK, CHUNK), bool), -1)
    eye = jnp.eye(CHUNK, dtype=F32)
    gcum = jnp.cumsum(g, -1)
    decay = jnp.where(tril, jnp.exp(jnp.where(tril, gcum[..., :, None] - gcum[..., None, :], 0.0)), 0.0)
    kb = k * beta[..., None]
    m = jnp.where(strict, jnp.einsum('bhncd,bhnsd->bhncs', kb, k) * decay, 0.0)
    tmat = lax.linalg.triangular_solve(eye + m, jnp.broadcast_to(eye, m.shape), left_side=True, lower=True)
    u = tmat @ (v * beta[..., None])
    w = tmat @ (kb * jnp.exp(gcum)[..., None])
    attn = jnp.where(tril, jnp.einsum('bhncd,bhnsd->bhncs', q, k) * decay, 0.0)
    qg = q * jnp.exp(gcum)[..., None]
    kg = k * jnp.exp(gcum[..., -1:] - gcum)[..., None]
    glast = jnp.exp(gcum[..., -1])

    def step(state, xs):
        u_i, w_i, qg_i, kg_i, a_i, gl_i = xs
        v_new = u_i - w_i @ state
        o = qg_i @ state + a_i @ v_new
        state = state * gl_i[..., None, None] + jnp.swapaxes(kg_i, -1, -2) @ v_new
        return state, o

    xs = tuple(jnp.moveaxis(t, 2, 0) for t in (u, w, qg, kg, attn, glast))
    state, o = lax.scan(step, s0, xs)
    return from_chunks(jnp.moveaxis(o, 0, 2)).astype(out_dtype), state

def gla_chunked(q, k, v, glog, s0):
    out_dtype = v.dtype
    q, k, v, glog = (to_chunks(t.astype(F32)) for t in (q, k, v, glog))
    tril = jnp.tril(jnp.ones((CHUNK, CHUNK), bool))
    bcum = jnp.cumsum(glog, -2)
    qe = q * jnp.exp(bcum)
    ke = k * jnp.exp(-bcum)
    attn = jnp.where(tril, jnp.einsum('bhncd,bhnsd->bhncs', qe, ke), 0.0)
    o_intra = attn @ v
    kg = k * jnp.exp(bcum[..., -1:, :] - bcum)
    glast = jnp.exp(bcum[..., -1, :])

    def step(state, xs):
        qe_i, kg_i, v_i, gl_i = xs
        o = qe_i @ state
        state = state * gl_i[..., :, None] + jnp.swapaxes(kg_i, -1, -2) @ v_i
        return state, o

    xs = tuple(jnp.moveaxis(t, 2, 0) for t in (qe, kg, v, glast))
    state, o_inter = lax.scan(step, s0, xs)
    o = o_intra + jnp.moveaxis(o_inter, 0, 2)
    return from_chunks(o).astype(out_dtype), state

def diff_attention(h_lat, h_ctx, w_in, w_o, lam_vec, subln, lam_init, rope, need_ctx):
    b, n, _ = h_lat.shape
    hh, d = DA_HEADS, DA_HEAD_DIM

    def proj(h):
        q, k, v = jnp.split(h @ w_in, 3, -1)
        l = h.shape[1]
        return q.reshape(b, l, hh, 2, d), k.reshape(b, l, hh, 2, d), v.reshape(b, l, hh, 2 * d)

    ql, kl, vl = proj(h_lat)
    qc, kc, vc = proj(h_ctx)
    cos, sin = rope
    ql = apply_rope(ql, cos, sin)
    kl = apply_rope(kl, cos, sin)
    lv = lam_vec.astype(F32)
    lam = jnp.exp(jnp.sum(lv[0] * lv[1])) - jnp.exp(jnp.sum(lv[2] * lv[3])) + lam_init
    k_all = jnp.concatenate([kc, kl], 1)
    v_all = jnp.concatenate([vc, vl], 1)

    def attend(q, k, v):
        s = jnp.einsum('bqhcd,bkhcd->bhcqk', q, k).astype(F32) * (d ** -0.5)
        p = jax.nn.softmax(s, -1)
        a = (p[:, :, 0] - lam * p[:, :, 1]).astype(v.dtype)
        return jnp.einsum('bhqk,bkhe->bqhe', a, v)

    qb = jnp.swapaxes(ql.reshape(b, n // Q_BLOCK, Q_BLOCK, hh, 2, d), 0, 1)
    ol = lax.map(lambda qblk: attend(qblk, k_all, v_all), qb)
    ol = jnp.swapaxes(ol, 0, 1).reshape(b, n, hh, 2 * d)

    def out(o):
        o = rms_norm(o, subln) * (1.0 - lam_init)
        return o.reshape(o.shape[0], o.shape[1], -1) @ w_o

    y_ctx = out(attend(qc, kc, vc)) if need_ctx else None
    return out(ol), y_ctx

def gated_deltanet(h_lat, h_ctx, w_in, conv_w, a_log, dt_bias, norm_g, w_o, need_ctx):
    hk, hv, dh = GDN_K_HEADS, GDN_V_HEADS, GDN_HEAD_DIM

    def prep(h):
        b, l, _ = h.shape
        p = h @ w_in
        qkv, z, a, bb = jnp.split(p, [2 * GDN_KEY_DIM + GDN_VAL_DIM, 2 * GDN_KEY_DIM + 2 * GDN_VAL_DIM,
                                      2 * GDN_KEY_DIM + 2 * GDN_VAL_DIM + 2 * hv], -1)
        qkv = jax.nn.silu(short_conv(qkv, conv_w))
        q, k, v = jnp.split(qkv, [GDN_KEY_DIM, 2 * GDN_KEY_DIM], -1)
        q = l2_norm(q.reshape(b, l, hk, dh)) * (dh ** -0.5)
        k = l2_norm(k.reshape(b, l, hk, dh))
        q = jnp.repeat(q, hv // hk, axis=2)
        k = jnp.repeat(k, hv // hk, axis=2)
        v = v.reshape(b, l, hv, dh)
        a = a.astype(F32).reshape(b, l, 2, hv)
        g = -jnp.exp(a_log.astype(F32)) * jax.nn.softplus(a + dt_bias.astype(F32))
        beta = jax.nn.sigmoid(bb.astype(F32).reshape(b, l, 2, hv))
        return q, k, v, z.reshape(b, l, hv, dh), g, beta

    def flip(t):
        return jnp.flip(t, 1)

    qc, kc, vc, zc, gc, bc = prep(h_ctx)
    ql, kl, vl, zl, gl, bl = prep(h_lat)
    s0 = jnp.zeros((h_lat.shape[0], hv, dh, dh), F32)
    oc_f, sc_f = gdn_chunked(qc, kc, vc, gc[:, :, 0], bc[:, :, 0], s0)
    oc_b, sc_b = gdn_chunked(flip(qc), flip(kc), flip(vc), flip(gc[:, :, 1]), flip(bc[:, :, 1]), s0)
    ol_f, _ = gdn_chunked(ql, kl, vl, gl[:, :, 0], bl[:, :, 0], sc_f)
    ol_b, _ = gdn_chunked(flip(ql), flip(kl), flip(vl), flip(gl[:, :, 1]), flip(bl[:, :, 1]), sc_b)

    def out(o, z):
        o = rms_norm(o, norm_g) * jax.nn.silu(z)
        return o.reshape(o.shape[0], o.shape[1], -1) @ w_o

    y_ctx = out(oc_f + flip(oc_b), zc) if need_ctx else None
    return out(ol_f + flip(ol_b), zl), y_ctx

def gla_mixer(h_lat, h_ctx, w_in, w_gate, gate_b, norm_g, w_o, need_ctx):
    hh, dk, dv = GLA_HEADS, GLA_DK, GLA_DV

    def prep(h):
        b, l, _ = h.shape
        p = h @ w_in
        q, k, v, r, gr = jnp.split(p, [GLA_KEY_DIM, 2 * GLA_KEY_DIM, 2 * GLA_KEY_DIM + GLA_VAL_DIM,
                                       2 * GLA_KEY_DIM + 2 * GLA_VAL_DIM], -1)
        q = q.reshape(b, l, hh, dk) * (dk ** -0.5)
        k = k.reshape(b, l, hh, dk)
        v = v.reshape(b, l, hh, dv)
        gr = gr.reshape(b, l, 2, GLA_GATE_RANK)
        glog = jax.nn.log_sigmoid(jnp.einsum('blzr,zrk->blzk', gr, w_gate).astype(F32) + gate_b.astype(F32)) / GLA_TAU
        return q, k, v, r.reshape(b, l, hh, dv), glog.reshape(b, l, 2, hh, dk)

    def flip(t):
        return jnp.flip(t, 1)

    qc, kc, vc, rc, gc = prep(h_ctx)
    ql, kl, vl, rl, gl = prep(h_lat)
    s0 = jnp.zeros((h_lat.shape[0], hh, dk, dv), F32)
    oc_f, sc_f = gla_chunked(qc, kc, vc, gc[:, :, 0], s0)
    oc_b, sc_b = gla_chunked(flip(qc), flip(kc), flip(vc), flip(gc[:, :, 1]), s0)
    ol_f, _ = gla_chunked(ql, kl, vl, gl[:, :, 0], sc_f)
    ol_b, _ = gla_chunked(flip(ql), flip(kl), flip(vl), flip(gl[:, :, 1]), sc_b)

    def out(o, r):
        o = rms_norm(o, norm_g) * jax.nn.silu(r)
        return o.reshape(o.shape[0], o.shape[1], -1) @ w_o

    y_ctx = out(oc_f + flip(oc_b), rc) if need_ctx else None
    return out(ol_f + flip(ol_b), rl), y_ctx

def moe_ffn(h, router_w, router_b, w_gu, w_dn, ws_gu, ws_dn):
    t, d = h.shape
    e = w_gu.shape[0]
    scores = jax.nn.sigmoid((h @ router_w).astype(F32))
    _, idx = lax.top_k(scores + router_b.astype(F32), TOP_K)
    wt = jnp.take_along_axis(scores, idx, -1)
    wt = wt / jnp.sum(wt, -1, keepdims=True) * ROUTE_SCALE
    n_pairs = t * TOP_K
    flat_e = idx.reshape(-1)
    order = jnp.argsort(flat_e)
    e_sorted = flat_e[order]
    sizes = jnp.bincount(flat_e, length=e)
    padded = (sizes + MOE_BLOCK - 1) // MOE_BLOCK * MOE_BLOCK
    pad_end = jnp.cumsum(padded)
    pad_start = pad_end - padded
    start = jnp.cumsum(sizes) - sizes
    dest = pad_start[e_sorted] + jnp.arange(n_pairs) - start[e_sorted]
    n_blocks = (n_pairs + e * (MOE_BLOCK - 1) + MOE_BLOCK - 1) // MOE_BLOCK
    n_slots = n_blocks * MOE_BLOCK
    slot_tok = jnp.full((n_slots,), t, jnp.int32).at[dest].set((order // TOP_K).astype(jnp.int32))
    slot_w = jnp.zeros((n_slots,), F32).at[dest].set(wt.reshape(-1)[order])
    block_e = jnp.minimum(jnp.searchsorted(pad_end, jnp.arange(n_blocks) * MOE_BLOCK, side='right'), e - 1)
    h_pad = jnp.concatenate([h, jnp.zeros((1, d), h.dtype)], 0)

    def step(acc, xs):
        tok, wgt, ex = xs
        xb = h_pad[tok]
        g, u = jnp.split(xb @ w_gu[ex], 2, -1)
        yb = ((jax.nn.silu(g) * u) @ w_dn[ex]) * wgt[:, None].astype(h.dtype)
        return acc.at[tok].add(yb), None

    acc, _ = lax.scan(step, jnp.zeros((t + 1, d), h.dtype),
                      (slot_tok.reshape(n_blocks, MOE_BLOCK), slot_w.reshape(n_blocks, MOE_BLOCK), block_e))
    gs, us = jnp.split(h @ ws_gu, 2, -1)
    return acc[:t] + (jax.nn.silu(gs) * us) @ ws_dn

def setup_inputs(seed: int = 0) -> dict:
    key = jax.random.key(seed)
    ks = iter(jax.random.split(key, 40))
    nrm = lambda shape, s: jax.random.normal(next(ks), shape, F32) * s
    gain = lambda shape: 1.0 + nrm(shape, 0.02)
    dt = jnp.exp(jax.random.uniform(next(ks), (N_B_LAYERS, 2, GDN_V_HEADS), F32, math.log(1e-3), math.log(1e-1)))
    return {
        'x': nrm((BATCH, SEQ, D_MODEL), 1.0),
        'c': nrm((BATCH, D_MODEL), 1.0),
        'ctx': nrm((BATCH, CTX_LEN, D_MODEL), 1.0),
        'c_ctx': nrm((D_MODEL,), 1.0),
        'ada_w': nrm((DEPTH, D_MODEL, ADA_CHUNKS * D_MODEL), 0.5 * D_MODEL ** -0.5),
        'ada_b': nrm((DEPTH, ADA_CHUNKS * D_MODEL), 0.02),
        'ln_g': gain((DEPTH, 2, D_MODEL)),
        'ln_b': nrm((DEPTH, 2, D_MODEL), 0.02),
        'da_w_in': nrm((N_A_LAYERS, D_MODEL, 3 * D_MODEL), D_MODEL ** -0.5),
        'da_w_o': nrm((N_A_LAYERS, D_MODEL, D_MODEL), DN_BETA * D_MODEL ** -0.5),
        'da_lambda': nrm((N_A_LAYERS, 4, DA_HEAD_DIM), 0.1),
        'da_subln': gain((N_A_LAYERS, 2 * DA_HEAD_DIM)),
        'gdn_w_in': nrm((N_B_LAYERS, D_MODEL, GDN_IN_DIM), D_MODEL ** -0.5),
        'gdn_conv': nrm((N_B_LAYERS, GDN_CONV_W, 2 * GDN_KEY_DIM + GDN_VAL_DIM), GDN_CONV_W ** -0.5),
        'gdn_a_log': jnp.log(jax.random.uniform(next(ks), (N_B_LAYERS, 2, GDN_V_HEADS), F32, 1.0, 16.0)),
        'gdn_dt_bias': dt + jnp.log(-jnp.expm1(-dt)),
        'gdn_norm': gain((N_B_LAYERS, GDN_HEAD_DIM)),
        'gdn_w_o': nrm((N_B_LAYERS, GDN_VAL_DIM, D_MODEL), DN_BETA * GDN_VAL_DIM ** -0.5),
        'gla_w_in': nrm((N_C_LAYERS, D_MODEL, GLA_IN_DIM), D_MODEL ** -0.5),
        'gla_w_gate': nrm((N_C_LAYERS, 2, GLA_GATE_RANK, GLA_KEY_DIM), GLA_GATE_RANK ** -0.5),
        'gla_gate_b': nrm((N_C_LAYERS, 2, GLA_KEY_DIM), 0.1),
        'gla_norm': gain((N_C_LAYERS, GLA_DV)),
        'gla_w_o': nrm((N_C_LAYERS, GLA_VAL_DIM, D_MODEL), DN_BETA * GLA_VAL_DIM ** -0.5),
        'moe_router': nrm((DEPTH, D_MODEL, N_EXPERTS), D_MODEL ** -0.5),
        'moe_router_b': nrm((DEPTH, N_EXPERTS), 0.01),
        'moe_w_gu': nrm((DEPTH, N_EXPERTS, D_MODEL, 2 * EXPERT_FF), D_MODEL ** -0.5),
        'moe_w_dn': nrm((DEPTH, N_EXPERTS, EXPERT_FF, D_MODEL), DN_BETA * EXPERT_FF ** -0.5),
        'moe_ws_gu': nrm((DEPTH, D_MODEL, 2 * SHARED_FF), D_MODEL ** -0.5),
        'moe_ws_dn': nrm((DEPTH, SHARED_FF, D_MODEL), DN_BETA * SHARED_FF ** -0.5),
    }

def reference(x, c, ctx, c_ctx, ada_w, ada_b, ln_g, ln_b, da_w_in, da_w_o, da_lambda, da_subln,
              gdn_w_in, gdn_conv, gdn_a_log, gdn_dt_bias, gdn_norm, gdn_w_o,
              gla_w_in, gla_w_gate, gla_gate_b, gla_norm, gla_w_o,
              moe_router, moe_router_b, moe_w_gu, moe_w_dn, moe_ws_gu, moe_ws_dn):
    b, n, d = x.shape
    lc = ctx.shape[1]
    rope = axial_rope(n, DA_HEAD_DIM)
    s_lat = jax.nn.silu(c)
    s_ctx = jax.nn.silu(c_ctx)
    for i in range(DEPTH):
        kind, j = i % N_MIXERS, i // N_MIXERS
        need_ctx = i < DEPTH - 1
        m_lat = jnp.split((s_lat @ ada_w[i] + ada_b[i])[:, None, :], ADA_CHUNKS, -1)
        m_ctx = jnp.split((s_ctx @ ada_w[i] + ada_b[i])[None, None, :], ADA_CHUNKS, -1)
        h_lat = x * (1 + m_lat[1]) + m_lat[0]
        h_ctx = ctx * (1 + m_ctx[1]) + m_ctx[0]
        if kind == 0:
            lam_init = 0.8 - 0.6 * math.exp(-0.3 * i)
            y_lat, y_ctx = diff_attention(h_lat, h_ctx, da_w_in[j], da_w_o[j], da_lambda[j], da_subln[j],
                                          lam_init, rope, need_ctx)
        elif kind == 1:
            y_lat, y_ctx = gated_deltanet(h_lat, h_ctx, gdn_w_in[j], gdn_conv[j], gdn_a_log[j], gdn_dt_bias[j],
                                          gdn_norm[j], gdn_w_o[j], need_ctx)
        else:
            y_lat, y_ctx = gla_mixer(h_lat, h_ctx, gla_w_in[j], gla_w_gate[j], gla_gate_b[j], gla_norm[j],
                                     gla_w_o[j], need_ctx)
        x = post_norm(x, y_lat, m_lat[2], ln_g[i, 0], ln_b[i, 0])
        h_lat = x * (1 + m_lat[4]) + m_lat[3]
        moe_args = (moe_router[i], moe_router_b[i], moe_w_gu[i], moe_w_dn[i], moe_ws_gu[i], moe_ws_dn[i])
        if need_ctx:
            ctx = post_norm(ctx, y_ctx, m_ctx[2], ln_g[i, 0], ln_b[i, 0])
            h_ctx = ctx * (1 + m_ctx[4]) + m_ctx[3]
            n_ctx = b * lc
            f = moe_ffn(jnp.concatenate([h_ctx.reshape(n_ctx, d), h_lat.reshape(b * n, d)], 0), *moe_args)
            ctx = post_norm(ctx, f[:n_ctx].reshape(b, lc, d), m_ctx[5], ln_g[i, 1], ln_b[i, 1])
            f_lat = f[n_ctx:].reshape(b, n, d)
        else:
            f_lat = moe_ffn(h_lat.reshape(b * n, d), *moe_args).reshape(b, n, d)
        x = post_norm(x, f_lat, m_lat[5], ln_g[i, 1], ln_b[i, 1])
    return x


_drawn_inputs = setup_inputs


def setup_inputs(seed=0):
    import zlib

    import numpy as np

    out = dict(_drawn_inputs(seed))
    spreads = {}
    factors = {'da_lambda': 5.223,
     'da_subln': 22.689,
     'gdn_a_log': 4.413,
     'gdn_norm': 107.485,
     'gdn_dt_bias': 3.281}
    for name, (base, spread) in spreads.items():
        noise = np.random.default_rng([zlib.crc32(name.encode()), seed]).standard_normal(out[name].shape)
        drawn = base * np.exp(spread * noise) if base else spread * noise
        out[name] = jnp.asarray(drawn.astype(out[name].dtype))
    for name, factor in factors.items():
        out[name] = (out[name] * factor).astype(out[name].dtype)
    return out
```

```python
from collections import namedtuple
from contextlib import ExitStack, contextmanager
import math

import numpy as np
import concourse.bass as bass
from concourse import mybir

F32 = mybir.dt.float32
I32 = mybir.dt.int32
ACT = mybir.ActivationFunctionType
ALU = mybir.AluOpType
AX = mybir.AxisListType
ds = bass.ds

P = 128
BANK = 512
D = 1024
KD = D // P
SEQ, CTX_LEN, DEPTH = 512, 256, 2
CTX_TILES, LAT_TILES = CTX_LEN // P, SEQ // P
TILES = CTX_TILES + LAT_TILES
TOKENS = TILES * P
DN_ALPHA = (2 * DEPTH) ** 0.25
LN_EPS, NORM_EPS = 1e-5, 1e-6
ADA = 6

DA_HEADS = 8
DA_DIM = D // DA_HEADS // 2
LAM_INIT = 0.8 - 0.6 * math.exp(-0.3 * 0)

HK, HV, DH = 8, 16, 128
VPK = HV // HK
GDN_KEY, GDN_VAL = HK * DH, HV * DH
CONV_W = 5
GDN_Z0 = 2 * GDN_KEY + GDN_VAL
GDN_A0 = GDN_Z0 + GDN_VAL

E, TOP_K, FF = 64, 8, 256
ROUTE_SCALE = 2.5


def named(kind, **values):
    return namedtuple(kind, list(values))(**values)


class Core:
    pass


class Own:

    def __init__(self, eng, sem):
        self.eng, self.sem, self.n, self.base = eng, sem, 0, 0

    def __call__(self, ins):
        self.mark(ins)
        self.wait()

    def mark(self, ins):
        ins.then_inc(self.sem, 1)
        self.n += 1

    def wait(self):
        self.eng.wait_ge(self.sem, self.base + self.n)

    def enter(self, i, per):
        self.before, self.per, self.base, self.n = self.base + self.n, per, self.base + self.n + i * per, 0

    def leave(self, count):
        assert self.n == self.per, f"{self.n} counted in the loop's body, {self.per} announced"
        self.base, self.n = self.before + count * self.per, 0


def bc(ap, shape):
    return ap.to_broadcast(shape)


def stream_of(t):
    return 1 if t < CTX_TILES else 0


def load_constants(nc, g, sem):
    landed, lam_dot, lam_exp, own_sem = sem("const_landed"), sem("lam_dot"), sem("lam_exp"), sem("const_own")
    zeroed, rows_zero = sem("const_zeroed"), sem("const_rows_zero")
    with nc.sbuf_tensor("zero_row", [P, D], F32) as zero, nc.sbuf_tensor("lam_in", [P, 4, DA_DIM], F32) as lam_in, \
            nc.sbuf_tensor("lam_tmp", [P, 2, DA_DIM], F32) as lam_tmp, \
            nc.sbuf_tensor("lam_s", [P, 2], F32) as lam_s, nc.Block() as block:
        loads = [(g.x[:, CTX_TILES:, :], g.d.x[0].rearrange("(t p) n -> p t n", p=P)),
                 (g.x[:, 0:CTX_TILES, :], g.d.ctx[0].rearrange("(t p) n -> p t n", p=P)),
                 (g.ident[:], g.d.c_ident), (g.upper[:], g.d.c_upper), (g.ones[:], g.d.c_ones),
                 (lam_in[:], g.d.da_lambda[0].partition_broadcast(P)),
                 (g.subln[:], g.d.da_subln[0].partition_broadcast(P)),
                 (g.gdn_gain[:], g.d.gdn_norm[0].partition_broadcast(P))]

        @block.sync
        def _(sp):
            for dst, src in loads:
                sp.dma_start(dst, src).then_inc(landed, 16)
            sp.wait_ge(zeroed, 1)
            for rows in (g.h_d[TOKENS:], g.acc_d[TOKENS:]):
                sp.dma_start(rows, zero[:]).then_inc(rows_zero, 16)
            sp.wait_ge(rows_zero, 32)

        @block.vector
        def _(dve):
            own = Own(dve, own_sem)
            nc.vector.memset(zero[:], 0.0).then_inc(zeroed, 1)
            dve.wait_ge(landed, 16 * len(loads))
            for a in range(2):
                own(nc.vector.tensor_tensor(lam_tmp[:, a], lam_in[:, 2 * a], lam_in[:, 2 * a + 1], ALU.mult))
            nc.vector.tensor_reduce(lam_s[:], lam_tmp[:], AX.X, ALU.add).then_inc(lam_dot, 1)
            own(nc.vector.tensor_scalar(g.subln[:], g.subln[:], 1.0 - LAM_INIT, None, ALU.mult))
            dve.wait_ge(lam_exp, 1)
            nc.vector.scalar_tensor_tensor(out=g.neg_lam[:], in0=lam_s[:, 1:2], scalar=-LAM_INIT,
                                           in1=lam_s[:, 0:1], op0=ALU.add, op1=ALU.subtract)

        @block.scalar
        def _(act):
            act.wait_ge(lam_dot, 1)
            nc.scalar.activation(lam_s[:], lam_s[:], ACT.Exp).then_inc(lam_exp, 1)


def modulation_vectors(nc, g, sem):
    NB = 3
    chunks = DEPTH * ADA * D // BANK
    c_in, c_silu, b_in = sem("ada_c_in"), sem("ada_c_silu"), sem("ada_b_in")
    w_in = [sem(f"ada_w_in{s}") for s in range(NB)]
    prod, added, stored = sem("ada_prod"), sem("ada_added"), sem("ada_stored")
    with nc.sbuf_tensor("ada_wb", [P, NB, KD, BANK], F32) as wb, \
            nc.sbuf_tensor("ada_c", [P, 2, KD], F32) as cs, \
            nc.sbuf_tensor("ada_bias", [2, DEPTH * ADA * D], F32) as bias, \
            nc.psum_tensor("ada_ps", [P, NB, BANK], F32) as ps, nc.Block() as block:
        per_layer = ADA * D // BANK
        w_dram = g.d.ada_w.rearrange("l (p k) (c n) -> l c p k n", k=KD, n=BANK)

        @block.sync
        def _(sp):
            sp.dma_start(cs[:, 0, :], g.d.c.rearrange("a (p k) -> p (a k)", k=KD)).then_inc(c_in, 16)
            sp.dma_start(cs[:, 1, :], g.d.c_ctx.rearrange("(p k) -> p k", k=KD)).then_inc(c_in, 16)
            sp.dma_start(bias[:], g.d.ada_b.rearrange("l n -> (l n)").partition_broadcast(2)).then_inc(b_in, 16)
            for n in range(NB):
                sp.dma_start(wb[:, n], w_dram[0, n]).then_inc(w_in[n], 16)
            for l in range(DEPTH):
                first = NB if l == 0 else 0
                with sp.Fori(0, (per_layer - first) // NB) as i:
                    for s in range(NB):
                        sp.wait_ge(prod, i * NB + (per_layer * l + first + s - NB + 1))
                        sp.dma_start(wb[:, s], w_dram[l, i * NB + (first + s)]).then_inc(w_in[s], 16)
            sp.wait_ge(added, chunks)
            sp.dma_start(g.mod_d, bias[:]).then_inc(stored, 16)
            sp.wait_ge(stored, 16)

        @block.scalar
        def _(act):
            act.wait_ge(c_in, 32)
            nc.scalar.activation(cs[:], cs[:], ACT.Silu).then_inc(c_silu, 1)

        @block.tensor
        def _(pe):
            pe.wait_ge(c_silu, 1)

            def chunk(s, landed, bank_read):
                pe.wait_ge(w_in[s], landed)
                if bank_read is not None:
                    pe.wait_ge(added, bank_read)
                for k in range(KD):
                    last = nc.tensor.matmul(ps[0:2, s], cs[:, :, k], wb[:, s, k], start=(k == 0), stop=(k == KD - 1))
                last.then_inc(prod, 1)

            for s in range(NB):
                chunk(s, 16, None)
            with pe.Fori(0, chunks // NB - 1) as i:
                for s in range(NB):
                    chunk(s, i * 16 + 32, i * NB + (s + 1))

        @block.vector
        def _(dve):
            dve.wait_ge(b_in, 16)
            with dve.Fori(0, chunks // NB) as i:
                for s in range(NB):
                    dve.wait_ge(prod, i * NB + (s + 1))
                    row = bias[:, ds(i * (NB * BANK) + s * BANK, BANK)]
                    nc.vector.tensor_tensor(row, ps[0:2, s], row, ALU.add).then_inc(added, 1)


def modulate(nc, g, sem, layer, sub, tiles, h_dram):
    tag = f"{layer}{sub}"
    vec_in, h_done, tr_done, evac = sem("mod_in" + tag), sem("mod_h" + tag), sem("mod_tr" + tag), sem("mod_evac" + tag)
    own_sem, h_out = sem("mod_own" + tag), [sem(f"mod_out{tag}_{s}") for s in range(2)]
    streams = sorted({stream_of(t) for t in tiles})
    with nc.sbuf_tensor("mod_htok" + tag, [P, 2, D], F32) as ht, nc.sbuf_tensor("mod_vec" + tag, [P, 2, 2, D], F32) as vec, \
            nc.psum_tensor("mod_ps" + tag, [P, 4, 4, P], F32) as ps, nc.Block() as block:
        @block.sync
        def _(sp):
            for s in streams:
                a = (layer * ADA + 3 * sub) * D
                sp.dma_start(vec[:, s], g.mod_d[s, a:a + 2 * D].partition_broadcast(P)).then_inc(vec_in, 16)
            if h_dram:
                for n, t in enumerate(tiles):
                    sp.wait_ge(h_done, n + 1)
                    sp.dma_start(g.h_d[t * P:(t + 1) * P, :], ht[:, n % 2]).then_inc(h_out[n % 2], 16)
                for s in range(2):
                    sp.wait_ge(h_out[s], 16 * ((len(tiles) + 1 - s) // 2))

        @block.vector
        def _(dve):
            own = Own(dve, own_sem)
            dve.wait_ge(vec_in, 16 * len(streams))
            for n, t in enumerate(tiles):
                s = stream_of(t)
                if n >= 2:
                    dve.wait_ge(tr_done, 2 * (n - 1))
                    if h_dram:
                        dve.wait_ge(h_out[n % 2], 16 * (n // 2))
                own(nc.vector.scalar_tensor_tensor(out=ht[:, n % 2], in0=vec[:, s, 1], scalar=1.0,
                                                   in1=g.x[:, t], op0=ALU.add, op1=ALU.mult))
                nc.vector.tensor_tensor(ht[:, n % 2], ht[:, n % 2], vec[:, s, 0], ALU.add).then_inc(h_done, 1)

        @block.tensor
        def _(pe):
            for n, t in enumerate(tiles):
                pe.wait_ge(h_done, n + 1)
                for half in range(2):
                    b = 2 * n + half
                    if b >= 4:
                        pe.wait_ge(evac, b - 3)
                    for q in range(4):
                        last = nc.tensor.transpose(ps[:, b % 4, q], ht[:, n % 2, 4 * half + q::KD], g.ident[:])
                    last.then_inc(tr_done, 1)

        @block.scalar
        def _(act):
            for n, t in enumerate(tiles):
                for half in range(2):
                    b = 2 * n + half
                    act.wait_ge(tr_done, b + 1)
                    nc.scalar.activation(g.hT[:, 4 * half:4 * half + 4, t * P:(t + 1) * P], ps[:, b % 4],
                                         ACT.Copy).then_inc(evac, 1)


def diff_attention(nc, g, sem, o_tok):
    w_in, proj, rotated, v_copied = sem("da_w_in"), sem("da_proj"), sem("da_rotated"), sem("da_v_copied")
    qk_turned, qk_copied = sem("da_qk_turned"), sem("da_qk_copied")
    scored, maxed, exped = sem("da_scored"), sem("da_maxed"), sem("da_exped")
    mixed, a_turned, a_copied, pv_done = sem("da_mixed"), sem("da_a_turned"), sem("da_a_copied"), sem("da_pv")
    o_kept, own_sem, tables_in = sem("da_o_kept"), sem("da_own"), sem("da_tables")
    KEYS = TOKENS
    SCALE = DA_DIM ** -0.5
    with ExitStack() as c:
        sb = lambda name, shape: c.enter_context(nc.sbuf_tensor("da_" + name, shape, F32))
        w = sb("w", [P, KD, 3 * P])
        cc, ss = sb("cc", [P, LAT_TILES, DA_DIM]), sb("ss", [P, LAT_TILES, DA_DIM])
        rot, rt1, rt2 = sb("rot", [P, 2, 4, DA_DIM]), sb("rt1", [P, 4, DA_DIM]), sb("rt2", [P, 4, DA_DIM])
        qT, kT, v = sb("qT", [P, KEYS]), sb("kT", [P, KEYS]), sb("v", [P, TILES, P])
        prob = sb("prob", [P, 2, 2, KEYS])
        diff = sb("diff", [P, KEYS])
        aT = sb("aT", [P, 2, TILES, P])
        mx, nb, l, r = (sb(n, [P, 2, 2]) for n in ("mx", "nb", "l", "r"))
        ps = c.enter_context(nc.psum_tensor("da_ps", [P, 8, BANK], F32))
        s_ps = [ps[:, 0:2].rearrange("p a b -> p (a b)"), ps[:, 2:4].rearrange("p a b -> p (a b)")]
        at_ps = ps[:, 4:6].rearrange("p a (b q) -> p (a b) q", q=P)
        block = c.enter_context(nc.Block())
        w_dram = g.d.da_w_in[0].rearrange("(p k) (m h n) -> p k m h n", k=KD, m=3, n=P)

        def keys(t):
            return CTX_LEN if t < CTX_TILES else KEYS

        @block.sync
        def _(sp):
            sp.dma_start(cc[:], g.d.c_cos).then_inc(tables_in, 16)
            sp.dma_start(ss[:], g.d.c_sin).then_inc(tables_in, 16)
            wv = w[:].rearrange("p k (m n) -> p k m n", m=3)
            for m in range(3):
                sp.dma_start(wv[:, :, m], w_dram[:, :, m, 0]).then_inc(w_in, 16)
            with sp.Fori(0, DA_HEADS - 1) as i:
                sp.wait_ge(proj, i * TILES + TILES)
                for m in range(3):
                    sp.dma_start(wv[:, :, m], w_dram[:, :, m, i + 1]).then_inc(w_in, 16)

        @block.tensor
        def _(pe):
            with pe.Fori(0, DA_HEADS) as i:
                def project(t):
                    if t == 0:
                        pe.wait_ge(w_in, i * 48 + 48)
                    if t >= 2:
                        pe.wait_ge(rotated, i * TILES + (t - 1))
                        pe.wait_ge(v_copied, i * TILES + (t - 1))
                    for k in range(KD):
                        last = nc.tensor.matmul(ps[:, t % 2, 0:3 * P], g.hT[:, k, t * P:(t + 1) * P], w[:, k],
                                                start=(k == 0), stop=(k == KD - 1))
                    last.then_inc(proj, 1)

                def turn_qk(t):
                    pe.wait_ge(rotated, i * TILES + (t + 1))
                    if t >= 2:
                        pe.wait_ge(qk_copied, i * TILES + (t - 1))
                    for m in range(2):
                        last = nc.tensor.transpose(
                            ps[:, 2 + t % 2, m * P:(m + 1) * P],
                            rot[:, t % 2, 2 * m:2 * m + 2].rearrange("p a b -> p (a b)"), g.ident[:])
                    last.then_inc(qk_turned, 1)

                def score(t, comp):
                    if t == 0:
                        pe.wait_ge(qk_copied, i * TILES + TILES)
                    else:
                        pe.wait_ge(exped, i * (2 * TILES) + (2 * (t - 1) + comp + 1))
                    rows = slice(DA_DIM * comp, DA_DIM * (comp + 1))
                    for a in range(0, keys(t), BANK):
                        n = min(BANK, keys(t) - a)
                        last = nc.tensor.matmul(s_ps[comp][:, a:a + n], qT[rows, t * P:(t + 1) * P],
                                                kT[rows, a:a + n], start=True, stop=True)
                    last.then_inc(scored, 1)

                def turn_a(t):
                    pe.wait_ge(mixed, i * TILES + (t + 1))
                    if t >= 1:
                        pe.wait_ge(a_copied, i * TILES + t)
                    for q in range(keys(t) // P):
                        last = nc.tensor.transpose(at_ps[:, q], diff[:, q * P:(q + 1) * P], g.ident[:])
                    last.then_inc(a_turned, 1)

                def times_v(t):
                    pe.wait_ge(a_copied, i * TILES + (t + 1))
                    if t >= 2:
                        pe.wait_ge(o_kept, i * TILES + (t - 1))
                    n = keys(t) // P
                    for q in range(n):
                        last = nc.tensor.matmul(ps[:, 6 + t % 2, 0:P], aT[:, t % 2, q], v[:, q],
                                                start=(q == 0), stop=(q == n - 1))
                    last.then_inc(pv_done, 1)

                project(0)
                for t in range(TILES):
                    if t + 1 < TILES:
                        project(t + 1)
                    turn_qk(t)
                score(0, 0)
                score(0, 1)
                for t in range(TILES):
                    if t + 1 < TILES:
                        score(t + 1, 0)
                        score(t + 1, 1)
                    if t >= 1:
                        times_v(t - 1)
                    turn_a(t)
                times_v(TILES - 1)

        @block.vector
        def _(dve):
            own = Own(dve, own_sem)
            dve.wait_ge(tables_in, 32)
            with dve.Fori(0, DA_HEADS) as i:
                own.enter(i, 42)

                def rotate(t):
                    dve.wait_ge(proj, i * TILES + (t + 1))
                    if t >= 2:
                        dve.wait_ge(qk_turned, i * TILES + (t - 1))
                    src = ps[:, t % 2, 0:2 * P].rearrange("p (a b) -> p a b", b=DA_DIM)
                    if t < CTX_TILES:
                        nc.vector.tensor_copy(rot[:, t % 2], src).then_inc(rotated, 1)
                        return
                    lt, h = t - CTX_TILES, DA_DIM // 2
                    dve.wait_ge(rotated, i * TILES + t)
                    own.mark(nc.vector.tensor_tensor(rt1[:], src, bc(cc[:, lt:lt + 1], [P, 4, DA_DIM]), ALU.mult))
                    own.mark(nc.vector.tensor_tensor(rt2[:, :, 0:h], src[:, :, h:], bc(ss[:, lt:lt + 1, 0:h], [P, 4, h]), ALU.mult))
                    own(nc.vector.tensor_tensor(rt2[:, :, h:], src[:, :, 0:h], bc(ss[:, lt:lt + 1, h:], [P, 4, h]), ALU.mult))
                    nc.vector.tensor_tensor(rot[:, t % 2], rt1[:], rt2[:], ALU.add).then_inc(rotated, 1)

                def row_max(t, comp):
                    dve.wait_ge(scored, i * (2 * TILES) + (2 * t + comp + 1))
                    m = mx[:, t % 2, comp:comp + 1]
                    own(nc.vector.tensor_reduce(m, s_ps[comp][:, 0:keys(t)], AX.X, ALU.max))
                    nc.vector.tensor_scalar(nb[:, t % 2, comp:comp + 1], m, -SCALE, None, ALU.mult).then_inc(maxed, 1)

                def mix(t):
                    dve.wait_ge(exped, i * (2 * TILES) + (2 * t + 2))
                    if t >= 1:
                        dve.wait_ge(a_turned, i * TILES + t)
                    n = keys(t)
                    own(nc.vector.reciprocal(r[:, t % 2], l[:, t % 2]))
                    own(nc.vector.tensor_tensor(r[:, t % 2, 1:2], r[:, t % 2, 1:2], g.neg_lam[:], ALU.mult))
                    own(nc.vector.tensor_scalar(diff[:, 0:n], prob[:, t % 2, 1, 0:n], r[:, t % 2, 1:2], None, ALU.mult))
                    nc.vector.scalar_tensor_tensor(out=diff[:, 0:n], in0=prob[:, t % 2, 0, 0:n],
                                                   scalar=r[:, t % 2, 0:1], in1=diff[:, 0:n],
                                                   op0=ALU.mult, op1=ALU.add).then_inc(mixed, 1)

                for t in range(TILES):
                    rotate(t)
                row_max(0, 0)
                row_max(0, 1)
                for t in range(TILES):
                    if t + 1 < TILES:
                        row_max(t + 1, 0)
                    mix(t)
                    if t + 1 < TILES:
                        row_max(t + 1, 1)
            own.leave(DA_HEADS)

        @block.scalar
        def _(act):
            with act.Fori(0, DA_HEADS) as i:
                def exponentiate(t, comp):
                    act.wait_ge(maxed, i * (2 * TILES) + (2 * t + comp + 1))
                    if t >= 2:
                        act.wait_ge(mixed, i * TILES + (t - 1))
                    n = keys(t)
                    nc.scalar.activation(prob[:, t % 2, comp, 0:n], s_ps[comp][:, 0:n], ACT.Exp,
                                         bias=nb[:, t % 2, comp:comp + 1], scale=SCALE,
                                         accum_out=l[:, t % 2, comp:comp + 1]).then_inc(exped, 1)

                def copy_a(t):
                    act.wait_ge(a_turned, i * TILES + (t + 1))
                    n = keys(t) // P
                    nc.scalar.activation(aT[:, t % 2, 0:n], at_ps[:, 0:n], ACT.Copy).then_inc(a_copied, 1)

                def keep_o(t):
                    act.wait_ge(pv_done, i * TILES + (t + 1))
                    nc.scalar.activation(o_tok[:, t, ds(i * P, P)], ps[:, 6 + t % 2, 0:P],
                                         ACT.Copy).then_inc(o_kept, 1)

                for t in range(TILES):
                    act.wait_ge(rotated, i * TILES + (t + 1))
                    nc.scalar.activation(v[:, t], ps[:, t % 2, 2 * P:3 * P], ACT.Copy).then_inc(v_copied, 1)
                    if t >= 1:
                        copy_qk(nc, act, i, t - 1, qk_turned, qk_copied, qT, kT, ps)
                copy_qk(nc, act, i, TILES - 1, qk_turned, qk_copied, qT, kT, ps)
                exponentiate(0, 0)
                exponentiate(0, 1)
                for t in range(TILES):
                    if t + 1 < TILES:
                        exponentiate(t + 1, 0)
                        exponentiate(t + 1, 1)
                    if t >= 1:
                        keep_o(t - 1)
                    copy_a(t)
                keep_o(TILES - 1)


def copy_qk(nc, act, i, t, qk_turned, qk_copied, qT, kT, ps):
    act.wait_ge(qk_turned, i * TILES + (t + 1))
    nc.scalar.activation(qT[:, t * P:(t + 1) * P], ps[:, 2 + t % 2, 0:P], ACT.Copy)
    nc.scalar.activation(kT[:, t * P:(t + 1) * P], ps[:, 2 + t % 2, P:2 * P], ACT.Copy).then_inc(qk_copied, 1)


def load_norm(g, eng, layer, sub, vec, landed):
    for s in range(2):
        a = (layer * ADA + 3 * sub + 2) * D
        eng.dma_start(vec[:, s], g.mod_d[s, a:a + D].partition_broadcast(P)).then_inc(landed, 16)
    eng.dma_start(vec[:, 2], g.d.ln_g[layer, sub].partition_broadcast(P)).then_inc(landed, 16)
    eng.dma_start(vec[:, 3], g.d.ln_b[layer, sub].partition_broadcast(P)).then_inc(landed, 16)


def post_norm_tile(nc, dve, own, g, vec, t, y, u, st, mv, var_sem, root_sem, n, out_sem):
    own(nc.vector.tensor_tensor(u, y, vec[:, stream_of(t)], ALU.mult))
    own(nc.vector.scalar_tensor_tensor(out=u, in0=g.x[:, t], scalar=DN_ALPHA, in1=u, op0=ALU.mult, op1=ALU.add))
    own.mark(nc.vector.bn_stats(st[:, 0:6], u[:, 0:BANK]))
    own(nc.vector.bn_stats(st[:, 6:12], u[:, BANK:D]))
    own(nc.vector.bn_aggr(mv[:, 0:2], st))
    nc.vector.tensor_scalar(mv[:, 1:2], mv[:, 1:2], LN_EPS, None, ALU.add).then_inc(var_sem, 1)
    dve.wait_ge(root_sem, n + 1)
    own(nc.vector.reciprocal(mv[:, 1:2], mv[:, 1:2]))
    own(nc.vector.tensor_scalar(u, u, mv[:, 0:1], mv[:, 1:2], ALU.subtract, ALU.mult))
    own(nc.vector.tensor_tensor(u, u, vec[:, 2], ALU.mult))
    nc.vector.tensor_tensor(g.x[:, t], u, vec[:, 3], ALU.add).then_inc(out_sem, 1)


def root(nc, act, x, done):
    nc.scalar.activation(x, x, ACT.Sqrt).then_inc(done, 1)


def project_out(nc, g, sem, layer, w_src, heads, o_tok, z_d, head_gain, tiles):
    KO, tag = heads, str(layer)
    vec_in = sem("po_vec" + tag)
    w_in, turned, copied = sem("po_w" + tag), sem("po_turned" + tag), sem("po_copied" + tag)
    y_done, x_done, own_sem = sem("po_y" + tag), sem("po_x" + tag), sem("po_own" + tag)
    var_done, var_root = sem("po_var" + tag), sem("po_var_root" + tag)
    ms_done, ms_root, normed = sem("po_ms" + tag), sem("po_ms_root" + tag), sem("po_normed" + tag)
    z_in = [sem(f"po_z{tag}_{s}") for s in range(2)]
    G, N = KO // 4, len(tiles)
    shape = [P, KO, P]
    with nc.sbuf_tensor("po_wo" + tag, [P, KO, D], F32) as wo, nc.sbuf_tensor("po_oT" + tag, [P, 2, KO, P], F32) as oT, \
            nc.sbuf_tensor("po_u" + tag, [P, D], F32) as u, nc.sbuf_tensor("po_st" + tag, [P, 12], F32) as st, \
            nc.sbuf_tensor("po_vecs" + tag, [P, 4, D], F32) as vec, \
            nc.sbuf_tensor("po_mv" + tag, [P, 2], F32) as mv, nc.sbuf_tensor("po_sq" + tag, [P, KO * P], F32) as sq, \
            nc.sbuf_tensor("po_ms" + tag, [P, KO], F32) as ms, \
            nc.sbuf_tensor("po_z" + tag, [P, 2, KO * P if z_d is not None else 1], F32) as z, \
            nc.psum_tensor("po_ps" + tag, [P, 8, BANK], F32) as ps, nc.Block() as block:
        @block.sync
        def _(sp):
            load_norm(g, sp, layer, 0, vec, vec_in)
            for q in range(4):
                sp.dma_start(wo[:, q * G:(q + 1) * G],
                             w_src.rearrange("(p k) n -> p k n", k=KO)[:, q * G:(q + 1) * G]).then_inc(w_in, 16)
            if z_d is not None:
                for n in range(N):
                    if n >= 2:
                        sp.wait_ge(normed, n - 1)
                    sp.dma_start(z[:, n % 2], z_d[:, n]).then_inc(z_in[n % 2], 16)

        @block.tensor
        def _(pe):
            def turn(n):
                pe.wait_ge(normed, n + 1)
                for q in range(G):
                    b = n * G + q
                    if b >= 4:
                        pe.wait_ge(copied, b - 3)
                    for a in range(4):
                        last = nc.tensor.transpose(ps[:, 4 + b % 4, a * P:(a + 1) * P],
                                                   o_tok[:, n, 4 * q + a::KO], g.ident[:])
                    last.then_inc(turned, 1)

            turn(0)
            for n in range(N):
                if n + 1 < N:
                    turn(n + 1)
                pe.wait_ge(copied, (n + 1) * G)
                if n == 0:
                    pe.wait_ge(w_in, 64)
                if n >= 2:
                    pe.wait_ge(x_done, n - 1)
                for half in range(2):
                    for k in range(KO):
                        last = nc.tensor.matmul(ps[:, 2 * (n % 2) + half], oT[:, n % 2, k],
                                                wo[:, k, half * BANK:(half + 1) * BANK],
                                                start=(k == 0), stop=(k == KO - 1))
                last.then_inc(y_done, 1)

        @block.scalar
        def _(act):
            def copy_o(n):
                if n >= 2:
                    act.wait_ge(y_done, n - 1)
                for q in range(G):
                    b = n * G + q
                    act.wait_ge(turned, b + 1)
                    nc.scalar.activation(oT[:, n % 2, 4 * q:4 * q + 4].rearrange("p a b -> p (a b)"),
                                         ps[:, 4 + b % 4], ACT.Copy).then_inc(copied, 1)

            for n in range(N + 2):
                if n < N:
                    act.wait_ge(ms_done, n + 1)
                    root(nc, act, ms[:], ms_root)
                    copy_o(n)
                if n >= 2:
                    act.wait_ge(var_done, n - 1)
                    root(nc, act, mv[:, 1:2], var_root)

        @block.vector
        def _(dve):
            own = Own(dve, own_sem)

            def norm_heads(n):
                o = o_tok[:, n]
                own(nc.vector.tensor_tensor(sq[:], o, o, ALU.mult))
                own(nc.vector.tensor_reduce(ms[:], sq[:].rearrange("p (h d) -> p h d", d=P), AX.X, ALU.add))
                nc.vector.tensor_scalar(ms[:], ms[:], 1.0 / P, NORM_EPS, ALU.mult, ALU.add).then_inc(ms_done, 1)
                dve.wait_ge(ms_root, n + 1)
                own(nc.vector.reciprocal(ms[:], ms[:]))
                oh = o.rearrange("p (h d) -> p h d", d=P)
                own(nc.vector.tensor_tensor(oh, oh, bc(ms[:].unsqueeze(2), shape), ALU.mult))
                if z_d is not None:
                    dve.wait_ge(z_in[n % 2], 16 * (n // 2 + 1))
                    own(nc.vector.tensor_tensor(o, o, z[:, n % 2], ALU.mult))
                nc.vector.tensor_tensor(oh, oh, bc(head_gain.unsqueeze(1), shape), ALU.mult).then_inc(normed, 1)
                dve.wait_ge(normed, n + 1)

            dve.wait_ge(vec_in, 64)
            for n in range(N + 2):
                if n < N:
                    norm_heads(n)
                if n >= 2:
                    m = n - 2
                    dve.wait_ge(y_done, m + 1)
                    y = ps[:, 2 * (m % 2):2 * (m % 2) + 2].rearrange("p a b -> p (a b)")
                    post_norm_tile(nc, dve, own, g, vec, tiles[m], y, u[:], st[:], mv[:], var_done, var_root, m, x_done)
                    dve.wait_ge(x_done, m + 1)


def most_blocks(tiles):
    return (len(tiles) * P * TOP_K + E * (P - 1)) // P


def slots(tiles):
    return (most_blocks(tiles) + 2) // 2 * 2 + 2


def moe(nc, g, sem, layer, tiles):
    NBLK = slots(tiles) - 2
    with ExitStack() as c:
        sb = lambda name, shape, dt: c.enter_context(nc.sbuf_tensor(f"moe_{name}{layer}", shape, dt))
        m = named(
            "Moe", tag=str(layer), tiles=tiles, N=len(tiles), NBLK=NBLK,
            slot_token=nc.dram_tensor(f"slot_token{layer}", ((NBLK + 2) * P, 2), I32, kind="Internal").ap(),
            expert=sb("expert", [1, P], I32), n_blocks=sb("n_blocks", [1, 1], I32))
        with nc.sbuf_tensor(f"hT_m{layer}", [P, KD, TOKENS], F32) as g.hT:
            modulate(nc, g, sem, layer, 1, tiles, True)
            route(nc, g, sem, layer, m)
            shared_expert(nc, g, sem, layer, m)
        run_blocks(nc, g, sem, layer, m)
        finish_moe(nc, g, sem, layer, m)


def route(nc, g, sem, layer, m):
    tag, N, tiles = m.tag, m.N, m.tiles
    landed, logits, scored = sem("rt_in" + tag), sem("rt_logits" + tag), sem("rt_scored" + tag)
    masked, counted, placed = sem("rt_masked" + tag), sem("rt_counted" + tag), sem("rt_placed" + tag)
    own_sem, based, be_col = sem("rt_own" + tag), sem("rt_based" + tag), sem("rt_be" + tag)
    be_row, cleared, scattered = sem("rt_be_row" + tag), sem("rt_cleared" + tag), sem("rt_scattered" + tag)
    with ExitStack() as c:
        sb = lambda name, shape, dt=F32: c.enter_context(nc.sbuf_tensor("rt_" + name + tag, shape, dt))
        w, bias, ranks, index = sb("w", [P, KD, E]), sb("bias", [P, E]), sb("ranks", [P, TOP_K, E]), sb("index", [P, 1])
        tokens = sb("tokens", [P, TILES], I32)
        slot_idx, pair = sb("slot_idx", [P, TILES, TOP_K], I32), sb("pair", [P, TILES, TOP_K, 2], I32)
        score, biased, top, left = sb("score", [P, TILES, E]), sb("biased", [P, E]), sb("top", [P, 8]), sb("left", [P, E])
        mask, wfull, wsum = sb("mask", [P, TILES, E]), sb("wfull", [P, TILES, E]), sb("wsum", [P, 1])
        nb, end, base, one = sb("nb", [P, E]), sb("end", [P, E]), sb("base", [P, E]), sb("one", [P, E])
        rank, eq, prod, slot, slot8 = (sb("rank", [P, E]), sb("eq", [P, TOP_K, E]), sb("prod", [P, TOP_K, E]),
                                       sb("slot", [P, E]), sb("slot8", [P, TOP_K]))
        le, be = sb("le", [P, E]), sb("becol", [P, 1])
        ps = c.enter_context(nc.psum_tensor("rt_ps" + tag, [P, 8, BANK], F32))
        block = c.enter_context(nc.Block())
        FIRST = tiles[0]

        @block.sync
        def _(sp):
            for dst, src in ((w[:], g.d.moe_router[layer].rearrange("(p k) e -> p k e", k=KD)),
                             (bias[:], g.d.moe_router_b[layer].partition_broadcast(P)),
                             (ranks[:], g.d.c_ranks), (index[:], g.d.c_index), (tokens[:], g.d.c_tokens)):
                sp.dma_start(dst, src).then_inc(landed, 16)
            sp.dma_start(m.slot_token.rearrange("(p b) a -> p (b a)", p=P),
                         g.d.c_empty.rearrange("(p b) a -> p (b a)", p=P) if layer == 0 else
                         g.d.c_empty[0:(m.NBLK + 2) * P].rearrange("(p b) a -> p (b a)", p=P)).then_inc(cleared, 16)

        @block.gpsimd
        def _(pool):
            pool.wait_ge(cleared, 16)
            for n in range(N):
                pool.wait_ge(placed, n + 1)
                for k in range(TOP_K):
                    pool.indirect_dma_start(
                        m.slot_token, bass.IndirectOffsetOnAxis(ap=slot_idx[:, n, k:k + 1], axis=0),
                        pair[:, n, k], None).then_inc(scattered, 16)
            pool.wait_ge(scattered, 16 * TOP_K * N)

        @block.tensor
        def _(pe):
            pe.wait_ge(landed, 16 * 5)
            for n, t in enumerate(tiles):
                if n >= 2:
                    pe.wait_ge(scored, n - 1)
                for k in range(KD):
                    last = nc.tensor.matmul(ps[:, n % 2, 0:E], g.hT[:, k, t * P:(t + 1) * P], w[:, k],
                                            start=(k == 0), stop=(k == KD - 1))
                last.then_inc(logits, 1)
            pe.wait_ge(masked, N)
            for n in range(N):
                last = nc.tensor.matmul(ps[:, 2, 0:E], g.ones[:], mask[:, n], start=(n == 0), stop=(n == N - 1))
            last.then_inc(counted, 1)
            for n in range(N):
                for a in range(n):
                    nc.tensor.matmul(ps[:, 3, n * E:(n + 1) * E], g.ones[:], mask[:, a], start=(a == 0), stop=False)
                last = nc.tensor.matmul(ps[:, 3, n * E:(n + 1) * E], g.upper[:, 1], mask[:, n],
                                        start=(n == 0), stop=True)
            last.then_inc(counted, 1)
            pe.wait_ge(be_col, 1)
            nc.tensor.transpose(ps[0:1, 4, 0:P], be[:], g.ident[:]).then_inc(be_row, 1)

        @block.scalar
        def _(act):
            for n in range(N):
                act.wait_ge(logits, n + 1)
                nc.scalar.activation(score[:, n], ps[:, n % 2, 0:E], ACT.Sigmoid).then_inc(scored, 1)

        @block.vector
        def _(dve):
            own = Own(dve, own_sem)
            own(nc.vector.memset(one[:], 1.0))
            for n in range(N):
                dve.wait_ge(scored, n + 1)
                own(nc.vector.tensor_tensor(biased[:], score[:, n], bias[:], ALU.add))
                own(nc.vector.max(top[:], biased[:]))
                own(nc.vector.match_replace(left[:], top[:], biased[:], -1e30))
                own(nc.vector.tensor_tensor(mask[:, n], left[:], biased[:], ALU.not_equal))
                own(nc.vector.tensor_tensor(wfull[:, n], score[:, n], mask[:, n], ALU.mult))
                own(nc.vector.tensor_reduce(wsum[:], wfull[:, n], AX.X, ALU.add))
                own(nc.vector.reciprocal(wsum[:], wsum[:]))
                nc.vector.tensor_scalar(wfull[:, n], wfull[:, n], wsum[:], ROUTE_SCALE, ALU.mult,
                                        ALU.mult).then_inc(masked, 1)
                dve.wait_ge(masked, n + 1)
            dve.wait_ge(counted, 1)
            own(nc.vector.tensor_scalar(nb[:], ps[:, 2, 0:E], 0.0, None, ALU.is_gt))
            for a in range(1, N):
                own(nc.vector.scalar_tensor_tensor(out=nb[:], in0=ps[:, 2, 0:E], scalar=float(a * P), in1=nb[:],
                                                   op0=ALU.is_gt, op1=ALU.add))
            own(nc.vector.tensor_tensor_scan(end[:], one[:], nb[:], 0.0, ALU.mult, ALU.add))
            own(nc.vector.tensor_tensor(base[:], end[:], nb[:], ALU.subtract))
            own(nc.vector.tensor_scalar(base[:], base[:], float(P), None, ALU.mult))
            own(nc.vector.tensor_scalar(le[:], end[:], index[:], None, ALU.is_le))
            own(nc.vector.tensor_reduce(be[:], le[:], AX.X, ALU.add))
            nc.vector.tensor_scalar(be[:], be[:], float(E - 1), None, ALU.min).then_inc(be_col, 1)
            own(nc.vector.tensor_copy(m.n_blocks[:], end[0:1, E - 1:E]))
            dve.wait_ge(counted, 2)
            for n in range(N):
                own(nc.vector.tensor_tensor(slot[:], ps[:, 3, n * E:(n + 1) * E], base[:], ALU.add))
                own(nc.vector.tensor_tensor_scan(rank[:], one[:], mask[:, n], 0.0, ALU.mult, ALU.add))
                own(nc.vector.tensor_tensor(rank[:], rank[:], mask[:, n], ALU.mult))
                shape = [P, TOP_K, E]
                own(nc.vector.tensor_tensor(eq[:], bc(rank[:].unsqueeze(1), shape), ranks[:], ALU.is_equal))
                own(nc.vector.tensor_tensor(prod[:], eq[:], bc(slot[:].unsqueeze(1), shape), ALU.mult))
                own(nc.vector.tensor_reduce(slot8[:], prod[:], AX.X, ALU.add))
                own.mark(nc.vector.tensor_copy(slot_idx[:, n], slot8[:]))
                own.mark(nc.vector.tensor_copy(pair[:, n, :, 0:1], bc(tokens[:, FIRST + n:FIRST + n + 1].unsqueeze(1), [P, TOP_K, 1])))
                own(nc.vector.tensor_tensor(prod[:], eq[:], bc(wfull[:, n].unsqueeze(1), shape), ALU.mult))
                nc.vector.tensor_reduce(pair[:, n].bitcast(F32)[:, :, 1:2], prod[:], AX.X, ALU.add).then_inc(placed, 1)
                dve.wait_ge(placed, n + 1)
            dve.wait_ge(be_row, 1)
            own(nc.vector.tensor_copy(m.expert[:], ps[0:1, 4, 0:P]))


def shared_expert(nc, g, sem, layer, m):
    tag, N, tiles = m.tag, m.N, m.tiles
    landed, up, silu, act_done = sem("sh_in" + tag), sem("sh_up" + tag), sem("sh_silu" + tag), sem("sh_act" + tag)
    stored = [sem(f"sh_stored{tag}_{s}") for s in range(2)]
    turned, copied, down, kept = sem("sh_turned" + tag), sem("sh_copied" + tag), sem("sh_down" + tag), sem("sh_kept" + tag)
    with ExitStack() as c:
        sb = lambda name, shape: c.enter_context(nc.sbuf_tensor("sh_" + name + tag, shape, F32))
        wg, wd = sb("wg", [P, KD, 2 * FF]), sb("wd", [P, 2, D])
        y = sb("y", [P, 2, D])
        sg, a, aT = sb("sg", [P, 2, FF]), sb("a", [P, 2, FF]), sb("aT", [P, 2, 2, P])
        ps = c.enter_context(nc.psum_tensor("sh_ps" + tag, [P, 8, BANK], F32))
        block = c.enter_context(nc.Block())

        @block.sync
        def _(sp):
            sp.dma_start(wg[:], g.d.moe_ws_gu[layer].rearrange("(p k) n -> p k n", k=KD)).then_inc(landed, 16)
            sp.dma_start(wd[:], g.d.moe_ws_dn[layer].rearrange("(p k) n -> p k n", k=2)).then_inc(landed, 16)
            for n, t in enumerate(tiles):
                sp.wait_ge(kept, n + 1)
                sp.dma_start(g.acc_d[t * P:(t + 1) * P], y[:, n % 2]).then_inc(stored[n % 2], 16)
            for s in range(2):
                sp.wait_ge(stored[s], 16 * (N // 2))

        @block.tensor
        def _(pe):
            pe.wait_ge(landed, 32)

            def project_up(n):
                if n >= 2:
                    pe.wait_ge(act_done, n - 1)
                t = tiles[n]
                for k in range(KD):
                    last = nc.tensor.matmul(ps[:, n % 2], g.hT[:, k, t * P:(t + 1) * P], wg[:, k],
                                            start=(k == 0), stop=(k == KD - 1))
                last.then_inc(up, 1)

            project_up(0)
            for n in range(N):
                if n + 1 < N:
                    project_up(n + 1)
                pe.wait_ge(act_done, n + 1)
                if n:
                    pe.wait_ge(copied, n)
                for k in range(2):
                    last = nc.tensor.transpose(ps[:, 2, k * P:(k + 1) * P], a[:, n % 2, k::2], g.ident[:])
                last.then_inc(turned, 1)
                pe.wait_ge(copied, n + 1)
                if n >= 2:
                    pe.wait_ge(kept, n - 1)
                for half in range(2):
                    for k in range(2):
                        last = nc.tensor.matmul(ps[:, 4 + 2 * (n % 2) + half], aT[:, n % 2, k],
                                                wd[:, k, half * BANK:(half + 1) * BANK], start=(k == 0), stop=(k == 1))
                last.then_inc(down, 1)

        @block.scalar
        def _(act):
            for n in range(N):
                act.wait_ge(up, n + 1)
                if n >= 2:
                    act.wait_ge(act_done, n - 1)
                nc.scalar.activation(sg[:, n % 2], ps[:, n % 2, 0:FF], ACT.Silu).then_inc(silu, 1)
                act.wait_ge(turned, n + 1)
                nc.scalar.activation(aT[:, n % 2].rearrange("p a b -> p (a b)"), ps[:, 2, 0:2 * P],
                                     ACT.Copy).then_inc(copied, 1)

        @block.vector
        def _(dve):
            for n in range(N + 1):
                if n < N:
                    dve.wait_ge(silu, n + 1)
                    if n >= 2:
                        dve.wait_ge(turned, n - 1)
                    nc.vector.tensor_tensor(a[:, n % 2], sg[:, n % 2], ps[:, n % 2, FF:2 * FF],
                                            ALU.mult).then_inc(act_done, 1)
                if n >= 1:
                    dve.wait_ge(down, n)
                    b = 4 + 2 * ((n - 1) % 2)
                    if n >= 3:
                        dve.wait_ge(stored[(n - 1) % 2], 16 * ((n - 1) // 2))
                    nc.vector.tensor_copy(y[:, (n - 1) % 2], ps[:, b:b + 2].rearrange("p a b -> p (a b)")).then_inc(kept, 1)


def run_blocks(nc, g, sem, layer, m):
    tag, NBLK = m.tag, m.NBLK
    two = lambda name: [sem(f"mb_{name}{tag}_{s}") for s in range(2)]
    wg_in, wd_in, idx_in, x_in, to_in = two("wg"), two("wd"), two("idx"), two("x"), two("to")
    x_turned, x_copied, up, silu, act_done = two("x_turned"), two("x_copied"), two("up"), two("silu"), two("act")
    a_turned, a_copied, down, y_lo, y_hi = two("a_turned"), two("a_copied"), two("down"), two("y_lo"), two("y_hi")
    added, held = sem("mb_added" + tag), sem("mb_held" + tag)
    with ExitStack() as c:
        sb = lambda name, shape, dt=F32: c.enter_context(nc.sbuf_tensor("mb_" + name + tag, shape, dt))
        wg = [sb(f"wg{s}", [P, KD, 2 * FF]) for s in range(2)]
        wd = [sb(f"wd{s}", [P, 2, D]) for s in range(2)]
        idx = [sb(f"idx{s}", [P, 2], I32) for s in range(2)]
        spare = sb("spare", [P, 2], I32)
        to = [sb(f"to{s}", [P, 2], I32) for s in range(2)]
        xg = [sb(f"xg{s}", [P, D]) for s in range(2)]
        xT = [sb(f"xT{s}", [P, KD, P]) for s in range(2)]
        sg = [sb(f"sg{s}", [P, FF]) for s in range(2)]
        a = [sb(f"a{s}", [P, FF]) for s in range(2)]
        aT = [sb(f"aT{s}", [P, 2, P]) for s in range(2)]
        y = [sb(f"y{s}", [P, D]) for s in range(2)]
        ps = c.enter_context(nc.psum_tensor("mb_ps" + tag, [P, 8, BANK], F32))
        x_ps, up_ps, a_ps, y_ps = ps[:, 0:2], ps[:, 2:4], ps[:, 4:6], ps[:, 6:8]
        block = c.enter_context(nc.Block())
        wg_dram = g.d.moe_w_gu[layer].rearrange("e (p k) n -> e p k n", k=KD)
        wd_dram = g.d.moe_w_dn[layer].rearrange("e (p k) n -> e p k n", k=2)
        tok_dram = m.slot_token.rearrange("(b p) a -> b p a", p=P)
        ADDED0 = 32

        def count(eng):
            return eng.value_load(m.n_blocks[0:1, 0:1], min_val=TOP_K, max_val=NBLK)

        @block.sync
        def _(sp):
            n = count(sp)
            sp.dma_start(to[0][:], tok_dram[0]).then_inc(to_in[0], 16)
            for s in range(2):
                e = sp.value_load(m.expert[0:1, s:s + 1], min_val=0, max_val=E - 1)
                sp.dma_start(wg[s][:], wg_dram[e]).then_inc(wg_in[s], 16)
                sp.dma_start(wd[s][:], wd_dram[e]).then_inc(wd_in[s], 16)
            with sp.Fori(0, NBLK // 2) as i:
                for s in range(2):
                    with sp.If(i * 2 + (s + 2) < n):
                        e = sp.value_load(m.expert[0:1, ds(i * 2 + (s + 2), 1)], min_val=0, max_val=E - 1)
                        sp.wait_ge(up[s], i + 1)
                        sp.dma_start(wg[s][:], wg_dram[e]).then_inc(wg_in[s], 16)
                        sp.wait_ge(down[s], i + 1)
                        sp.dma_start(wd[s][:], wd_dram[e]).then_inc(wd_in[s], 16)
                    with sp.If(i * 2 + s < n):
                        sp.wait_ge(added, i * 32 + (16 * s + ADDED0))
                        sp.dma_start(to[1 - s][:], tok_dram[i * 2 + (s + 1)]).then_inc(to_in[1 - s], 16)
            sp.wait_ge(to_in[0], (n >> 1) * 16 + 16)
            sp.wait_ge(to_in[1], ((n + 1) >> 1) * 16)
            sp.sem_inc(held, 1)

        @block.gpsimd
        def _(pool):
            n = count(pool)
            for a in range(2):
                pool.dma_start(spare[:], tok_dram[0]).then_inc(added, 16)
                pool.wait_ge(added, 16 * (a + 1))

            def gather(b, s, got):
                pool.dma_start(idx[s][:], tok_dram[b]).then_inc(idx_in[s], 16)
                pool.wait_ge(idx_in[s], got)
                pool.sem_inc(held, 1)
                pool.indirect_dma_start(xg[s][:], None, g.h_d, bass.IndirectOffsetOnAxis(ap=idx[s][:, 0:1], axis=0)
                                        ).then_inc(x_in[s], 16)

            gather(0, 0, 16)
            gather(1, 1, 16)
            with pool.Fori(0, NBLK // 2) as i:
                for s in range(2):
                    with pool.If(i * 2 + s < n):
                        pool.wait_ge(x_turned[s], i + 1)
                        gather(i * 2 + (s + 2), s, i * 16 + 32)
                        pool.wait_ge(to_in[s], i * 16 + 16)
                        pool.wait_ge(y_lo[s], i + (s + 1))
                        pool.wait_ge(y_hi[s], i + (s + 1))
                        pool.wait_ge(added, i * 32 + (16 * s + ADDED0))
                        pool.sem_inc(held, 1)
                        pool.indirect_dma_start(g.acc_d, bass.IndirectOffsetOnAxis(ap=to[s][:, 0:1], axis=0), y[s][:], None,
                                                compute_op=ALU.add).then_inc(added, 16)
            pool.wait_ge(added, n * 16 + ADDED0)
            for s in range(2):
                pool.wait_ge(x_in[s], ((n + (1 - s)) >> 1) * 16 + 16)
            pool.sem_inc(held, 1)

        @block.tensor
        def _(pe):
            n = count(pe)

            def turn_x(s, i):
                pe.wait_ge(x_in[s], 16 if i is None else i * 16 + 16)
                for k in range(KD):
                    last = nc.tensor.transpose(x_ps[:, k // 4, (k % 4) * P:(k % 4 + 1) * P], xg[s][:, k::KD], g.ident[:])
                last.then_inc(x_turned[s], 1)

            turn_x(0, None)
            with pe.Fori(0, NBLK // 2) as i:
                for s in range(2):
                    with pe.If(i * 2 + s < n):
                        pe.wait_ge(x_copied[s], i + 1)
                        pe.wait_ge(wg_in[s], i * 16 + 16)
                        for k in range(KD):
                            last = nc.tensor.matmul(up_ps[:, s], xT[s][:, k], wg[s][:, k], start=(k == 0), stop=(k == KD - 1))
                        last.then_inc(up[s], 1)
                        if s == 0:
                            turn_x(1, i)
                        else:
                            turn_x(0, i + 1)
                        pe.wait_ge(act_done[s], i + 1)
                        for k in range(2):
                            last = nc.tensor.transpose(a_ps[:, s, k * P:(k + 1) * P], a[s][:, k::2], g.ident[:])
                        last.then_inc(a_turned[s], 1)
                        pe.wait_ge(a_copied[s], i + 1)
                        pe.wait_ge(wd_in[s], i * 16 + 16)
                        pe.wait_ge(y_lo[1 - s], i + 1)
                        pe.wait_ge(y_hi[1 - s], i + 1)
                        for half in range(2):
                            for k in range(2):
                                last = nc.tensor.matmul(y_ps[:, half], aT[s][:, k], wd[s][:, k, half * BANK:(half + 1) * BANK],
                                                        start=(k == 0), stop=(k == 1))
                        last.then_inc(down[s], 1)

        @block.scalar
        def _(act):
            n = count(act)
            act.sem_inc(y_hi[1], 1)

            def copy_x(s, i):
                act.wait_ge(x_turned[s], 1 if i is None else i + 1)
                nc.scalar.activation(xT[s][:].rearrange("p k n -> p (k n)"), x_ps.rearrange("p a b -> p (a b)"),
                                     ACT.Copy).then_inc(x_copied[s], 1)

            copy_x(0, None)
            with act.Fori(0, NBLK // 2) as i:
                for s in range(2):
                    with act.If(i * 2 + s < n):
                        act.wait_ge(up[s], i + 1)
                        nc.scalar.activation(sg[s][:], up_ps[:, s, 0:FF], ACT.Silu).then_inc(silu[s], 1)
                        if s == 0:
                            copy_x(1, i)
                        else:
                            copy_x(0, i + 1)
                        act.wait_ge(to_in[s], i * 16 + 16)
                        act.wait_ge(down[s], i + 1)
                        act.wait_ge(added, i * 32 + (16 * s + ADDED0 - 16))
                        nc.scalar.activation(y[s][:, BANK:D], y_ps[:, 1], ACT.Copy,
                                             scale=to[s][:].bitcast(F32)[:, 1:2]).then_inc(y_hi[s], 1)
            act.wait_ge(y_hi[1], 1)

        @block.vector
        def _(dve):
            n = count(dve)
            dve.sem_inc(y_lo[1], 1)
            with dve.Fori(0, NBLK // 2) as i:
                for s in range(2):
                    with dve.If(i * 2 + s < n):
                        dve.wait_ge(silu[s], i + 1)
                        nc.vector.tensor_tensor(a[s][:], sg[s][:], up_ps[:, s, FF:2 * FF], ALU.mult).then_inc(act_done[s], 1)
                        dve.wait_ge(a_turned[s], i + 1)
                        nc.vector.tensor_copy(aT[s][:].rearrange("p a b -> p (a b)"), a_ps[:, s, 0:2 * P]).then_inc(a_copied[s], 1)
                        dve.wait_ge(to_in[s], i * 16 + 16)
                        dve.wait_ge(down[s], i + 1)
                        dve.wait_ge(added, i * 32 + (16 * s + ADDED0 - 16))
                        nc.vector.tensor_scalar(y[s][:, 0:BANK], y_ps[:, 0], to[s][:].bitcast(F32)[:, 1:2], None,
                                                ALU.mult).then_inc(y_lo[s], 1)


def finish_moe(nc, g, sem, layer, m):
    tag, N, tiles = m.tag, m.N, m.tiles
    got = [sem(f"fm_got{tag}_{n}") for n in range(N)]
    vec_in = sem("fm_vec" + tag)
    x_done, own_sem = sem("fm_x" + tag), sem("fm_own" + tag)
    var_done, var_root = sem("fm_var" + tag), sem("fm_root" + tag)
    with ExitStack() as c:
        sb = lambda name, shape: c.enter_context(nc.sbuf_tensor("fm_" + name + tag, shape, F32))
        vec = sb("vecs", [P, 4, D])
        f, u, st, mv = sb("f", [P, N, D]), sb("u", [P, D]), sb("st", [P, 12]), sb("mv", [P, 2])
        block = c.enter_context(nc.Block())

        @block.sync
        def _(sp):
            load_norm(g, sp, layer, 1, vec, vec_in)
            for n, t in enumerate(tiles):
                sp.dma_start(f[:, n], g.acc_d[t * P:(t + 1) * P]).then_inc(got[n], 16)

        @block.scalar
        def _(act):
            for n in range(N):
                act.wait_ge(var_done, n + 1)
                root(nc, act, mv[:, 1:2], var_root)

        @block.vector
        def _(dve):
            own = Own(dve, own_sem)
            for n in range(N):
                if n == 0:
                    dve.wait_ge(vec_in, 64)
                dve.wait_ge(got[n], 16)
                post_norm_tile(nc, dve, own, g, vec, tiles[n], f[:, n], u[:], st[:], mv[:], var_done, var_root, n, x_done)
                dve.wait_ge(x_done, n + 1)


STEPS = TILES
PAIRS = STEPS // 2
LEVELS = 7


def step_tiles(n):
    if n < CTX_TILES:
        return n, CTX_TILES - 1 - n
    return n, TILES - 1 - (n - CTX_TILES)


def gdn_gates(nc, g, sem, gates, conv):
    landed, ab, turned, own_sem = sem("gg_in"), sem("gg_ab"), sem("gg_turned"), sem("gg_own")
    copied, arg1, exp1 = sem("gg_copied"), sem("gg_arg1"), sem("gg_exp1")
    NG = 2 * HV
    with ExitStack() as c:
        sb = lambda name, shape: c.enter_context(nc.sbuf_tensor("gg_" + name, shape, F32))
        w, rows = sb("w", [P, KD, 2 * NG]), sb("rows", [80, 2, P])
        dt, al, t1, t2, t3, t4 = (sb("dt", [P, 1, NG]), sb("al", [P, 1, NG]), *(sb(f"t{n}", [P, TILES, NG]) for n in (1, 2, 3, 4)))
        ps = c.enter_context(nc.psum_tensor("gg_ps", [P, 8, BANK], F32))
        block = c.enter_context(nc.Block())
        shape = [P, TILES, NG]

        @block.sync
        def _(sp):
            sp.dma_start(w[:], g.d.gdn_w_in[0].rearrange("(p k) n -> p k n", k=KD)[:, :, GDN_A0:GDN_A0 + 2 * NG]).then_inc(landed, 16)
            sp.dma_start(rows[:], g.d.gdn_conv[0].rearrange("j (c p) -> (j c) p", p=P).rearrange("(a r) p -> r a p", a=2)).then_inc(landed, 16)
            sp.dma_start(dt[:, 0], g.d.gdn_dt_bias[0].rearrange("a b -> (a b)").partition_broadcast(P)).then_inc(landed, 16)
            sp.dma_start(al[:, 0], g.d.gdn_a_log[0].rearrange("a b -> (a b)").partition_broadcast(P)).then_inc(landed, 16)

        @block.tensor
        def _(pe):
            pe.wait_ge(landed, 64)
            for a in range(2):
                last = nc.tensor.transpose(ps[:, 6, a * 80:(a + 1) * 80], rows[:, a], g.ident[0:80, 0:80])
            last.then_inc(turned, 1)
            for t in range(TILES):
                for k in range(KD):
                    last = nc.tensor.matmul(ps[:, 0, t * 2 * NG:(t + 1) * 2 * NG], g.hT[:, k, t * P:(t + 1) * P], w[:, k],
                                            start=(k == 0), stop=(k == KD - 1))
            last.then_inc(ab, 1)

        @block.scalar
        def _(act):
            act.wait_ge(turned, 1)
            nc.scalar.activation(conv, ps[:, 6, 0:160], ACT.Copy)
            act.wait_ge(ab, 1)
            abp = ps[:, 0, 0:TILES * 2 * NG].rearrange("p (t n) -> p t n", t=TILES)
            nc.scalar.activation(gates[:, 1], abp[:, :, NG:], ACT.Sigmoid).then_inc(copied, 1)
            act.wait_ge(arg1, 1)
            nc.scalar.activation(t2[:], t2[:], ACT.Exp)
            nc.scalar.activation(al[:], al[:], ACT.Exp).then_inc(exp1, 1)

        @block.vector
        def _(dve):
            own = Own(dve, own_sem)
            dve.wait_ge(landed, 64)
            dve.wait_ge(copied, 1)
            abp = ps[:, 0, 0:TILES * 2 * NG].rearrange("p (t n) -> p t n", t=TILES)
            own(nc.vector.tensor_tensor(t1[:], abp[:, :, 0:NG], bc(dt[:], shape), ALU.add))
            nc.vector.scalar_tensor_tensor(out=t2[:], in0=t1[:], scalar=-1.0, in1=t1[:], op0=ALU.mult, op1=ALU.min).then_inc(arg1, 1)
            dve.wait_ge(exp1, 1)
            own(nc.vector.tensor_scalar(t3[:], t2[:], 2.0, None, ALU.add))
            own(nc.vector.reciprocal(t3[:], t3[:]))
            own(nc.vector.tensor_tensor(t2[:], t2[:], t3[:], ALU.mult))
            own(nc.vector.tensor_tensor(t4[:], t2[:], t2[:], ALU.mult))
            own(nc.vector.tensor_scalar(t3[:], t4[:], 1.0 / 17, None, ALU.mult))
            for odd in range(15, 1, -2):
                own(nc.vector.scalar_tensor_tensor(out=t3[:], in0=t3[:], scalar=1.0 / odd, in1=t4[:], op0=ALU.add, op1=ALU.mult))
            own(nc.vector.scalar_tensor_tensor(out=t2[:], in0=t3[:], scalar=1.0, in1=t2[:], op0=ALU.add, op1=ALU.mult))
            own(nc.vector.tensor_scalar(t1[:], t1[:], 0.0, None, ALU.max))
            own(nc.vector.scalar_tensor_tensor(out=t1[:], in0=t2[:], scalar=2.0, in1=t1[:], op0=ALU.mult, op1=ALU.add))
            own(nc.vector.scalar_tensor_tensor(out=gates[:, 0], in0=t1[:], scalar=-1.0, in1=bc(al[:], shape),
                                               op0=ALU.mult, op1=ALU.mult))


def gated_deltanet(nc, g, sem, o_tok):
    with nc.sbuf_tensor("gdn_gates", [P, 2, TILES, 2 * HV], F32) as gates, \
            nc.sbuf_tensor("gdn_conv", [P, 160], F32) as conv:
        gdn_gates(nc, g, sem, gates, conv[:])
        gdn_heads(nc, g, sem, o_tok, gates, conv)


def gdn_heads(nc, g, sem, o_tok, gates, conv):
    names = ("w_in cin_copied conved silued projected z_done z_copied v_turned v_copied squared ssq ss_read rooted "
             "normed k_turned k_copied kk_prod kk_read gcol_set gsum gsum_read gates_exp gates_done "
             "g_prod d_arg d_exp mt_done t_turned t_copied x_prod x_masked p_prod tt_done "
             "ks_done r_done oq_done y_done v_scaled kv_done s_done o_done z_kept own_v levels_in cin_zeroed")
    q = named("Semaphores", **{n: sem("gd_" + n) for n in names.split()})
    NCH = 4
    LAT = LAT_TILES * P
    CIN = TOKENS + 6
    with ExitStack() as c:
        sb = lambda name, shape: c.enter_context(nc.sbuf_tensor("gd_" + name, shape, F32))
        w, taps = sb("w", [P, KD, 6 * P]), sb("taps", [P, CONV_W, NCH])
        cin, cout = sb("cin", [P, 2, CIN]), sb("cout", [P, 2, CIN - 4])
        kT, qT, k_tok, v_tok = sb("kT", [P, TOKENS]), sb("qT", [P, LAT]), sb("k_tok", [P, TILES, P]), sb("v_tok", [P, TILES, 2, P])
        z = sb("z", [P, LAT_TILES, 2 * P])
        kk, kq = sb("kk", [P, 2, TILES, P]), sb("kq", [P, 2, LAT_TILES, P])
        levels = sb("levels", [P, LEVELS, 2, P])
        NC = 4 * TILES
        gsel, gall = sb("gsel", [P, 2, NC]), sb("gall", [P, 3, NC])
        gc, neg_eg, beta_el = sb("gc", [P, NC]), sb("neg_eg", [P, NC]), sb("beta_el", [P, NC])
        dx, tm = sb("dx", [P, 4, BANK]), sb("tm", [P, 4, BANK])
        Dm, X, T, M = [dx[:, s] for s in (0, 1)], [dx[:, s] for s in (2, 3)], [tm[:, s] for s in (0, 1)], [tm[:, s] for s in (2, 3)]
        TT, attn = sb("TT", [P, 2, 2, BANK]), sb("attn", [P, 2, 2, BANK])
        R, V2, Vn, oq, S = (sb(n, [P, BANK]) for n in ("R", "V2", "Vn", "oq", "S"))
        vx = dx[:].rearrange("p a b -> p (a b)")
        sq = tm[:].rearrange("p a b -> p (a b)")
        vx = [vx[:, 0:TOKENS], vx[:, TOKENS:2 * TOKENS]]
        sq = [sq[:, 0:TOKENS], sq[:, TOKENS:TOKENS + LAT]]
        ps = c.enter_context(nc.psum_tensor("gd_ps", [P, 8, BANK], F32))
        block = c.enter_context(nc.Block())
        w_dram = g.d.gdn_w_in[0].rearrange("(p k) n -> p k n", k=KD)

        ch = lambda ap, n: ap[:, n * P:(n + 1) * P]
        chains = [(dr, v, dr * 2 + v) for dr in range(2) for v in range(2)]
        four = lambda ap: ap.rearrange("p (d v n) -> p d v n", d=2, v=2)
        perdir = lambda ap: bc(ap.unsqueeze(2), [P, 2, 2, P])

        def col(ap, dr, t, v):
            n = dr * 2 * TILES + t * 2 + v
            return ap[:, n:n + 1]

        def load_w(sp, i):
            for at, first, size in ((0, 2 * GDN_KEY, 2 * P), (2, GDN_KEY, P), (3, 0, P), (4, GDN_Z0, 2 * P)):
                src = w_dram[:, :, ds(i * size + first, size)] if not isinstance(i, int) else w_dram[:, :, first:first + size]
                sp.dma_start(w[:, :, at * P:at * P + size], src).then_inc(q.w_in, 16)

        @block.sync
        def _(sp):
            sp.dma_start(levels[:], g.d.c_levels).then_inc(q.levels_in, 16)
            load_w(sp, 0)
            with sp.Fori(0, HK - 1) as i:
                sp.wait_ge(q.z_done, i * LAT_TILES + LAT_TILES)
                load_w(sp, i + 1)

        @block.tensor
        def _(pe):
            with pe.Fori(0, HK) as i:
                def project(ct):
                    if ct >= 2:
                        pe.wait_ge(q.cin_copied, i * NCH + (ct - 1))
                    b = 2 * (ct % 2)
                    for bank, lo, hi in ((b, 0, CTX_LEN), (b + 1, CTX_LEN, TOKENS)):
                        if ct == 3 and lo == 0:
                            continue
                        for k in range(KD):
                            last = nc.tensor.matmul(ps[:, bank, 0:hi - lo], w[:, k, ct * P:(ct + 1) * P],
                                                    g.hT[:, k, lo:hi], start=(k == 0), stop=(k == KD - 1))
                    last.then_inc(q.projected, 1)

                def project_z(lt):
                    if lt >= 2:
                        pe.wait_ge(q.z_copied, i * LAT_TILES + (lt - 1))
                    t = lt + CTX_TILES
                    for k in range(KD):
                        last = nc.tensor.matmul(ps[:, 4 + lt % 2, 0:2 * P], g.hT[:, k, t * P:(t + 1) * P],
                                                w[:, k, 4 * P:6 * P], start=(k == 0), stop=(k == KD - 1))
                    last.then_inc(q.z_done, 1)

                def turn_six(src, done):
                    for t in range(TILES):
                        last = nc.tensor.transpose(ps[:, 6 + t // 4, (t % 4) * P:(t % 4 + 1) * P],
                                                   src[:, t * P:(t + 1) * P], g.ident[:])
                    last.then_inc(done, 1)

                def decays(pair, s):
                    n = 2 * pair + s
                    for dr, v, a in chains:
                        t = step_tiles(n)[dr]
                        last = nc.tensor.matmul(ch(ps[:, 3 * s], a), bc(col(gsel[:, 0], dr, t, v), [P, P]),
                                                g.upper[:, 2 * dr], start=True, stop=True)
                    last.then_inc(q.g_prod, 1)

                def turn_t(s, done, pair):
                    for _, _, a in chains:
                        last = nc.tensor.transpose(ch(ps[:, 3 * s + 2], a), ch(TT[:, pair % 2, s], a), g.ident[:])
                    last.then_inc(q.t_turned, 1)

                def state_qk(n):
                    if n >= 1:
                        pe.wait_ge(q.s_done, i * STEPS + n)
                        for dr, v, a in chains:
                            t = step_tiles(n)[dr]
                            last = nc.tensor.matmul(ch(ps[:, 6], a), kT[:, t * P:(t + 1) * P], ch(S, a), start=True, stop=True)
                    if n >= CTX_TILES:
                        if n > CTX_TILES:
                            pe.wait_ge(q.o_done, i * LAT_TILES + (n - CTX_TILES))
                        for dr, v, a in chains:
                            t = step_tiles(n)[dr] - CTX_TILES
                            last = nc.tensor.matmul(ch(ps[:, 7], a), qT[:, t * P:(t + 1) * P], ch(S, a), start=True, stop=True)
                    if n >= 1:
                        last.then_inc(q.ks_done, 1)

                def state_y(n):
                    pair, s = divmod(n, 2)
                    if n >= 1:
                        pe.wait_ge(q.r_done, i * (STEPS - 1) + n)
                    for dr, v, a in chains:
                        rhs = ch(R, a) if n >= 1 else v_tok[:, step_tiles(n)[dr], v]
                        last = nc.tensor.matmul(ch(ps[:, 6], a), ch(TT[:, pair % 2, s], a), rhs, start=True, stop=True)
                    last.then_inc(q.y_done, 1)

                def state_kv(n):
                    pair, s = divmod(n, 2)
                    pe.wait_ge(q.v_scaled, i * STEPS + (n + 1))
                    for dr, v, a in chains:
                        last = nc.tensor.matmul(ch(ps[:, 6], a), k_tok[:, step_tiles(n)[dr]], ch(V2, a), start=True, stop=True)
                    if n >= CTX_TILES:
                        pe.wait_ge(q.oq_done, i * LAT_TILES + (n - CTX_TILES + 1))
                        for dr, v, a in chains:
                            last = nc.tensor.matmul(ch(ps[:, 7], a), ch(attn[:, pair % 2, s], a), ch(Vn, a), start=True, stop=True)
                    last.then_inc(q.kv_done, 1)

                def piece(pair, j):
                    (state_qk, state_y, state_kv)[j % 3](2 * pair + j // 3)

                pe.wait_ge(q.w_in, i * 64 + 64)
                for ct in range(NCH):
                    project(ct)
                for lt in range(LAT_TILES):
                    project_z(lt)
                for v in range(2):
                    pe.wait_ge(q.silued, i * NCH + (v + 1))
                    if v:
                        pe.wait_ge(q.v_copied, i * 2 + 1)
                    turn_six(vx[v], q.v_turned)
                pe.wait_ge(q.squared, i + 1)
                nc.tensor.matmul(ps[:, 0], g.ones[:], sq[0][:, 0:BANK], start=True, stop=True)
                nc.tensor.matmul(ps[:, 1, 0:TOKENS - BANK], g.ones[:], sq[0][:, BANK:TOKENS], start=True, stop=True)
                nc.tensor.matmul(ps[:, 2], g.ones[:], sq[1], start=True, stop=True).then_inc(q.ssq, 1)
                pe.wait_ge(q.gcol_set, i + 1)
                pe.wait_ge(q.z_copied, i * LAT_TILES + LAT_TILES)
                half = 2 * TILES
                for dr in range(2):
                    nc.tensor.matmul(ps[:, 3, dr * half:(dr + 1) * half], g.upper[:, 2 * dr],
                                     gsel[:, 0, dr * half:(dr + 1) * half], start=True, stop=True)
                nc.tensor.matmul(ps[:, 3, NC:2 * NC], g.ones[:], gsel[:, 0], start=True, stop=True).then_inc(q.gsum, 1)
                pe.wait_ge(q.normed, i + 1)
                pe.wait_ge(q.v_copied, i * 2 + 2)
                turn_six(kT[:], q.k_turned)
                for t in range(TILES):
                    last = nc.tensor.matmul(ps[:, 4 + t // 4, (t % 4) * P:(t % 4 + 1) * P], kT[:, t * P:(t + 1) * P],
                                            kT[:, t * P:(t + 1) * P], start=True, stop=True)
                for lt in range(LAT_TILES):
                    t = lt + CTX_TILES
                    last = nc.tensor.matmul(ch(ps[:, 0], lt), kT[:, t * P:(t + 1) * P], qT[:, lt * P:(lt + 1) * P],
                                            start=True, stop=True)
                last.then_inc(q.kk_prod, 1)
                pe.wait_ge(q.gsum_read, i + 1)
                pe.wait_ge(q.kk_read, i + 1)
                pe.wait_ge(q.k_copied, i + 1)
                for pair in range(PAIRS):
                    for s in range(2):
                        decays(pair, s)
                    for s in range(2):
                        pe.wait_ge(q.mt_done, i * STEPS + (2 * pair + s + 1))
                        turn_t(s, q.t_turned, pair)
                    for b in range(1, LEVELS):
                        at = (pair * (LEVELS - 1) + b - 1) * 2
                        for s in range(2):
                            pe.wait_ge(q.t_copied, i * (PAIRS * 12) + (at + s + 1))
                            for _, _, a in chains:
                                last = nc.tensor.matmul(ch(ps[:, 3 * s], a), ch(M[s], a), ch(T[s], a), start=True, stop=True)
                            last.then_inc(q.x_prod, 1)
                        for s in range(2):
                            pe.wait_ge(q.x_masked, i * (PAIRS * 12) + (at + s + 1))
                            for _, _, a in chains:
                                last = nc.tensor.matmul(ch(ps[:, 3 * s + 1], a), ch(X[s], a), ch(TT[:, pair % 2, s], a),
                                                        start=True, stop=True)
                            last.then_inc(q.p_prod, 1)
                        if b < LEVELS - 1:
                            for s in range(2):
                                pe.wait_ge(q.tt_done, i * (PAIRS * 12) + (at + s + 1))
                                turn_t(s, q.t_turned, pair)
                        if pair:
                            piece(pair - 1, b - 1)
                for s in range(2):
                    pe.wait_ge(q.tt_done, i * (PAIRS * 12) + (PAIRS * 12 - 1 + s))
                for j in range(6):
                    piece(PAIRS - 1, j)

        @block.vector
        def _(dve):
            own = Own(dve, q.own_v)
            nc.vector.memset(cin[:], 0.0).then_inc(q.cin_zeroed, 1)
            dve.wait_ge(q.levels_in, 16)
            with dve.Fori(0, HK) as i:
                own.enter(i, DVE_PER_HEAD)

                for kind in range(2):
                    for dr in range(2):
                        src = gates[:, kind].rearrange("p t (d h) -> p t d h", d=2)[:, :, dr, ds(i * 2, 2)]
                        dst = gsel[:, kind, dr * 2 * TILES:(dr + 1) * 2 * TILES].rearrange("p (t v) -> p t v", v=2)
                        own(nc.vector.tensor_copy(dst, src))
                dve.sem_inc(q.gcol_set, 1)
                cw = conv[:].rearrange("p (j c) -> p j c", j=CONV_W)
                for at, first, size in ((0, 2 * GDN_KEY // P, 2), (2, GDN_KEY // P, 1), (3, 0, 1)):
                    own(nc.vector.tensor_copy(taps[:, :, at:at + size], cw[:, :, ds(i * size + first, size)]))

                def convolve(ct):
                    dve.wait_ge(q.cin_copied, i * NCH + (ct + 1))
                    if ct >= 2:
                        dve.wait_ge(q.silued, i * NCH + (ct - 1))
                    lo = CTX_LEN + 2 if ct == 3 else 0
                    n = CIN - 4
                    src, dst = cin[:, ct % 2], cout[:, ct % 2, lo:n]
                    own(nc.vector.tensor_scalar(dst, src[:, lo:n], taps[:, 0, ct:ct + 1], None, ALU.mult))
                    for j in range(1, CONV_W):
                        ins = nc.vector.scalar_tensor_tensor(out=dst, in0=src[:, lo + j:n + j], scalar=taps[:, j, ct:ct + 1],
                                                             in1=dst, op0=ALU.mult, op1=ALU.add)
                        if j < CONV_W - 1:
                            own(ins)
                    ins.then_inc(q.conved, 1)

                for ct in range(NCH):
                    convolve(ct)
                dve.wait_ge(q.ssq, i + 1)
                own.mark(nc.vector.tensor_scalar(sq[0], ps[:, 0:2].rearrange("p a b -> p (a b)")[:, 0:TOKENS], NORM_EPS, None, ALU.add))
                own(nc.vector.tensor_scalar(sq[1], ps[:, 2], NORM_EPS, None, ALU.add))
                dve.sem_inc(q.ss_read, 1)
                dve.wait_ge(q.gsum, i + 1)
                own.mark(nc.vector.tensor_copy(gc[:], ps[:, 3, 0:NC]))
                own(nc.vector.tensor_copy(gall[:, 2], ps[:, 3, NC:2 * NC]))
                own.mark(nc.vector.tensor_copy(gall[:, 0], gc[:]))
                own(nc.vector.tensor_tensor(gall[:, 1], gall[:, 2], gc[:], ALU.subtract))
                dve.sem_inc(q.gsum_read, 1)
                dve.wait_ge(q.rooted, i + 1)
                own.mark(nc.vector.reciprocal(sq[0], sq[0]))
                own(nc.vector.reciprocal(sq[1], sq[1]))
                own(nc.vector.tensor_tensor(kT[:], kT[:], sq[0], ALU.mult))
                nc.vector.scalar_tensor_tensor(out=qT[:], in0=qT[:], scalar=DH ** -0.5, in1=sq[1],
                                               op0=ALU.mult, op1=ALU.mult).then_inc(q.normed, 1)
                dve.wait_ge(q.gates_exp, i + 1)
                own.mark(nc.vector.tensor_scalar(neg_eg[:], gall[:, 0], -1.0, None, ALU.mult))
                own(nc.vector.tensor_tensor(beta_el[:], gall[:, 1], gsel[:, 1], ALU.mult))
                dve.sem_inc(q.gates_done, 1)
                dve.wait_ge(q.kk_prod, i + 1)
                kk_ps = ps[:, 4:6].rearrange("p a b -> p (a b)")[:, 0:TILES * P].rearrange("p (t n) -> p t n", n=P)
                kq_ps = ps[:, 0].rearrange("p (t n) -> p t n", n=P)
                for dr in range(2):
                    own.mark(nc.vector.tensor_tensor(kk[:, dr], kk_ps, bc(g.upper[:, 2 * dr + 1:2 * dr + 2], [P, TILES, P]), ALU.mult))
                    own(nc.vector.tensor_tensor(kq[:, dr], kq_ps, bc(g.upper[:, 2 * dr:2 * dr + 1], [P, LAT_TILES, P]), ALU.mult))
                dve.sem_inc(q.kk_read, 1)

                def decay_args(pair, s):
                    n = 2 * pair + s
                    dve.wait_ge(q.g_prod, i * STEPS + (n + 1))
                    for dr, v, a in chains:
                        t = step_tiles(n)[dr]
                        ins = nc.vector.tensor_scalar(ch(Dm[s], a), ch(ps[:, 3 * s], a), col(gc, dr, t, v), 0.0,
                                                      ALU.subtract, ALU.min)
                    ins.then_inc(q.d_arg, 1)

                def matrices(pair, s):
                    n = 2 * pair + s
                    tt = TT[:, pair % 2, s]
                    dve.wait_ge(q.d_exp, i * STEPS + (n + 1))
                    for dr, v, a in chains:
                        t = step_tiles(n)[dr]
                        ins = nc.vector.scalar_tensor_tensor(out=ch(M[s], a), in0=ch(Dm[s], a), scalar=col(gsel[:, 1], dr, t, v),
                                                             in1=kk[:, dr, t], op0=ALU.mult, op1=ALU.mult)
                        own.mark(ins)
                    own.wait()
                    if n >= CTX_TILES:
                        for dr in range(2):
                            t = step_tiles(n)[dr] - CTX_TILES
                            half = slice(dr * 2 * P, (dr + 1) * 2 * P)
                            dst = attn[:, pair % 2, s, half].rearrange("p (v n) -> p v n", v=2)
                            own.mark(nc.vector.tensor_tensor(dst, Dm[s][:, half].rearrange("p (v n) -> p v n", v=2),
                                                             bc(kq[:, dr, t:t + 1], [P, 2, P]), ALU.mult))
                    own(nc.vector.tensor_tensor(four(tt), four(M[s]), perdir(levels[:, 0]), ALU.mult))
                    nc.vector.tensor_tensor(tt.rearrange("p (a n) -> p a n", n=P), bc(g.ident[:].unsqueeze(1), [P, 4, P]),
                                            tt.rearrange("p (a n) -> p a n", n=P), ALU.subtract).then_inc(q.mt_done, 1)

                def state_r(n):
                    if n == 0:
                        return
                    dve.wait_ge(q.ks_done, i * (STEPS - 1) + n)
                    for dr, v, a in chains:
                        t = step_tiles(n)[dr]
                        ins = nc.vector.scalar_tensor_tensor(out=ch(R, a), in0=ch(ps[:, 6], a), scalar=col(neg_eg, dr, t, v),
                                                             in1=v_tok[:, t, v], op0=ALU.mult, op1=ALU.add)
                    ins.then_inc(q.r_done, 1)

                def state_s(n):
                    dve.wait_ge(q.kv_done, i * STEPS + (n + 1))
                    if n == 0:
                        nc.vector.tensor_copy(S[:], ps[:, 6]).then_inc(q.s_done, 1)
                        return
                    dve.wait_ge(q.s_done, i * STEPS + n)
                    for dr, v, a in chains:
                        t = step_tiles(n)[dr]
                        ins = nc.vector.scalar_tensor_tensor(out=ch(S, a), in0=ch(S, a), scalar=col(gall[:, 2], dr, t, v),
                                                             in1=ch(ps[:, 6], a), op0=ALU.mult, op1=ALU.add)
                    ins.then_inc(q.s_done, 1)

                def state_o(n):
                    if n < CTX_TILES:
                        return
                    for dr in range(2):
                        t = step_tiles(n)[dr] - CTX_TILES
                        half = slice(dr * 2 * P, (dr + 1) * 2 * P)
                        dst = o_tok[:, t, ds(i * (2 * P), 2 * P)]
                        again = n >= CTX_TILES + LAT_TILES // 2
                        if again:
                            own(nc.vector.tensor_tensor(dst, dst, oq[:, half], ALU.add))
                        ins = nc.vector.tensor_tensor(dst, ps[:, 7, half], dst if again else oq[:, half], ALU.add)
                        own.mark(ins)
                    own.wait()
                    dve.sem_inc(q.o_done, 1)

                def piece(pair, j):
                    n = 2 * pair + j // 3
                    if j % 3 == 0:
                        state_r(n)
                    if j % 3 == 2:
                        state_s(n)
                        state_o(n)

                for pair in range(PAIRS):
                    for s in range(2):
                        decay_args(pair, s)
                    for s in range(2):
                        matrices(pair, s)
                    for b in range(1, LEVELS):
                        at = (pair * (LEVELS - 1) + b - 1) * 2
                        for s in range(2):
                            dve.wait_ge(q.x_prod, i * (PAIRS * 12) + (at + s + 1))
                            nc.vector.tensor_tensor(four(X[s]), four(ps[:, 3 * s]), perdir(levels[:, b]),
                                                    ALU.mult).then_inc(q.x_masked, 1)
                        for s in range(2):
                            dve.wait_ge(q.p_prod, i * (PAIRS * 12) + (at + s + 1))
                            tt = TT[:, pair % 2, s]
                            nc.vector.tensor_tensor(tt, tt, ps[:, 3 * s + 1], ALU.subtract).then_inc(q.tt_done, 1)
                        if pair:
                            piece(pair - 1, b - 1)
                for j in range(6):
                    piece(PAIRS - 1, j)
            own.leave(HK)

        @block.scalar
        def _(act):
            act.wait_ge(q.cin_zeroed, 1)
            act.dma_start(z[:, 0, 0:P], g.d.c_ident).then_inc(q.z_kept, 16)
            with act.Fori(0, HK) as i:
                def copy_in(ct):
                    act.wait_ge(q.projected, i * NCH + (ct + 1))
                    if ct >= 2:
                        act.wait_ge(q.conved, i * NCH + (ct - 1))
                    b = 2 * (ct % 2)
                    if ct < 3:
                        nc.scalar.activation(cin[:, ct % 2, 2:2 + CTX_LEN], ps[:, b, 0:CTX_LEN], ACT.Copy)
                    nc.scalar.activation(cin[:, ct % 2, CTX_LEN + 4:CTX_LEN + 4 + LAT], ps[:, b + 1],
                                         ACT.Copy).then_inc(q.cin_copied, 1)

                def silu(ct):
                    act.wait_ge(q.conved, i * NCH + (ct + 1))
                    dst = (vx[0], vx[1], kT, qT)[ct]
                    src = cout[:, ct % 2]
                    if ct < 3:
                        nc.scalar.activation(dst[:, 0:CTX_LEN], src[:, 0:CTX_LEN], ACT.Silu)
                        dst = dst[:, CTX_LEN:TOKENS]
                    nc.scalar.activation(dst[:, 0:LAT], src[:, CTX_LEN + 2:CTX_LEN + 2 + LAT], ACT.Silu).then_inc(q.silued, 1)

                copy_in(0)
                copy_in(1)
                silu(0)
                copy_in(2)
                silu(1)
                copy_in(3)
                silu(2)
                silu(3)
                act.wait_ge(q.silued, i * NCH + NCH)
                nc.scalar.activation(sq[0], kT[:], ACT.Square)
                nc.scalar.activation(sq[1], qT[:], ACT.Square).then_inc(q.squared, 1)
                for lt in range(LAT_TILES):
                    act.wait_ge(q.z_done, i * LAT_TILES + (lt + 1))
                    if lt == 0:
                        act.wait_ge(q.z_kept, i * 16 + 16)
                    nc.scalar.activation(z[:, lt], ps[:, 4 + lt % 2, 0:2 * P], ACT.Silu).then_inc(q.z_copied, 1)
                act.wait_ge(q.z_copied, i * LAT_TILES + LAT_TILES)
                act.dma_start(g.z_d[:, :, ds(i * (2 * P), 2 * P)], z[:]).then_inc(q.z_kept, 16)
                for v in range(2):
                    act.wait_ge(q.v_turned, i * 2 + (v + 1))
                    nc.scalar.activation(v_tok[:, 0:4, v], ps[:, 6].rearrange("p (t n) -> p t n", n=P), ACT.Copy)
                    nc.scalar.activation(v_tok[:, 4:6, v], ps[:, 7, 0:2 * P].rearrange("p (t n) -> p t n", n=P),
                                         ACT.Copy).then_inc(q.v_copied, 1)
                act.wait_ge(q.ss_read, i + 1)
                nc.scalar.activation(sq[0], sq[0], ACT.Sqrt)
                nc.scalar.activation(sq[1], sq[1], ACT.Sqrt).then_inc(q.rooted, 1)
                act.wait_ge(q.gsum_read, i + 1)
                nc.scalar.activation(gall[:], gall[:], ACT.Exp).then_inc(q.gates_exp, 1)
                act.wait_ge(q.k_turned, i + 1)
                nc.scalar.activation(k_tok[:, 0:4], ps[:, 6].rearrange("p (t n) -> p t n", n=P), ACT.Copy)
                nc.scalar.activation(k_tok[:, 4:6], ps[:, 7, 0:2 * P].rearrange("p (t n) -> p t n", n=P),
                                     ACT.Copy).then_inc(q.k_copied, 1)
                act.wait_ge(q.gates_done, i + 1)

                def copy_t(s, at):
                    act.wait_ge(q.t_turned, i * (PAIRS * 12) + (at + s + 1))
                    nc.scalar.activation(T[s], ps[:, 3 * s + 2], ACT.Copy).then_inc(q.t_copied, 1)

                def state_oq(n):
                    if n < CTX_TILES:
                        return
                    act.wait_ge(q.ks_done, i * (STEPS - 1) + n)
                    if n > CTX_TILES:
                        act.wait_ge(q.o_done, i * LAT_TILES + (n - CTX_TILES))
                    for dr, v, a in chains:
                        t = step_tiles(n)[dr]
                        ins = nc.scalar.activation(ch(oq, a), ch(ps[:, 7], a), ACT.Copy, scale=col(gall[:, 0], dr, t, v))
                    ins.then_inc(q.oq_done, 1)

                def state_v(n):
                    act.wait_ge(q.y_done, i * STEPS + (n + 1))
                    for dr, v, a in chains:
                        t = step_tiles(n)[dr]
                        if n >= CTX_TILES:
                            nc.scalar.activation(ch(Vn, a), ch(ps[:, 6], a), ACT.Copy, scale=col(gsel[:, 1], dr, t, v))
                        ins = nc.scalar.activation(ch(V2, a), ch(ps[:, 6], a), ACT.Copy, scale=col(beta_el, dr, t, v))
                    ins.then_inc(q.v_scaled, 1)

                def piece(pair, j):
                    n = 2 * pair + j // 3
                    if j % 3 == 0:
                        state_oq(n)
                    if j % 3 == 1:
                        state_v(n)

                for pair in range(PAIRS):
                    for s in range(2):
                        act.wait_ge(q.d_arg, i * STEPS + (2 * pair + s + 1))
                        nc.scalar.activation(Dm[s], Dm[s], ACT.Exp).then_inc(q.d_exp, 1)
                    for b in range(0, LEVELS):
                        if b < LEVELS - 1:
                            for s in range(2):
                                copy_t(s, (pair * (LEVELS - 1) + b) * 2)
                        if pair and b:
                            piece(pair - 1, b - 1)
                for j in range(6):
                    piece(PAIRS - 1, j)
            act.wait_ge(q.z_kept, 16 * HK + 16)


DVE_PER_HEAD = 88
@contextmanager
def semaphores(nc):
    taken = []

    def sem(name):
        taken.append(nc.alloc_semaphore(name=name))
        return taken[-1]

    yield sem
    nc.clear_and_free_semaphores(taken)
    nc.all_engine_barrier()


def build_program(nc, d, out, stages=None):
    on = lambda s: stages is None or s in stages
    with ExitStack() as c:
        sb = lambda name, shape: c.enter_context(nc.sbuf_tensor(name, shape, F32))
        dram = lambda name, shape, dt: nc.dram_tensor(name, shape, dt, kind="Internal").ap()
        g = Core()
        g.d = d
        g.mod_d = dram("mod_d", (2, DEPTH * ADA * D), F32)
        g.h_d = dram("h_d", (TOKENS + P, D), F32)
        g.acc_d = dram("acc_d", (TOKENS + P, D), F32)
        g.z_d = dram("z_d", (P, LAT_TILES, GDN_VAL), F32)
        g.x = sb("x_res", [P, TILES, D])
        g.ident, g.ones, g.upper = sb("ident", [P, P]), sb("ones", [P, P]), sb("upper", [P, 4, P])
        g.subln, g.gdn_gain, g.neg_lam = sb("subln", [P, P]), sb("gdn_gain", [P, P]), sb("neg_lam", [P, 1])
        with semaphores(nc) as sem:
            load_constants(nc, g, sem)
            if on("ada"):
                modulation_vectors(nc, g, sem)
        if on("attn"):
            with semaphores(nc) as sem, nc.sbuf_tensor("da_o", [P, TILES, D], F32) as o_tok:
                with nc.sbuf_tensor("hT_a", [P, KD, TOKENS], F32) as g.hT:
                    modulate(nc, g, sem, 0, 0, range(TILES), False)
                    diff_attention(nc, g, sem, o_tok)
                project_out(nc, g, sem, 0, d.da_w_o[0], DA_HEADS, o_tok, None, g.subln[:], range(TILES))
        if on("moe0"):
            with semaphores(nc) as sem:
                moe(nc, g, sem, 0, range(TILES))
        if on("gdn"):
            with semaphores(nc) as sem, nc.sbuf_tensor("gdn_o", [P, LAT_TILES, GDN_VAL], F32) as o_tok:
                with nc.sbuf_tensor("hT_b", [P, KD, TOKENS], F32) as g.hT:
                    modulate(nc, g, sem, 1, 0, range(TILES), False)
                    gated_deltanet(nc, g, sem, o_tok)
                project_out(nc, g, sem, 1, d.gdn_w_o[0], HV, o_tok, g.z_d, g.gdn_gain[:], range(CTX_TILES, TILES))
        if on("moe1"):
            with semaphores(nc) as sem:
                moe(nc, g, sem, 1, range(CTX_TILES, TILES))
        with nc.semaphore("out_stored") as stored, nc.Block() as block:
            @block.sync
            def _(sp):
                sp.dma_start(out[0].rearrange("(t p) n -> p t n", p=P), g.x[:, CTX_TILES:]).then_inc(stored, 16)
                sp.wait_ge(stored, 16)


def empty_slots():
    n = slots(range(TILES)) * P
    return np.stack([TOKENS + np.arange(n) % P, np.zeros(n)], 1).astype(np.int32)


def constants():
    i = np.arange(P)
    n_freq = DA_DIM // 4
    inv = 1.0 / (10000.0 ** (np.arange(n_freq, dtype=np.float32) / n_freq))
    tok = np.arange(SEQ)
    ang = np.concatenate([(tok // 64)[:, None] * inv, (tok % 64)[:, None] * inv], -1).astype(np.float32)
    cos, sin = np.cos(ang), np.sin(ang)
    tiled = lambda a: np.ascontiguousarray(a.reshape(LAT_TILES, P, -1).transpose(1, 0, 2)).astype(np.float32)
    upper = np.stack([i[:, None] <= i, i[:, None] < i, i[:, None] >= i, i[:, None] > i], 1)
    def level(b):
        pair, half = i // (2 * b), (i // b) % 2
        same = pair[:, None] == pair
        fwd = same & (half[:, None] == 1) & (half == 0)
        return np.stack([fwd, fwd.T], 0)
    levels = np.stack([level(2 ** n) for n in range(7)], 0)
    levels[0] = levels[0].transpose(0, 2, 1)
    return {
        "c_ident": np.eye(P, dtype=np.float32), "c_ones": np.ones((P, P), np.float32),
        "c_upper": upper.astype(np.float32),
        "c_cos": tiled(np.concatenate([cos, cos], -1)), "c_sin": tiled(np.concatenate([-sin, sin], -1)),
        "c_levels": np.ascontiguousarray(levels.transpose(2, 0, 1, 3)).astype(np.float32),
        "c_ranks": np.broadcast_to(np.arange(1, TOP_K + 1, dtype=np.float32)[None, :, None], (P, TOP_K, E)).copy(),
        "c_index": i[:, None].astype(np.float32),
        "c_empty": empty_slots(),
        "c_tokens": (i[:, None] + P * np.arange(TILES)[None]).astype(np.int32),
    }


INS = ["x", "c", "ctx", "c_ctx", "ada_w", "ada_b", "ln_g", "ln_b", "da_w_in", "da_w_o", "da_lambda", "da_subln",
       "gdn_w_in", "gdn_conv", "gdn_a_log", "gdn_dt_bias", "gdn_norm", "gdn_w_o",
       "moe_router", "moe_router_b", "moe_w_gu", "moe_w_dn", "moe_ws_gu", "moe_ws_dn"]


def kernel(**inputs):
    import concourse.bacc as bacc
    from concourse.bass_utils import run_bass_kernel_spmd as run

    nc = bacc.Bacc("TRN2", target_bir_lowering=False, num_devices=1)
    arrays, aps = {}, {}
    given = {name: inputs[name] for name in INS}
    given.update(constants())
    for name, a in given.items():
        a = np.ascontiguousarray(a)
        arrays[f"in_{name}"] = a
        aps[name] = nc.dram_tensor(f"in_{name}", a.shape, mybir.dt.from_np(a.dtype), kind="ExternalInput").ap()
    out = nc.dram_tensor("out_0", (1, SEQ, D), F32, kind="ExternalOutput").ap()
    build_program(nc, named("Inputs", **aps), out)
    r = run(nc, [arrays], core_ids=[0])
    return r.results[0]["out_0"]
```

```python
from collections import namedtuple
from contextlib import ExitStack, contextmanager
import math

import numpy as np
import concourse.bass as bass
from concourse import mybir

F32 = mybir.dt.float32
I32 = mybir.dt.int32
ACT = mybir.ActivationFunctionType
ALU = mybir.AluOpType
AX = mybir.AxisListType
ds = bass.ds

P = 128
BANK = 512
D = 1024
KD = D // P
SEQ, CTX_LEN, DEPTH = 512, 256, 2
CTX_TILES, LAT_TILES = CTX_LEN // P, SEQ // P
TILES = CTX_TILES + LAT_TILES
TOKENS = TILES * P
DN_ALPHA = (2 * DEPTH) ** 0.25
LN_EPS, NORM_EPS = 1e-5, 1e-6
ADA = 6

DA_HEADS = 8
DA_DIM = D // DA_HEADS // 2
LAM_INIT = 0.8 - 0.6 * math.exp(-0.3 * 0)

HK, HV, DH = 8, 16, 128
VPK = HV // HK
GDN_KEY, GDN_VAL = HK * DH, HV * DH
CONV_W = 5
GDN_Z0 = 2 * GDN_KEY + GDN_VAL
GDN_A0 = GDN_Z0 + GDN_VAL

E, TOP_K, FF = 64, 8, 256
ROUTE_SCALE = 2.5


def named(kind, **values):
    return namedtuple(kind, list(values))(**values)


class Core:
    pass


class Own:

    def __init__(self, eng, sem):
        self.eng, self.sem, self.n, self.base = eng, sem, 0, 0

    def __call__(self, ins):
        self.mark(ins)
        self.wait()

    def mark(self, ins):
        ins.then_inc(self.sem, 1)
        self.n += 1

    def wait(self):
        self.eng.wait_ge(self.sem, self.base + self.n)

    def enter(self, i, per):
        self.before, self.per, self.base, self.n = self.base + self.n, per, self.base + self.n + i * per, 0

    def leave(self, count):
        assert self.n == self.per, f"{self.n} counted in the loop's body, {self.per} announced"
        self.base, self.n = self.before + count * self.per, 0


def bc(ap, shape):
    return ap.to_broadcast(shape)


def stream_of(t):
    return 1 if t < CTX_TILES else 0


def first_stage(nc, g, sem):
    landed, lam_dot, lam_exp, own_sem = sem("const_landed"), sem("lam_dot"), sem("lam_exp"), sem("const_own")
    zeroed, rows_zero = sem("const_zeroed"), sem("const_rows_zero")
    with nc.sbuf_tensor("zero_row", [P, D], F32) as zero, nc.sbuf_tensor("lam_in", [P, 4, DA_DIM], F32) as lam_in, \
            nc.sbuf_tensor("lam_tmp", [P, 2, DA_DIM], F32) as lam_tmp, \
            nc.sbuf_tensor("lam_s", [P, 2], F32) as lam_s:
        loads = [(g.ident[:], g.d.c_ident), (g.upper[:], g.d.c_upper), (g.ones[:], g.d.c_ones),
                 (lam_in[:], g.d.da_lambda[0].partition_broadcast(P)),
                 (g.subln[:], g.d.da_subln[0].partition_broadcast(P)),
                 (g.gdn_gain[:], g.d.gdn_norm[0].partition_broadcast(P)),
                 (g.x[:, CTX_TILES:, :], g.d.x[0].rearrange("(t p) n -> p t n", p=P)),
                 (g.x[:, 0:CTX_TILES, :], g.d.ctx[0].rearrange("(t p) n -> p t n", p=P))]

        def load_constants(act):
            for dst, src in loads:
                act.dma_start(dst, src).then_inc(landed, 16)

        modulation_vectors(nc, g, sem, load_constants)
        with nc.Block() as block:
            @block.sync
            def _(sp):
                sp.wait_ge(zeroed, 1)
                for rows in (g.h_d[TOKENS:], g.acc_d[TOKENS:]):
                    sp.dma_start(rows, zero[:]).then_inc(rows_zero, 16)
                sp.wait_ge(rows_zero, 32)

            @block.vector
            def _(dve):
                own = Own(dve, own_sem)
                nc.vector.memset(zero[:], 0.0).then_inc(zeroed, 1)
                dve.wait_ge(landed, 16 * len(loads))
                for a in range(2):
                    own(nc.vector.tensor_tensor(lam_tmp[:, a], lam_in[:, 2 * a], lam_in[:, 2 * a + 1], ALU.mult))
                nc.vector.tensor_reduce(lam_s[:], lam_tmp[:], AX.X, ALU.add).then_inc(lam_dot, 1)
                own(nc.vector.tensor_scalar(g.subln[:], g.subln[:], 1.0 - LAM_INIT, None, ALU.mult))
                dve.wait_ge(lam_exp, 1)
                nc.vector.scalar_tensor_tensor(out=g.neg_lam[:], in0=lam_s[:, 1:2], scalar=-LAM_INIT,
                                               in1=lam_s[:, 0:1], op0=ALU.add, op1=ALU.subtract)

            @block.scalar
            def _(act):
                act.wait_ge(lam_dot, 1)
                nc.scalar.activation(lam_s[:], lam_s[:], ACT.Exp).then_inc(lam_exp, 1)


def modulation_vectors(nc, g, sem, load_constants):
    NB = 3
    chunks = DEPTH * ADA * D // BANK
    c_in, c_silu, b_in = sem("ada_c_in"), sem("ada_c_silu"), sem("ada_b_in")
    w_in = [sem(f"ada_w_in{s}") for s in range(NB)]
    prod, added, stored = sem("ada_prod"), sem("ada_added"), sem("ada_stored")
    with nc.sbuf_tensor("ada_wb", [P, NB, KD, BANK], F32) as wb, \
            nc.sbuf_tensor("ada_c", [P, 2, KD], F32) as cs, \
            nc.sbuf_tensor("ada_bias", [2, DEPTH * ADA * D], F32) as bias, \
            nc.psum_tensor("ada_ps", [P, NB, BANK], F32) as ps, nc.Block() as block:
        per_layer = ADA * D // BANK
        w_dram = g.d.ada_w.rearrange("l (p k) (c n) -> l c p k n", k=KD, n=BANK)

        @block.sync
        def _(sp):
            sp.dma_start(cs[:, 0, :], g.d.c.rearrange("a (p k) -> p (a k)", k=KD)).then_inc(c_in, 16)
            sp.dma_start(cs[:, 1, :], g.d.c_ctx.rearrange("(p k) -> p k", k=KD)).then_inc(c_in, 16)
            sp.dma_start(bias[:], g.d.ada_b.rearrange("l n -> (l n)").partition_broadcast(2)).then_inc(b_in, 16)
            for n in range(NB):
                sp.dma_start(wb[:, n], w_dram[0, n]).then_inc(w_in[n], 16)
            for l in range(DEPTH):
                first = NB if l == 0 else 0
                with sp.Fori(0, (per_layer - first) // NB) as i:
                    for s in range(NB):
                        sp.wait_ge(prod, i * NB + (per_layer * l + first + s - NB + 1))
                        sp.dma_start(wb[:, s], w_dram[l, i * NB + (first + s)]).then_inc(w_in[s], 16)
            sp.wait_ge(added, chunks)
            sp.dma_start(g.mod_d, bias[:]).then_inc(stored, 16)
            sp.wait_ge(stored, 16)

        @block.scalar
        def _(act):
            act.wait_ge(c_in, 32)
            nc.scalar.activation(cs[:], cs[:], ACT.Silu).then_inc(c_silu, 1)
            act.wait_ge(prod, NB)
            load_constants(act)

        @block.tensor
        def _(pe):
            pe.wait_ge(c_silu, 1)

            def chunk(s, landed, bank_read):
                pe.wait_ge(w_in[s], landed)
                if bank_read is not None:
                    pe.wait_ge(added, bank_read)
                for k in range(KD):
                    last = nc.tensor.matmul(ps[0:2, s], cs[:, :, k], wb[:, s, k], start=(k == 0), stop=(k == KD - 1))
                last.then_inc(prod, 1)

            for s in range(NB):
                chunk(s, 16, None)
            with pe.Fori(0, chunks // NB - 1) as i:
                for s in range(NB):
                    chunk(s, i * 16 + 32, i * NB + (s + 1))

        @block.vector
        def _(dve):
            dve.wait_ge(b_in, 16)
            with dve.Fori(0, chunks // NB) as i:
                for s in range(NB):
                    dve.wait_ge(prod, i * NB + (s + 1))
                    row = bias[:, ds(i * (NB * BANK) + s * BANK, BANK)]
                    nc.vector.tensor_tensor(row, ps[0:2, s], row, ALU.add).then_inc(added, 1)


def modulate(nc, g, sem, layer, sub, tiles, h_dram, load_ahead):
    tag = f"{layer}{sub}"
    vec_in, h_done, tr_done, evac = sem("mod_in" + tag), sem("mod_h" + tag), sem("mod_tr" + tag), sem("mod_evac" + tag)
    own_sem, h_out = sem("mod_own" + tag), [sem(f"mod_out{tag}_{s}") for s in range(2)]
    streams = sorted({stream_of(t) for t in tiles})
    with nc.sbuf_tensor("mod_htok" + tag, [P, 2, D], F32) as ht, nc.sbuf_tensor("mod_vec" + tag, [P, 2, 2, D], F32) as vec, \
            nc.psum_tensor("mod_ps" + tag, [P, 4, 4, P], F32) as ps, nc.Block() as block:
        @block.sync
        def _(sp):
            for s in streams:
                a = (layer * ADA + 3 * sub) * D
                sp.dma_start(vec[:, s], g.mod_d[s, a:a + 2 * D].partition_broadcast(P)).then_inc(vec_in, 16)
            if h_dram:
                for n, t in enumerate(tiles):
                    sp.wait_ge(h_done, n + 1)
                    sp.dma_start(g.h_d[t * P:(t + 1) * P, :], ht[:, n % 2]).then_inc(h_out[n % 2], 16)
                for s in range(2):
                    sp.wait_ge(h_out[s], 16 * ((len(tiles) + 1 - s) // 2))

        @block.vector
        def _(dve):
            own = Own(dve, own_sem)
            dve.wait_ge(vec_in, 16 * len(streams))
            for n, t in enumerate(tiles):
                s = stream_of(t)
                if n >= 2:
                    dve.wait_ge(tr_done, 2 * (n - 1))
                    if h_dram:
                        dve.wait_ge(h_out[n % 2], 16 * (n // 2))
                own(nc.vector.scalar_tensor_tensor(out=ht[:, n % 2], in0=vec[:, s, 1], scalar=1.0,
                                                   in1=g.x[:, t], op0=ALU.add, op1=ALU.mult))
                nc.vector.tensor_tensor(ht[:, n % 2], ht[:, n % 2], vec[:, s, 0], ALU.add).then_inc(h_done, 1)

        @block.tensor
        def _(pe):
            for n, t in enumerate(tiles):
                pe.wait_ge(h_done, n + 1)
                for half in range(2):
                    b = 2 * n + half
                    if b >= 4:
                        pe.wait_ge(evac, b - 3)
                    for q in range(4):
                        last = nc.tensor.transpose(ps[:, b % 4, q], ht[:, n % 2, 4 * half + q::KD], g.ident[:])
                    last.then_inc(tr_done, 1)

        @block.scalar
        def _(act):
            load_ahead(act)
            for n, t in enumerate(tiles):
                for half in range(2):
                    b = 2 * n + half
                    act.wait_ge(tr_done, b + 1)
                    nc.scalar.activation(g.hT[:, 4 * half:4 * half + 4, t * P:(t + 1) * P], ps[:, b % 4],
                                         ACT.Copy).then_inc(evac, 1)


def diff_attention(nc, g, sem, o_tok):
    w_in, proj, rotated, v_copied = sem("da_w_in"), sem("da_proj"), sem("da_rotated"), sem("da_v_copied")
    qk_turned, qk_copied = sem("da_qk_turned"), sem("da_qk_copied")
    scored, maxed, exped = sem("da_scored"), sem("da_maxed"), sem("da_exped")
    mixed, a_turned, a_copied, pv_done = sem("da_mixed"), sem("da_a_turned"), sem("da_a_copied"), sem("da_pv")
    o_kept, own_sem, tables_in = sem("da_o_kept"), sem("da_own"), sem("da_tables")
    KEYS = TOKENS
    SCALE = DA_DIM ** -0.5
    with ExitStack() as c:
        sb = lambda name, shape: c.enter_context(nc.sbuf_tensor("da_" + name, shape, F32))
        w = sb("w", [P, KD, 3 * P])
        cc, ss = sb("cc", [P, LAT_TILES, DA_DIM]), sb("ss", [P, LAT_TILES, DA_DIM])
        w_dram = g.d.da_w_in[0].rearrange("(p k) (m h n) -> p k m h n", k=KD, m=3, n=P)
        wv = w[:].rearrange("p k (m n) -> p k m n", m=3)

        def load_first(sp):
            for m in range(3):
                sp.dma_start(wv[:, :, m], w_dram[:, :, m, 0]).then_inc(w_in, 16)
            sp.dma_start(cc[:], g.d.c_cos).then_inc(tables_in, 16)
            sp.dma_start(ss[:], g.d.c_sin).then_inc(tables_in, 16)

        modulate(nc, g, sem, 0, 0, range(TILES), False, load_first)
        rot, rt1, rt2 = sb("rot", [P, 2, 4, DA_DIM]), sb("rt1", [P, 4, DA_DIM]), sb("rt2", [P, 4, DA_DIM])
        qT, kT, v = sb("qT", [P, KEYS]), sb("kT", [P, KEYS]), sb("v", [P, TILES, P])
        prob = sb("prob", [P, 2, 2, KEYS])
        diff = sb("diff", [P, KEYS])
        aT = sb("aT", [P, 2, TILES, P])
        mx, nb, l, r = (sb(n, [P, 2, 2]) for n in ("mx", "nb", "l", "r"))
        ps = c.enter_context(nc.psum_tensor("da_ps", [P, 8, BANK], F32))
        s_ps = [ps[:, 0:2].rearrange("p a b -> p (a b)"), ps[:, 2:4].rearrange("p a b -> p (a b)")]
        at_ps = ps[:, 4:6].rearrange("p a (b q) -> p (a b) q", q=P)
        block = c.enter_context(nc.Block())

        def keys(t):
            return CTX_LEN if t < CTX_TILES else KEYS

        @block.sync
        def _(sp):
            with sp.Fori(0, DA_HEADS - 1) as i:
                sp.wait_ge(proj, i * TILES + TILES)
                for m in range(3):
                    sp.dma_start(wv[:, :, m], w_dram[:, :, m, i + 1]).then_inc(w_in, 16)

        @block.tensor
        def _(pe):
            with pe.Fori(0, DA_HEADS) as i:
                def project(t):
                    if t == 0:
                        pe.wait_ge(w_in, i * 48 + 48)
                    if t >= 2:
                        pe.wait_ge(rotated, i * TILES + (t - 1))
                        pe.wait_ge(v_copied, i * TILES + (t - 1))
                    for k in range(KD):
                        last = nc.tensor.matmul(ps[:, t % 2, 0:3 * P], g.hT[:, k, t * P:(t + 1) * P], w[:, k],
                                                start=(k == 0), stop=(k == KD - 1))
                    last.then_inc(proj, 1)

                def turn_qk(t):
                    pe.wait_ge(rotated, i * TILES + (t + 1))
                    if t >= 2:
                        pe.wait_ge(qk_copied, i * TILES + (t - 1))
                    for m in range(2):
                        last = nc.tensor.transpose(
                            ps[:, 2 + t % 2, m * P:(m + 1) * P],
                            rot[:, t % 2, 2 * m:2 * m + 2].rearrange("p a b -> p (a b)"), g.ident[:])
                    last.then_inc(qk_turned, 1)

                def score(t, comp):
                    if t == 0:
                        pe.wait_ge(qk_copied, i * TILES + TILES)
                    else:
                        pe.wait_ge(exped, i * (2 * TILES) + (2 * (t - 1) + comp + 1))
                    rows = slice(DA_DIM * comp, DA_DIM * (comp + 1))
                    for a in range(0, keys(t), BANK):
                        n = min(BANK, keys(t) - a)
                        last = nc.tensor.matmul(s_ps[comp][:, a:a + n], qT[rows, t * P:(t + 1) * P],
                                                kT[rows, a:a + n], start=True, stop=True)
                    last.then_inc(scored, 1)

                def turn_a(t):
                    pe.wait_ge(mixed, i * TILES + (t + 1))
                    if t >= 1:
                        pe.wait_ge(a_copied, i * TILES + t)
                    for q in range(keys(t) // P):
                        last = nc.tensor.transpose(at_ps[:, q], diff[:, q * P:(q + 1) * P], g.ident[:])
                    last.then_inc(a_turned, 1)

                def times_v(t):
                    pe.wait_ge(a_copied, i * TILES + (t + 1))
                    if t >= 2:
                        pe.wait_ge(o_kept, i * TILES + (t - 1))
                    n = keys(t) // P
                    for q in range(n):
                        last = nc.tensor.matmul(ps[:, 6 + t % 2, 0:P], aT[:, t % 2, q], v[:, q],
                                                start=(q == 0), stop=(q == n - 1))
                    last.then_inc(pv_done, 1)

                project(0)
                for t in range(TILES):
                    if t + 1 < TILES:
                        project(t + 1)
                    turn_qk(t)
                score(0, 0)
                score(0, 1)
                for t in range(TILES):
                    if t + 1 < TILES:
                        score(t + 1, 0)
                        score(t + 1, 1)
                    if t >= 1:
                        times_v(t - 1)
                    turn_a(t)
                times_v(TILES - 1)

        @block.vector
        def _(dve):
            own = Own(dve, own_sem)
            dve.wait_ge(tables_in, 32)
            with dve.Fori(0, DA_HEADS) as i:
                own.enter(i, 42)

                def rotate(t):
                    dve.wait_ge(proj, i * TILES + (t + 1))
                    if t >= 2:
                        dve.wait_ge(qk_turned, i * TILES + (t - 1))
                    src = ps[:, t % 2, 0:2 * P].rearrange("p (a b) -> p a b", b=DA_DIM)
                    if t < CTX_TILES:
                        nc.vector.tensor_copy(rot[:, t % 2], src).then_inc(rotated, 1)
                        return
                    lt, h = t - CTX_TILES, DA_DIM // 2
                    dve.wait_ge(rotated, i * TILES + t)
                    own.mark(nc.vector.tensor_tensor(rt1[:], src, bc(cc[:, lt:lt + 1], [P, 4, DA_DIM]), ALU.mult))
                    own.mark(nc.vector.tensor_tensor(rt2[:, :, 0:h], src[:, :, h:], bc(ss[:, lt:lt + 1, 0:h], [P, 4, h]), ALU.mult))
                    own(nc.vector.tensor_tensor(rt2[:, :, h:], src[:, :, 0:h], bc(ss[:, lt:lt + 1, h:], [P, 4, h]), ALU.mult))
                    nc.vector.tensor_tensor(rot[:, t % 2], rt1[:], rt2[:], ALU.add).then_inc(rotated, 1)

                def row_max(t, comp):
                    dve.wait_ge(scored, i * (2 * TILES) + (2 * t + comp + 1))
                    m = mx[:, t % 2, comp:comp + 1]
                    own(nc.vector.tensor_reduce(m, s_ps[comp][:, 0:keys(t)], AX.X, ALU.max))
                    nc.vector.tensor_scalar(nb[:, t % 2, comp:comp + 1], m, -SCALE, None, ALU.mult).then_inc(maxed, 1)

                def mix(t):
                    dve.wait_ge(exped, i * (2 * TILES) + (2 * t + 2))
                    if t >= 1:
                        dve.wait_ge(a_turned, i * TILES + t)
                    n = keys(t)
                    own(nc.vector.reciprocal(r[:, t % 2], l[:, t % 2]))
                    own(nc.vector.tensor_tensor(r[:, t % 2, 1:2], r[:, t % 2, 1:2], g.neg_lam[:], ALU.mult))
                    own(nc.vector.tensor_scalar(diff[:, 0:n], prob[:, t % 2, 1, 0:n], r[:, t % 2, 1:2], None, ALU.mult))
                    nc.vector.scalar_tensor_tensor(out=diff[:, 0:n], in0=prob[:, t % 2, 0, 0:n],
                                                   scalar=r[:, t % 2, 0:1], in1=diff[:, 0:n],
                                                   op0=ALU.mult, op1=ALU.add).then_inc(mixed, 1)

                for t in range(TILES):
                    rotate(t)
                row_max(0, 0)
                row_max(0, 1)
                for t in range(TILES):
                    if t + 1 < TILES:
                        row_max(t + 1, 0)
                    mix(t)
                    if t + 1 < TILES:
                        row_max(t + 1, 1)
            own.leave(DA_HEADS)

        @block.scalar
        def _(act):
            with act.Fori(0, DA_HEADS) as i:
                def exponentiate(t, comp):
                    act.wait_ge(maxed, i * (2 * TILES) + (2 * t + comp + 1))
                    if t >= 2:
                        act.wait_ge(mixed, i * TILES + (t - 1))
                    n = keys(t)
                    nc.scalar.activation(prob[:, t % 2, comp, 0:n], s_ps[comp][:, 0:n], ACT.Exp,
                                         bias=nb[:, t % 2, comp:comp + 1], scale=SCALE,
                                         accum_out=l[:, t % 2, comp:comp + 1]).then_inc(exped, 1)

                def copy_a(t):
                    act.wait_ge(a_turned, i * TILES + (t + 1))
                    n = keys(t) // P
                    nc.scalar.activation(aT[:, t % 2, 0:n], at_ps[:, 0:n], ACT.Copy).then_inc(a_copied, 1)

                def keep_o(t):
                    act.wait_ge(pv_done, i * TILES + (t + 1))
                    nc.scalar.activation(o_tok[:, t, ds(i * P, P)], ps[:, 6 + t % 2, 0:P],
                                         ACT.Copy).then_inc(o_kept, 1)

                for t in range(TILES):
                    act.wait_ge(rotated, i * TILES + (t + 1))
                    nc.scalar.activation(v[:, t], ps[:, t % 2, 2 * P:3 * P], ACT.Copy).then_inc(v_copied, 1)
                    if t >= 1:
                        copy_qk(nc, act, i, t - 1, qk_turned, qk_copied, qT, kT, ps)
                copy_qk(nc, act, i, TILES - 1, qk_turned, qk_copied, qT, kT, ps)
                exponentiate(0, 0)
                exponentiate(0, 1)
                for t in range(TILES):
                    if t + 1 < TILES:
                        exponentiate(t + 1, 0)
                        exponentiate(t + 1, 1)
                    if t >= 1:
                        keep_o(t - 1)
                    copy_a(t)
                keep_o(TILES - 1)


def copy_qk(nc, act, i, t, qk_turned, qk_copied, qT, kT, ps):
    act.wait_ge(qk_turned, i * TILES + (t + 1))
    nc.scalar.activation(qT[:, t * P:(t + 1) * P], ps[:, 2 + t % 2, 0:P], ACT.Copy)
    nc.scalar.activation(kT[:, t * P:(t + 1) * P], ps[:, 2 + t % 2, P:2 * P], ACT.Copy).then_inc(qk_copied, 1)


def load_norm(g, eng, layer, sub, vec, landed):
    for s in range(2):
        a = (layer * ADA + 3 * sub + 2) * D
        eng.dma_start(vec[:, s], g.mod_d[s, a:a + D].partition_broadcast(P)).then_inc(landed, 16)
    eng.dma_start(vec[:, 2], g.d.ln_g[layer, sub].partition_broadcast(P)).then_inc(landed, 16)
    eng.dma_start(vec[:, 3], g.d.ln_b[layer, sub].partition_broadcast(P)).then_inc(landed, 16)


def post_norm_tile(nc, dve, own, g, vec, t, y, u, st, mv, var_sem, root_sem, n, out_sem):
    own(nc.vector.tensor_tensor(u, y, vec[:, stream_of(t)], ALU.mult))
    own(nc.vector.scalar_tensor_tensor(out=u, in0=g.x[:, t], scalar=DN_ALPHA, in1=u, op0=ALU.mult, op1=ALU.add))
    own.mark(nc.vector.bn_stats(st[:, 0:6], u[:, 0:BANK]))
    own(nc.vector.bn_stats(st[:, 6:12], u[:, BANK:D]))
    own(nc.vector.bn_aggr(mv[:, 0:2], st))
    nc.vector.tensor_scalar(mv[:, 1:2], mv[:, 1:2], LN_EPS, None, ALU.add).then_inc(var_sem, 1)
    own(nc.vector.scalar_tensor_tensor(out=u, in0=u, scalar=mv[:, 0:1], in1=vec[:, 2], op0=ALU.subtract, op1=ALU.mult))
    dve.wait_ge(root_sem, n + 1)
    own(nc.vector.reciprocal(mv[:, 1:2], mv[:, 1:2]))
    nc.vector.scalar_tensor_tensor(out=g.x[:, t], in0=u, scalar=mv[:, 1:2], in1=vec[:, 3],
                                   op0=ALU.mult, op1=ALU.add).then_inc(out_sem, 1)


def root(nc, act, x, done):
    nc.scalar.activation(x, x, ACT.Sqrt).then_inc(done, 1)


def project_out(nc, g, sem, layer, w_src, heads, o_tok, z_d, head_gain, tiles):
    KO, tag = heads, str(layer)
    vec_in = sem("po_vec" + tag)
    w_in, turned, copied = [sem(f"po_w{tag}_{q}") for q in range(4)], sem("po_turned" + tag), sem("po_copied" + tag)
    y_done, x_done, own_sem = sem("po_y" + tag), sem("po_x" + tag), sem("po_own" + tag)
    var_done, var_root = sem("po_var" + tag), sem("po_var_root" + tag)
    ms_done, ms_root, normed = sem("po_ms" + tag), sem("po_ms_root" + tag), sem("po_normed" + tag)
    z_in = [sem(f"po_z{tag}_{s}") for s in range(2)]
    G, N = KO // 4, len(tiles)
    shape = [P, KO, P]
    with nc.sbuf_tensor("po_wo" + tag, [P, KO, D], F32) as wo, nc.sbuf_tensor("po_oT" + tag, [P, 2, KO, P], F32) as oT, \
            nc.sbuf_tensor("po_u" + tag, [P, D], F32) as u, nc.sbuf_tensor("po_st" + tag, [P, 12], F32) as st, \
            nc.sbuf_tensor("po_vecs" + tag, [P, 4, D], F32) as vec, \
            nc.sbuf_tensor("po_mv" + tag, [P, 2], F32) as mv, nc.sbuf_tensor("po_sq" + tag, [P, KO * P], F32) as sq, \
            nc.sbuf_tensor("po_ms" + tag, [P, KO], F32) as ms, \
            nc.sbuf_tensor("po_z" + tag, [P, 2, KO * P if z_d is not None else 1], F32) as z, \
            nc.psum_tensor("po_ps" + tag, [P, 8, BANK], F32) as ps, nc.Block() as block:
        @block.sync
        def _(sp):
            if z_d is not None:
                for n in range(2):
                    sp.dma_start(z[:, n], z_d[:, n]).then_inc(z_in[n], 16)
            for q in range(4):
                sp.dma_start(wo[:, q * G:(q + 1) * G],
                             w_src.rearrange("(p k) n -> p k n", k=KO)[:, q * G:(q + 1) * G]).then_inc(w_in[q], 16)
            load_norm(g, sp, layer, 0, vec, vec_in)
            if z_d is not None:
                for n in range(2, N):
                    sp.wait_ge(normed, n - 1)
                    sp.dma_start(z[:, n % 2], z_d[:, n]).then_inc(z_in[n % 2], 16)

        @block.tensor
        def _(pe):
            def turn(n):
                pe.wait_ge(normed, n + 1)
                for q in range(G):
                    b = n * G + q
                    if b >= 4:
                        pe.wait_ge(copied, b - 3)
                    for a in range(4):
                        last = nc.tensor.transpose(ps[:, 4 + b % 4, a * P:(a + 1) * P],
                                                   o_tok[:, n, 4 * q + a::KO], g.ident[:])
                    last.then_inc(turned, 1)

            turn(0)
            for n in range(N):
                if n + 1 < N:
                    turn(n + 1)
                pe.wait_ge(copied, (n + 1) * G)
                if n >= 2:
                    pe.wait_ge(x_done, n - 1)
                for half in range(2):
                    for k in range(KO):
                        if n == 0 and half == 0 and k % G == 0:
                            pe.wait_ge(w_in[k // G], 16)
                        last = nc.tensor.matmul(ps[:, 2 * (n % 2) + half], oT[:, n % 2, k],
                                                wo[:, k, half * BANK:(half + 1) * BANK],
                                                start=(k == 0), stop=(k == KO - 1))
                last.then_inc(y_done, 1)

        @block.scalar
        def _(act):
            def copy_o(n):
                if n >= 2:
                    act.wait_ge(y_done, n - 1)
                for q in range(G):
                    b = n * G + q
                    act.wait_ge(turned, b + 1)
                    nc.scalar.activation(oT[:, n % 2, 4 * q:4 * q + 4].rearrange("p a b -> p (a b)"),
                                         ps[:, 4 + b % 4], ACT.Copy).then_inc(copied, 1)

            for n in range(N + 2):
                if n < N:
                    act.wait_ge(ms_done, n + 1)
                    root(nc, act, ms[:], ms_root)
                    copy_o(n)
                if n >= 2:
                    act.wait_ge(var_done, n - 1)
                    root(nc, act, mv[:, 1:2], var_root)

        @block.vector
        def _(dve):
            own = Own(dve, own_sem)

            def norm_heads(n):
                o = o_tok[:, n]
                own(nc.vector.tensor_tensor(sq[:], o, o, ALU.mult))
                own(nc.vector.tensor_reduce(ms[:], sq[:].rearrange("p (h d) -> p h d", d=P), AX.X, ALU.add))
                nc.vector.tensor_scalar(ms[:], ms[:], 1.0 / P, NORM_EPS, ALU.mult, ALU.add).then_inc(ms_done, 1)
                dve.wait_ge(ms_root, n + 1)
                own(nc.vector.reciprocal(ms[:], ms[:]))
                oh = o.rearrange("p (h d) -> p h d", d=P)
                own(nc.vector.tensor_tensor(oh, oh, bc(ms[:].unsqueeze(2), shape), ALU.mult))
                if z_d is not None:
                    dve.wait_ge(z_in[n % 2], 16 * (n // 2 + 1))
                    own(nc.vector.tensor_tensor(o, o, z[:, n % 2], ALU.mult))
                nc.vector.tensor_tensor(oh, oh, bc(head_gain.unsqueeze(1), shape), ALU.mult).then_inc(normed, 1)
                dve.wait_ge(normed, n + 1)

            for n in range(N + 2):
                if n < N:
                    norm_heads(n)
                if n >= 2:
                    m = n - 2
                    dve.wait_ge(y_done, m + 1)
                    if m == 0:
                        dve.wait_ge(vec_in, 64)
                    y = ps[:, 2 * (m % 2):2 * (m % 2) + 2].rearrange("p a b -> p (a b)")
                    post_norm_tile(nc, dve, own, g, vec, tiles[m], y, u[:], st[:], mv[:], var_done, var_root, m, x_done)
                    dve.wait_ge(x_done, m + 1)


def most_blocks(tiles):
    return (len(tiles) * P * TOP_K + E * (P - 1)) // P


RUN = 4


def lane_blocks(tiles):
    return -(-(most_blocks(tiles) // 2 + len(tiles)) // RUN) * RUN


def slots(tiles):
    return 2 * (lane_blocks(tiles) + 2)


def moe(nc, g, sem, layer, tiles):
    NBLK = 2 * lane_blocks(tiles)
    tag = str(layer)
    with ExitStack() as c:
        sb = lambda name, shape, dt: c.enter_context(nc.sbuf_tensor(f"moe_{name}{layer}", shape, dt))
        m = named(
            "Moe", tag=str(layer), tiles=tiles, N=len(tiles), NBLK=NBLK,
            slot_token=nc.dram_tensor(f"slot_token{layer}", (slots(tiles) * P, 2), I32, kind="Internal").ap(),
            expert=sb("expert", [1, 2 * P], I32), fresh=sb("fresh", [1, 2 * P], I32), n_blocks=sb("n_blocks", [1, 1], I32),
            wg=[sb(f"wg{s}", [P, KD, 2 * FF], F32) for s in range(2)], wd=[sb(f"wd{s}", [P, 2, D], F32) for s in range(2)],
            vec=sb("vecs", [P, 4, D], F32), vec_in=sem("mb_vec" + tag),
            wg_in=[sem(f"mb_wg{tag}_{s}") for s in range(2)], wd_in=[sem(f"mb_wd{tag}_{s}") for s in range(2)],
            wg_dram=g.d.moe_w_gu[layer].rearrange("e (p k) n -> e p k n", k=KD),
            wd_dram=g.d.moe_w_dn[layer].rearrange("e (p k) n -> e p k n", k=2))
        with nc.sbuf_tensor(f"hT_m{layer}", [P, KD, TOKENS], F32) as g.hT:
            route_and_share(nc, g, sem, layer, m)
        run_blocks(nc, g, sem, layer, m)
        finish_moe(nc, g, sem, layer, m)


def route_and_share(nc, g, sem, layer, m):
    tag, N, tiles = m.tag, m.N, m.tiles
    landed, logits, scored = sem("rt_in" + tag), sem("rt_logits" + tag), sem("rt_scored" + tag)
    masked, counted, placed = sem("rt_masked" + tag), sem("rt_counted" + tag), sem("rt_placed" + tag)
    own_sem, based, be_col = sem("rt_own" + tag), sem("rt_based" + tag), sem("rt_be" + tag)
    be_row, cleared, experts_set = sem("rt_be_row" + tag), sem("rt_cleared" + tag), sem("rt_experts" + tag)
    shared_in, up, silu, act_done = sem("sh_in" + tag), sem("sh_up" + tag), sem("sh_silu" + tag), sem("sh_act" + tag)
    stored = [sem(f"sh_stored{tag}_{s}") for s in range(2)]
    scattered = sem("sh_scattered" + tag)
    turned, copied, down, kept = sem("sh_turned" + tag), sem("sh_copied" + tag), sem("sh_down" + tag), sem("sh_kept" + tag)
    with ExitStack() as c:
        sb = lambda name, shape, dt=F32: c.enter_context(nc.sbuf_tensor("rt_" + name + tag, shape, dt))
        w, bias, ranks, index = sb("w", [P, KD, E]), sb("bias", [P, E]), sb("ranks", [P, TOP_K, E]), sb("index", [P, 1])
        tokens = sb("tokens", [P, TILES], I32)
        slot_idx, pair = sb("slot_idx", [P, TILES, TOP_K], I32), sb("pair", [P, TILES, TOP_K, 2], I32)
        score, biased, top, left = sb("score", [P, TILES, E]), sb("biased", [P, E]), sb("top", [P, 8]), sb("left", [P, E])
        mask, wfull, wsum = sb("mask", [P, TILES, E]), sb("wfull", [P, TILES, E]), sb("wsum", [P, 1])
        nb, end, base, one = sb("nb", [P, E]), sb("end", [P, E]), sb("base", [P, E]), sb("one", [P, E])
        rank, eq, prod, slot, slot8 = (sb("rank", [P, E]), sb("eq", [P, TOP_K, E]), sb("prod", [P, TOP_K, E]),
                                       sb("slot", [P, E]), sb("slot8", [P, TOP_K]))
        le, be, row = sb("le", [P, E]), sb("becol", [P, 2]), sb("row", [1, 2 * P])
        lane, total, len0, step, index1 = sb("lane", [P, E]), sb("total", [P, 1]), sb("len0", [P, 1]), sb("step", [P, 1]), sb("index1", [P, 1])
        shared = lambda name, shape: sb("shared_" + name, shape)
        wg, wd, y = shared("wg", [P, KD, 2 * FF]), shared("wd", [P, 2, D]), shared("y", [P, 2, D])
        sg, a, aT = shared("sg", [P, 2, FF]), shared("a", [P, 2, FF]), shared("aT", [P, 2, 2, P])
        def load_first(sp):
            for dst, src in ((w[:], g.d.moe_router[layer].rearrange("(p k) e -> p k e", k=KD)),
                             (bias[:], g.d.moe_router_b[layer].partition_broadcast(P)),
                             (ranks[:], g.d.c_ranks), (index[:], g.d.c_index), (tokens[:], g.d.c_tokens)):
                sp.dma_start(dst, src).then_inc(landed, 16)
            sp.dma_start(m.slot_token.rearrange("(p b) a -> p (b a)", p=P),
                         g.d.c_empty.rearrange("(p b) a -> p (b a)", p=P) if layer == 0 else
                         g.d.c_empty[0:slots(tiles) * P].rearrange("(p b) a -> p (b a)", p=P)).then_inc(cleared, 16)
            sp.dma_start(wg[:], g.d.moe_ws_gu[layer].rearrange("(p k) n -> p k n", k=KD)).then_inc(shared_in, 16)
            sp.dma_start(wd[:], g.d.moe_ws_dn[layer].rearrange("(p k) n -> p k n", k=2)).then_inc(shared_in, 16)

        modulate(nc, g, sem, layer, 1, tiles, True, load_first)
        ps = c.enter_context(nc.psum_tensor("rt_ps" + tag, [P, 8, BANK], F32))
        COUNTS, TURN, E_ROW = ps[:, 3, N * E:(N + 1) * E], ps[:, 2, 0:2 * P], ps[0:1, 2, 2 * P:4 * P]
        block = c.enter_context(nc.Block())
        FIRST = tiles[0]

        @block.sync
        def _(sp):
            sp.wait_ge(experts_set, 1)
            for s in range(2):
                e = sp.value_load(m.expert[0:1, s * P:s * P + 1], min_val=0, max_val=E - 1)
                sp.dma_start(m.wg[s][:], m.wg_dram[e]).then_inc(m.wg_in[s], 16)
                sp.dma_start(m.wd[s][:], m.wd_dram[e]).then_inc(m.wd_in[s], 16)
            for n, t in enumerate(tiles):
                sp.wait_ge(kept, n + 1)
                sp.dma_start(g.acc_d[t * P:(t + 1) * P], y[:, n % 2]).then_inc(stored[n % 2], 16)
            for s in range(2):
                sp.wait_ge(stored[s], 16 * (N // 2))

        @block.gpsimd
        def _(pool):
            pool.wait_ge(cleared, 16)
            for n in range(N):
                pool.wait_ge(placed, n + 1)
                for k in range(TOP_K):
                    pool.indirect_dma_start(
                        m.slot_token, bass.IndirectOffsetOnAxis(ap=slot_idx[:, n, k:k + 1], axis=0),
                        pair[:, n, k], None).then_inc(scattered, 16)
            pool.wait_ge(scattered, 16 * TOP_K * N)

        @block.tensor
        def _(pe):
            pe.wait_ge(landed, 16 * 5)
            for n, t in enumerate(tiles):
                if n >= 2:
                    pe.wait_ge(scored, n - 1)
                for k in range(KD):
                    last = nc.tensor.matmul(ps[:, n % 2, 0:E], g.hT[:, k, t * P:(t + 1) * P], w[:, k],
                                            start=(k == 0), stop=(k == KD - 1))
                last.then_inc(logits, 1)

            def project_up(n):
                if n >= 2:
                    pe.wait_ge(act_done, n - 1)
                t = tiles[n]
                for k in range(KD):
                    last = nc.tensor.matmul(ps[:, n % 2], g.hT[:, k, t * P:(t + 1) * P], wg[:, k],
                                            start=(k == 0), stop=(k == KD - 1))
                last.then_inc(up, 1)

            pe.wait_ge(scored, N)
            pe.wait_ge(shared_in, 32)
            project_up(0)
            pe.wait_ge(masked, N)
            for n in range(N):
                for b in range(n):
                    nc.tensor.matmul(ps[:, 3, n * E:(n + 1) * E], g.ones[:], mask[:, b], start=(b == 0), stop=False)
                nc.tensor.matmul(ps[:, 3, n * E:(n + 1) * E], g.upper[:, 1], mask[:, n], start=(n == 0), stop=True)
            for n in range(N):
                last = nc.tensor.matmul(COUNTS, g.ones[:], mask[:, n], start=(n == 0), stop=(n == N - 1))
            last.then_inc(counted, 1)
            project_up(1)
            pe.wait_ge(be_col, 1)
            for s in range(2):
                last = nc.tensor.transpose(E_ROW[:, s * P:(s + 1) * P], be[:, s:s + 1], g.ident[:])
            last.then_inc(be_row, 1)
            pe.wait_ge(experts_set, 1)
            for n in range(N):
                if 1 <= n < N - 1:
                    project_up(n + 1)
                pe.wait_ge(act_done, n + 1)
                if n:
                    pe.wait_ge(copied, n)
                for k in range(2):
                    last = nc.tensor.transpose(TURN[:, k * P:(k + 1) * P], a[:, n % 2, k::2], g.ident[:])
                last.then_inc(turned, 1)
                pe.wait_ge(copied, n + 1)
                if n >= 2:
                    pe.wait_ge(kept, n - 1)
                for half in range(2):
                    for k in range(2):
                        last = nc.tensor.matmul(ps[:, 4 + 2 * (n % 2) + half], aT[:, n % 2, k],
                                                wd[:, k, half * BANK:(half + 1) * BANK], start=(k == 0), stop=(k == 1))
                last.then_inc(down, 1)

        @block.scalar
        def _(act):
            for n in range(N):
                act.wait_ge(logits, n + 1)
                nc.scalar.activation(score[:, n], ps[:, n % 2, 0:E], ACT.Sigmoid).then_inc(scored, 1)
            for n in range(N + 1):
                if n < N:
                    act.wait_ge(up, n + 1)
                    if n >= 2:
                        act.wait_ge(act_done, n - 1)
                    nc.scalar.activation(sg[:, n % 2], ps[:, n % 2, 0:FF], ACT.Silu).then_inc(silu, 1)
                    act.wait_ge(turned, n + 1)
                    nc.scalar.activation(aT[:, n % 2].rearrange("p a b -> p (a b)"), TURN, ACT.Copy).then_inc(copied, 1)
                if n >= 1:
                    act.wait_ge(down, n)
                    b = 4 + 2 * ((n - 1) % 2)
                    if n >= 3:
                        act.wait_ge(stored[(n - 1) % 2], 16 * ((n - 1) // 2))
                    nc.scalar.activation(y[:, (n - 1) % 2], ps[:, b:b + 2].rearrange("p a b -> p (a b)"),
                                         ACT.Copy).then_inc(kept, 1)

        @block.vector
        def _(dve):
            own = Own(dve, own_sem)
            own(nc.vector.memset(one[:], 1.0))
            for n in range(N):
                dve.wait_ge(scored, n + 1)
                own(nc.vector.tensor_tensor(biased[:], score[:, n], bias[:], ALU.add))
                own(nc.vector.max(top[:], biased[:]))
                own(nc.vector.match_replace(left[:], top[:], biased[:], -1e30))
                own(nc.vector.tensor_tensor(mask[:, n], left[:], biased[:], ALU.not_equal))
                own(nc.vector.tensor_tensor(wfull[:, n], score[:, n], mask[:, n], ALU.mult))
                own(nc.vector.tensor_reduce(wsum[:], wfull[:, n], AX.X, ALU.add))
                own(nc.vector.reciprocal(wsum[:], wsum[:]))
                nc.vector.tensor_scalar(wfull[:, n], wfull[:, n], wsum[:], ROUTE_SCALE, ALU.mult,
                                        ALU.mult).then_inc(masked, 1)
                dve.wait_ge(masked, n + 1)

            def gate(n):
                dve.wait_ge(silu, n + 1)
                if n >= 2:
                    dve.wait_ge(turned, n - 1)
                nc.vector.tensor_tensor(a[:, n % 2], sg[:, n % 2], ps[:, n % 2, FF:2 * FF], ALU.mult).then_inc(act_done, 1)

            gate(0)
            dve.wait_ge(counted, 1)
            own(nc.vector.tensor_scalar(nb[:], COUNTS, 0.0, None, ALU.is_gt))
            for b in range(1, N):
                own(nc.vector.scalar_tensor_tensor(out=nb[:], in0=COUNTS, scalar=float(b * P), in1=nb[:],
                                                   op0=ALU.is_gt, op1=ALU.add))
            own(nc.vector.tensor_tensor_scan(end[:], one[:], nb[:], 0.0, ALU.mult, ALU.add))
            own(nc.vector.tensor_tensor(base[:], end[:], nb[:], ALU.subtract))
            own(nc.vector.tensor_copy(total[:], end[:, E - 1:E]))
            own(nc.vector.tensor_scalar(lane[:], base[:], 2.0, total[:], ALU.mult, ALU.is_ge))
            own(nc.vector.tensor_tensor(le[:], nb[:], lane[:], ALU.mult))
            own(nc.vector.tensor_reduce(step[:], le[:], AX.X, ALU.add))
            own(nc.vector.tensor_tensor(len0[:], total[:], step[:], ALU.subtract))
            own(nc.vector.tensor_tensor(total[:], len0[:], step[:], ALU.max))
            own(nc.vector.tensor_scalar(total[:], total[:], 2.0, None, ALU.mult))
            own(nc.vector.tensor_copy(m.n_blocks[:], total[0:1]))
            own(nc.vector.tensor_tensor(index1[:], index[:], len0[:], ALU.add))
            for s, at in enumerate((index, index1)):
                own(nc.vector.tensor_scalar(le[:], end[:], at[:], None, ALU.is_le))
                own(nc.vector.tensor_reduce(be[:, s:s + 1], le[:], AX.X, ALU.add))
            nc.vector.tensor_scalar(be[:], be[:], float(E - 1), None, ALU.min).then_inc(be_col, 1)
            own(nc.vector.tensor_scalar(base[:], base[:], float(P), None, ALU.mult))
            own(nc.vector.tensor_scalar(step[:], len0[:], -float(P), float(slots(tiles) // 2 * P), ALU.mult, ALU.add))
            own(nc.vector.scalar_tensor_tensor(out=base[:], in0=lane[:], scalar=step[:], in1=base[:],
                                               op0=ALU.mult, op1=ALU.add))
            dve.wait_ge(be_row, 1)
            own(nc.vector.tensor_copy(row[:], E_ROW))
            own.mark(nc.vector.tensor_copy(m.expert[:], row[:]))
            own.mark(nc.vector.memset(m.fresh[:, 0:1], 1))
            own(nc.vector.tensor_tensor(m.fresh[:, 1:], row[:, 1:], row[:, 0:2 * P - 1], ALU.not_equal))
            dve.sem_inc(experts_set, 1)

            def place(n):
                own(nc.vector.tensor_tensor(slot[:], ps[:, 3, n * E:(n + 1) * E], base[:], ALU.add))
                own(nc.vector.tensor_tensor_scan(rank[:], one[:], mask[:, n], 0.0, ALU.mult, ALU.add))
                own(nc.vector.tensor_tensor(rank[:], rank[:], mask[:, n], ALU.mult))
                shape = [P, TOP_K, E]
                own(nc.vector.tensor_tensor(eq[:], bc(rank[:].unsqueeze(1), shape), ranks[:], ALU.is_equal))
                own(nc.vector.tensor_tensor(prod[:], eq[:], bc(slot[:].unsqueeze(1), shape), ALU.mult))
                own(nc.vector.tensor_reduce(slot8[:], prod[:], AX.X, ALU.add))
                own.mark(nc.vector.tensor_copy(slot_idx[:, n], slot8[:]))
                own.mark(nc.vector.tensor_copy(pair[:, n, :, 0:1], bc(tokens[:, FIRST + n:FIRST + n + 1].unsqueeze(1), [P, TOP_K, 1])))
                own(nc.vector.tensor_tensor(prod[:], eq[:], bc(wfull[:, n].unsqueeze(1), shape), ALU.mult))
                nc.vector.tensor_reduce(pair[:, n].bitcast(F32)[:, :, 1:2], prod[:], AX.X, ALU.add).then_inc(placed, 1)
                dve.wait_ge(placed, n + 1)

            for n in range(1, N + 2):
                for b in (2 * n - 2, 2 * n - 1):
                    if b < N:
                        place(b)
                if n < N:
                    gate(n)


def run_blocks(nc, g, sem, layer, m):
    tag, NBLK = m.tag, m.NBLK
    two = lambda name: [sem(f"mb_{name}{tag}_{s}") for s in range(2)]
    wg_in, wd_in, idx_in, x_in, to_in = m.wg_in, m.wd_in, two("idx"), two("x"), two("to")
    x_turned, x_copied, up, silu, act_done = two("x_turned"), two("x_copied"), two("up"), two("silu"), two("act")
    a_turned, a_copied, down, y_lo, y_hi = two("a_turned"), two("a_copied"), two("down"), two("y_lo"), two("y_hi")
    added, held = sem("mb_added" + tag), sem("mb_held" + tag)
    with ExitStack() as c:
        sb = lambda name, shape, dt=F32: c.enter_context(nc.sbuf_tensor("mb_" + name + tag, shape, dt))
        wg, wd, wg_dram, wd_dram = m.wg, m.wd, m.wg_dram, m.wd_dram
        idx = [sb(f"idx{s}", [P, 2], I32) for s in range(2)]
        spare = sb("spare", [P, 2], I32)
        to = [sb(f"to{s}", [P, 2], I32) for s in range(2)]
        xg = [sb(f"xg{s}", [P, D]) for s in range(2)]
        xT = [sb(f"xT{s}", [P, KD, P]) for s in range(2)]
        sg = [sb(f"sg{s}", [P, FF]) for s in range(2)]
        a = [sb(f"a{s}", [P, FF]) for s in range(2)]
        aT = [sb(f"aT{s}", [P, 2, P]) for s in range(2)]
        y = [sb(f"y{s}", [P, D]) for s in range(2)]
        ps = c.enter_context(nc.psum_tensor("mb_ps" + tag, [P, 8, BANK], F32))
        x_ps, up_ps, a_ps, y_ps = ps[:, 0:2], ps[:, 2:4], ps[:, 4:6], ps[:, 6:8]
        block = c.enter_context(nc.Block())
        tok_dram = m.slot_token.rearrange("(s b p) a -> s b p a", s=2, p=P)
        ADDED0 = 32

        def count(eng):
            return eng.value_load(m.n_blocks[0:1, 0:1], min_val=TOP_K, max_val=NBLK)

        @block.sync
        def _(sp):
            n = count(sp)
            sp.dma_start(to[0][:], tok_dram[0, 0]).then_inc(to_in[0], 16)
            load_norm(g, sp, layer, 1, m.vec, m.vec_in)

            def renew(s, j, buffers, dram, used, landed):
                e = sp.value_load(m.expert[0:1, ds(j + s * P, 1)], min_val=0, max_val=E - 1)
                fresh = sp.value_load(m.fresh[0:1, ds(j + s * P, 1)], min_val=0, max_val=1)
                with sp.If(fresh > 0):
                    sp.wait_ge(used[s], j)
                    sp.dma_start(buffers[s][:], dram[e]).then_inc(landed[s], 16)
                with sp.If(fresh < 1):
                    sp.wait_ge(used[s], j)
                    sp.sem_inc(landed[s], 16)

            renew(0, 1, wg, wg_dram, up, wg_in)
            with sp.Fori(0, NBLK // 2 // RUN) as run, sp.If(run * (2 * RUN) < n), sp.Fori(0, RUN) as step:
                i = run * RUN + step
                for s in range(2):
                    with sp.If(i * 2 + (2 * s + 2) < n):
                        renew(1 - s, i + (1 + s), wg, wg_dram, up, wg_in)
                    with sp.If(i * 2 + 2 < n):
                        renew(s, i + 1, wd, wd_dram, down, wd_in)
                    with sp.If(i * 2 + s < n):
                        sp.wait_ge(added, i * 32 + (16 * s + ADDED0))
                        sp.dma_start(to[1 - s][:], tok_dram[1 - s, i + s]).then_inc(to_in[1 - s], 16)
            sp.wait_ge(to_in[0], n * 8 + 16)
            sp.wait_ge(to_in[1], n * 8)
            sp.sem_inc(held, 1)

        @block.gpsimd
        def _(pool):
            n = count(pool)
            for a in range(2):
                pool.dma_start(spare[:], tok_dram[0, 0]).then_inc(added, 16)
                pool.wait_ge(added, 16 * (a + 1))

            def gather(s, j):
                pool.dma_start(idx[s][:], tok_dram[s, j]).then_inc(idx_in[s], 16)
                pool.wait_ge(idx_in[s], j * 16 + 16)
                pool.sem_inc(held, 1)
                pool.indirect_dma_start(xg[s][:], None, g.h_d, bass.IndirectOffsetOnAxis(ap=idx[s][:, 0:1], axis=0)
                                        ).then_inc(x_in[s], 16)

            gather(0, 0)
            gather(1, 0)
            pool.wait_ge(x_turned[0], 1)
            gather(0, 1)
            with pool.Fori(0, NBLK // 2 // RUN) as run, pool.If(run * (2 * RUN) < n), pool.Fori(0, RUN) as step:
                i = run * RUN + step
                for s in range(2):
                    with pool.If(i * 2 + s < n):
                        pool.wait_ge(x_turned[1 - s], i + (s + 1))
                        gather(1 - s, i + (s + 1))
                        pool.wait_ge(to_in[s], i * 16 + 16)
                        pool.wait_ge(y_lo[s], i + (s + 1))
                        pool.wait_ge(y_hi[s], i + (s + 1))
                        pool.wait_ge(added, i * 32 + (16 * s + ADDED0))
                        pool.sem_inc(held, 1)
                        pool.indirect_dma_start(g.acc_d, bass.IndirectOffsetOnAxis(ap=to[s][:, 0:1], axis=0), y[s][:], None,
                                                compute_op=ALU.add).then_inc(added, 16)
            pool.wait_ge(added, n * 16 + ADDED0)
            for s in range(2):
                pool.wait_ge(x_in[s], n * 8 + (32 - 16 * s))
            pool.sem_inc(held, 1)

        @block.tensor
        def _(pe):
            n = count(pe)

            def turn_x(s, j):
                pe.wait_ge(x_in[s], j * 16 + 16)
                for k in range(KD):
                    last = nc.tensor.transpose(x_ps[:, k // 4, (k % 4) * P:(k % 4 + 1) * P], xg[s][:, k::KD], g.ident[:])
                last.then_inc(x_turned[s], 1)

            def project_up(s, j):
                pe.wait_ge(x_copied[s], j + 1)
                pe.wait_ge(wg_in[s], j * 16 + 16)
                for k in range(KD):
                    last = nc.tensor.matmul(up_ps[:, s], xT[s][:, k], wg[s][:, k], start=(k == 0), stop=(k == KD - 1))
                last.then_inc(up[s], 1)

            def turn_a(s, j):
                pe.wait_ge(act_done[s], j + 1)
                for k in range(2):
                    last = nc.tensor.transpose(a_ps[:, s, k * P:(k + 1) * P], a[s][:, k::2], g.ident[:])
                last.then_inc(a_turned[s], 1)

            def project_down(s, j):
                pe.wait_ge(a_copied[s], j + 1)
                pe.wait_ge(wd_in[s], j * 16 + 16)
                pe.wait_ge(y_lo[1 - s], j + 1)
                pe.wait_ge(y_hi[1 - s], j + 1)
                for half in range(2):
                    for k in range(2):
                        last = nc.tensor.matmul(y_ps[:, half], aT[s][:, k], wd[s][:, k, half * BANK:(half + 1) * BANK],
                                                start=(k == 0), stop=(k == 1))
                last.then_inc(down[s], 1)

            turn_x(0, 0)
            project_up(0, 0)
            turn_x(1, 0)
            turn_a(0, 0)
            with pe.Fori(0, NBLK // 2 // RUN) as run, pe.If(run * (2 * RUN) < n), pe.Fori(0, RUN) as step:
                i = run * RUN + step
                with pe.If(i * 2 < n):
                    project_up(1, i)
                    turn_x(0, i + 1)
                    project_down(0, i)
                    turn_a(1, i)
                with pe.If(i * 2 + 2 < n):
                    project_up(0, i + 1)
                    turn_x(1, i + 1)
                with pe.If(i * 2 < n):
                    project_down(1, i)
                with pe.If(i * 2 + 2 < n):
                    turn_a(0, i + 1)

        @block.scalar
        def _(act):
            n = count(act)
            act.sem_inc(y_hi[1], 1)

            def copy_x(s, j):
                act.wait_ge(x_turned[s], j + 1)
                nc.scalar.activation(xT[s][:].rearrange("p k n -> p (k n)"), x_ps.rearrange("p a b -> p (a b)"),
                                     ACT.Copy).then_inc(x_copied[s], 1)

            def silu_gate(s, j):
                act.wait_ge(up[s], j + 1)
                nc.scalar.activation(sg[s][:], up_ps[:, s, 0:FF], ACT.Silu).then_inc(silu[s], 1)

            def weigh_high(s, i):
                act.wait_ge(to_in[s], i * 16 + 16)
                act.wait_ge(down[s], i + 1)
                act.wait_ge(added, i * 32 + (16 * s + ADDED0 - 16))
                nc.scalar.activation(y[s][:, BANK:D], y_ps[:, 1], ACT.Copy,
                                     scale=to[s][:].bitcast(F32)[:, 1:2]).then_inc(y_hi[s], 1)

            copy_x(0, 0)
            silu_gate(0, 0)
            copy_x(1, 0)
            with act.Fori(0, NBLK // 2 // RUN) as run, act.If(run * (2 * RUN) < n), act.Fori(0, RUN) as step:
                i = run * RUN + step
                with act.If(i * 2 < n):
                    silu_gate(1, i)
                    copy_x(0, i + 1)
                    weigh_high(0, i)
                with act.If(i * 2 + 2 < n):
                    silu_gate(0, i + 1)
                    copy_x(1, i + 1)
                with act.If(i * 2 < n):
                    weigh_high(1, i)
            act.wait_ge(y_hi[1], 1)

        @block.vector
        def _(dve):
            n = count(dve)
            dve.sem_inc(y_lo[1], 1)

            def gate(s, j):
                dve.wait_ge(silu[s], j + 1)
                nc.vector.tensor_tensor(a[s][:], sg[s][:], up_ps[:, s, FF:2 * FF], ALU.mult).then_inc(act_done[s], 1)

            def copy_a(s, j):
                dve.wait_ge(a_turned[s], j + 1)
                nc.vector.tensor_copy(aT[s][:].rearrange("p a b -> p (a b)"), a_ps[:, s, 0:2 * P]).then_inc(a_copied[s], 1)

            def weigh_low(s, i):
                dve.wait_ge(to_in[s], i * 16 + 16)
                dve.wait_ge(down[s], i + 1)
                dve.wait_ge(added, i * 32 + (16 * s + ADDED0 - 16))
                nc.vector.tensor_scalar(y[s][:, 0:BANK], y_ps[:, 0], to[s][:].bitcast(F32)[:, 1:2], None,
                                        ALU.mult).then_inc(y_lo[s], 1)

            gate(0, 0)
            copy_a(0, 0)
            with dve.Fori(0, NBLK // 2 // RUN) as run, dve.If(run * (2 * RUN) < n), dve.Fori(0, RUN) as step:
                i = run * RUN + step
                with dve.If(i * 2 < n):
                    gate(1, i)
                    weigh_low(0, i)
                    copy_a(1, i)
                with dve.If(i * 2 + 2 < n):
                    gate(0, i + 1)
                with dve.If(i * 2 < n):
                    weigh_low(1, i)
                with dve.If(i * 2 + 2 < n):
                    copy_a(0, i + 1)


def finish_moe(nc, g, sem, layer, m):
    tag, N, tiles = m.tag, m.N, m.tiles
    got = [sem(f"fm_got{tag}_{n}") for n in range(N)]
    x_done, own_sem, gated, ready = sem("fm_x" + tag), sem("fm_own" + tag), sem("fm_gated" + tag), sem("fm_ready" + tag)
    var_done, var_root = sem("fm_var" + tag), sem("fm_root" + tag)
    vec = m.vec
    with ExitStack() as c:
        sb = lambda name, shape: c.enter_context(nc.sbuf_tensor("fm_" + name + tag, shape, F32))
        f, u, st, mv = sb("f", [P, N, D]), sb("u", [P, 2, D]), sb("st", [P, 12]), sb("mv", [P, 2, 2])
        block = c.enter_context(nc.Block())

        @block.sync
        def _(sp):
            for n, t in enumerate(tiles):
                sp.dma_start(f[:, n], g.acc_d[t * P:(t + 1) * P]).then_inc(got[n], 16)

        @block.gpsimd
        def _(pool):
            def gate(n):
                pool.wait_ge(got[n], 16)
                nc.gpsimd.tensor_tensor(f[:, n], f[:, n], vec[:, stream_of(tiles[n])], ALU.mult).then_inc(gated, 1)

            pool.wait_ge(m.vec_in, 64)
            gate(0)
            for n in range(1, N):
                gate(n)

        @block.scalar
        def _(act):
            for n in range(N):
                act.wait_ge(var_done, n + 1)
                root(nc, act, mv[:, n % 2, 1:2], var_root)
                act.wait_ge(ready, n + 1)
                nc.scalar.activation(u[:, n % 2], u[:, n % 2], ACT.Copy, scale=mv[:, n % 2, 1:2]).then_inc(x_done, 1)

        @block.vector
        def _(dve):
            own = Own(dve, own_sem)

            def add_bias(n):
                dve.wait_ge(x_done, n + 1)
                own(nc.vector.tensor_tensor(g.x[:, tiles[n]], u[:, n % 2], vec[:, 3], ALU.add))

            for n in range(N):
                un, mn = u[:, n % 2], mv[:, n % 2]
                dve.wait_ge(gated, n + 1)
                own(nc.vector.scalar_tensor_tensor(out=un, in0=g.x[:, tiles[n]], scalar=DN_ALPHA, in1=f[:, n],
                                                   op0=ALU.mult, op1=ALU.add))
                own.mark(nc.vector.bn_stats(st[:, 0:6], un[:, 0:BANK]))
                own(nc.vector.bn_stats(st[:, 6:12], un[:, BANK:D]))
                own(nc.vector.bn_aggr(mn[:, 0:2], st[:]))
                nc.vector.tensor_scalar(mn[:, 1:2], mn[:, 1:2], LN_EPS, None, ALU.add).then_inc(var_done, 1)
                own(nc.vector.scalar_tensor_tensor(out=un, in0=un, scalar=mn[:, 0:1], in1=vec[:, 2],
                                                   op0=ALU.subtract, op1=ALU.mult))
                dve.wait_ge(var_root, n + 1)
                nc.vector.reciprocal(mn[:, 1:2], mn[:, 1:2]).then_inc(ready, 1)
                if n:
                    add_bias(n - 1)
            add_bias(N - 1)


STEPS = TILES
PAIRS = STEPS // 2
LEVELS = 7
FRONT_AFTER = (0, 1, 3, 5)


def step_tiles(n):
    if n < CTX_TILES:
        return n, CTX_TILES - 1 - n
    return n, TILES - 1 - (n - CTX_TILES)


def load_head_qkv(g, eng, q, w, i):
    src = g.d.gdn_w_in[0].rearrange("(p k) n -> p k n", k=KD)
    for at, first, size in ((0, GDN_KEY, P), (1, 0, P), (2, 2 * GDN_KEY, 2 * P)):
        eng.dma_start(w[:, :, at * P:at * P + size], src[:, :, ds(i * size + first, size)]).then_inc(q.w_in, 16)


def load_head_z(g, eng, q, w, i):
    src = g.d.gdn_w_in[0].rearrange("(p k) n -> p k n", k=KD)
    eng.dma_start(w[:, :, 4 * P:6 * P], src[:, :, ds(i * (2 * P) + GDN_Z0, 2 * P)]).then_inc(q.wz_in, 16)


def gdn_gates(nc, g, sem, gates, conv, q, w_head, levels):
    landed, ab, turned, own_sem = sem("gg_in"), sem("gg_ab"), sem("gg_turned"), sem("gg_own")
    copied, arg1, exp1 = sem("gg_copied"), sem("gg_arg1"), sem("gg_exp1")
    abT_done, abT_copied = sem("gg_abT"), sem("gg_abT_copied")
    NG = 2 * HV
    with ExitStack() as c:
        sb = lambda name, shape: c.enter_context(nc.sbuf_tensor("gg_" + name, shape, F32))
        w, rows, abT = sb("w", [P, KD, 2 * NG]), sb("rows", [80, 2, P]), sb("abT", [2 * NG, TOKENS])
        dt, al, t1, t2, t3, t4 = (sb("dt", [P, 1, NG]), sb("al", [P, 1, NG]), *(sb(f"t{n}", [P, TILES, NG]) for n in (1, 2, 3, 4)))
        def load_first(sp):
            sp.dma_start(w[:], g.d.gdn_w_in[0].rearrange("(p k) n -> p k n", k=KD)[:, :, GDN_A0:GDN_A0 + 2 * NG]).then_inc(landed, 16)
            sp.dma_start(rows[:], g.d.gdn_conv[0].rearrange("j (c p) -> (j c) p", p=P).rearrange("(a r) p -> r a p", a=2)).then_inc(landed, 16)
            sp.dma_start(dt[:, 0], g.d.gdn_dt_bias[0].rearrange("a b -> (a b)").partition_broadcast(P)).then_inc(landed, 16)
            sp.dma_start(al[:, 0], g.d.gdn_a_log[0].rearrange("a b -> (a b)").partition_broadcast(P)).then_inc(landed, 16)
            load_head_qkv(g, sp, q, w_head, 0)
            sp.dma_start(levels[:], g.d.c_levels).then_inc(q.levels_in, 16)
            load_head_z(g, sp, q, w_head, 0)

        modulate(nc, g, sem, 1, 0, range(TILES), False, load_first)
        ps = c.enter_context(nc.psum_tensor("gg_ps", [P, 8, BANK], F32))
        block = c.enter_context(nc.Block())
        shape = [P, TILES, NG]

        @block.tensor
        def _(pe):
            pe.wait_ge(landed, 64)
            for a in range(2):
                last = nc.tensor.transpose(ps[:, 6, a * 80:(a + 1) * 80], rows[:, a], g.ident[0:80, 0:80])
            last.then_inc(turned, 1)
            for bank, lo, hi in ((1, 0, BANK), (2, BANK, TOKENS)):
                for k in range(KD):
                    last = nc.tensor.matmul(ps[0:2 * NG, bank, 0:hi - lo], w[:, k], g.hT[:, k, lo:hi],
                                            start=(k == 0), stop=(k == KD - 1))
            last.then_inc(abT_done, 1)
            pe.wait_ge(abT_copied, 1)
            for t in range(TILES):
                last = nc.tensor.transpose(ps[:, 0, t * 2 * NG:(t + 1) * 2 * NG], abT[:, t * P:(t + 1) * P],
                                           g.ident[0:2 * NG, 0:2 * NG])
            last.then_inc(ab, 1)

        @block.scalar
        def _(act):
            act.wait_ge(turned, 1)
            nc.scalar.activation(conv, ps[:, 6, 0:160], ACT.Copy)
            act.wait_ge(abT_done, 1)
            nc.scalar.activation(abT[:], ps[0:2 * NG, 1:3].rearrange("p a b -> p (a b)")[:, 0:TOKENS], ACT.Copy).then_inc(abT_copied, 1)
            act.wait_ge(ab, 1)
            abp = ps[:, 0, 0:TILES * 2 * NG].rearrange("p (t n) -> p t n", t=TILES)
            nc.scalar.activation(gates[:, 1], abp[:, :, NG:], ACT.Sigmoid).then_inc(copied, 1)
            act.wait_ge(arg1, 1)
            nc.scalar.activation(t2[:], t2[:], ACT.Exp)
            nc.scalar.activation(al[:], al[:], ACT.Exp).then_inc(exp1, 1)

        @block.vector
        def _(dve):
            own = Own(dve, own_sem)
            dve.wait_ge(landed, 64)
            dve.wait_ge(copied, 1)
            abp = ps[:, 0, 0:TILES * 2 * NG].rearrange("p (t n) -> p t n", t=TILES)
            own(nc.vector.tensor_tensor(t1[:], abp[:, :, 0:NG], bc(dt[:], shape), ALU.add))
            nc.vector.scalar_tensor_tensor(out=t2[:], in0=t1[:], scalar=-1.0, in1=t1[:], op0=ALU.mult, op1=ALU.min).then_inc(arg1, 1)
            dve.wait_ge(exp1, 1)
            own(nc.vector.tensor_scalar(t3[:], t2[:], 2.0, None, ALU.add))
            own(nc.vector.reciprocal(t3[:], t3[:]))
            own(nc.vector.tensor_tensor(t2[:], t2[:], t3[:], ALU.mult))
            own(nc.vector.tensor_tensor(t4[:], t2[:], t2[:], ALU.mult))
            own(nc.vector.tensor_scalar(t3[:], t4[:], 1.0 / 17, None, ALU.mult))
            for odd in range(15, 1, -2):
                own(nc.vector.scalar_tensor_tensor(out=t3[:], in0=t3[:], scalar=1.0 / odd, in1=t4[:], op0=ALU.add, op1=ALU.mult))
            own(nc.vector.scalar_tensor_tensor(out=t2[:], in0=t3[:], scalar=1.0, in1=t2[:], op0=ALU.add, op1=ALU.mult))
            own(nc.vector.tensor_scalar(t1[:], t1[:], 0.0, None, ALU.max))
            own(nc.vector.scalar_tensor_tensor(out=t1[:], in0=t2[:], scalar=2.0, in1=t1[:], op0=ALU.mult, op1=ALU.add))
            own(nc.vector.scalar_tensor_tensor(out=gates[:, 0], in0=t1[:], scalar=-1.0, in1=bc(al[:], shape),
                                               op0=ALU.mult, op1=ALU.mult))


def gated_deltanet(nc, g, sem, o_tok):
    names = ("w_in wz_in cin_copied conved silued projected z_done z_copied v_turned v_copied squared ssq ss_read rooted "
             "normed k_turned k_copied kk_prod kk_read gcol_set gsum gsum_read gates_exp gates_done "
             "g_prod d_arg d_exp mt_done t_turned t_copied x_prod x_masked p_prod tt_done "
             "ks_done r_done oq_done y_done v_scaled kv_done s_done o_done z_kept own_v levels_in cin_zeroed")
    q = named("Semaphores", **{n: sem("gd_" + n) for n in names.split()})
    with nc.sbuf_tensor("gdn_gates", [P, 2, TILES, 2 * HV], F32) as gates, \
            nc.sbuf_tensor("gdn_conv", [P, 160], F32) as conv, \
            nc.sbuf_tensor("gdn_w", [P, KD, 6 * P], F32) as w, \
            nc.sbuf_tensor("gdn_levels", [P, LEVELS, 2, P], F32) as levels:
        gdn_gates(nc, g, sem, gates, conv[:], q, w, levels)
        gdn_heads(nc, g, sem, o_tok, gates, conv, q, w, levels)


def gdn_heads(nc, g, sem, o_tok, gates, conv, q, w, levels):
    NCH = 4
    LAT = LAT_TILES * P
    CIN = TOKENS + 6
    with ExitStack() as c:
        sb = lambda name, shape: c.enter_context(nc.sbuf_tensor("gd_" + name, shape, F32))
        taps = sb("taps", [P, CONV_W, NCH])
        cin, cout = sb("cin", [P, 2, CIN]), sb("cout", [P, 2, CIN - 4])
        kT, qT, k_tok, v_tok = sb("kT", [P, TOKENS]), sb("qT", [P, LAT]), sb("k_tok", [P, TILES, P]), sb("v_tok", [P, TILES, 2, P])
        z = sb("z", [P, LAT_TILES, 2 * P])
        kk, kq = sb("kk", [P, 2, TILES, P]), sb("kq", [P, 2, LAT_TILES, P])
        NC = 4 * TILES
        gsel, gall = sb("gsel", [P, 2, NC]), sb("gall", [P, 3, NC])
        gc, neg_eg, beta_el = sb("gc", [P, NC]), sb("neg_eg", [P, NC]), sb("beta_el", [P, NC])
        dx, tm = sb("dx", [P, 4, BANK]), sb("tm", [P, 4, BANK])
        Dm, X, T, M = [dx[:, s] for s in (0, 1)], [dx[:, s] for s in (2, 3)], [tm[:, s] for s in (0, 1)], [tm[:, s] for s in (2, 3)]
        TT, attn = sb("TT", [P, 2, 2, BANK]), sb("attn", [P, 2, 2, BANK])
        R, V2, Vn, oq, S = (sb(n, [P, BANK]) for n in ("R", "V2", "Vn", "oq", "S"))
        vx = dx[:].rearrange("p a b -> p (a b)")
        sq = tm[:].rearrange("p a b -> p (a b)")
        vx = [vx[:, 0:TOKENS], vx[:, TOKENS:2 * TOKENS]]
        sq = [sq[:, 0:TOKENS], sq[:, TOKENS:TOKENS + LAT]]
        ps = c.enter_context(nc.psum_tensor("gd_ps", [P, 8, BANK], F32))
        block = c.enter_context(nc.Block())

        ch = lambda ap, n: ap[:, n * P:(n + 1) * P]
        chains = [(dr, v, dr * 2 + v) for dr in range(2) for v in range(2)]
        four = lambda ap: ap.rearrange("p (d v n) -> p d v n", d=2, v=2)
        perdir = lambda ap: bc(ap.unsqueeze(2), [P, 2, 2, P])

        def g_bank(pair, s):
            return 3 * s + 2 if pair else 2 + s

        def col(ap, dr, t, v):
            n = dr * 2 * TILES + t * 2 + v
            return ap[:, n:n + 1]

        @block.sync
        def _(sp):
            with sp.Fori(0, HK - 1) as i:
                sp.wait_ge(q.projected, i * NCH + NCH)
                load_head_qkv(g, sp, q, w, i + 1)
                sp.wait_ge(q.z_done, i * LAT_TILES + LAT_TILES)
                load_head_z(g, sp, q, w, i + 1)

        @block.tensor
        def _(pe):
            def project(i, ct):
                    if ct == 0:
                        pe.wait_ge(q.w_in, i * 48 + 48)
                    if ct >= 2:
                        pe.wait_ge(q.cin_copied, i * NCH + (ct - 1))
                    b = 2 * (ct % 2)
                    for bank, lo, hi in ((b, 0, CTX_LEN), (b + 1, CTX_LEN, TOKENS)):
                        if ct == 1 and lo == 0:
                            continue
                        for k in range(KD):
                            last = nc.tensor.matmul(ps[:, bank, 0:hi - lo], w[:, k, ct * P:(ct + 1) * P],
                                                    g.hT[:, k, lo:hi], start=(k == 0), stop=(k == KD - 1))
                    last.then_inc(q.projected, 1)

            def back(i, more):
                def project_z(lt):
                    if lt >= 2:
                        pe.wait_ge(q.z_copied, i * LAT_TILES + (lt - 1))
                    t = lt + CTX_TILES
                    for k in range(KD):
                        last = nc.tensor.matmul(ps[:, 4 + lt % 2, 0:2 * P], g.hT[:, k, t * P:(t + 1) * P],
                                                w[:, k, 4 * P:6 * P], start=(k == 0), stop=(k == KD - 1))
                    last.then_inc(q.z_done, 1)

                def turn_six(src, done):
                    for t in range(TILES):
                        last = nc.tensor.transpose(ps[:, 6 + t // 4, (t % 4) * P:(t % 4 + 1) * P],
                                                   src[:, t * P:(t + 1) * P], g.ident[:])
                    last.then_inc(done, 1)

                def decays(pair, s):
                    n = 2 * pair + s
                    for dr, v, a in chains:
                        t = step_tiles(n)[dr]
                        last = nc.tensor.matmul(ch(ps[:, g_bank(pair, s)], a), bc(col(gsel[:, 0], dr, t, v), [P, P]),
                                                g.upper[:, 2 * dr], start=True, stop=True)
                    last.then_inc(q.g_prod, 1)

                def turn_t(s, done, pair):
                    for _, _, a in chains:
                        last = nc.tensor.transpose(ch(ps[:, 3 * s + 2], a), ch(TT[:, pair % 2, s], a), g.ident[:])
                    last.then_inc(q.t_turned, 1)

                def state_qk(n):
                    if n >= 1:
                        pe.wait_ge(q.s_done, i * STEPS + n)
                        for dr, v, a in chains:
                            t = step_tiles(n)[dr]
                            last = nc.tensor.matmul(ch(ps[:, 6], a), kT[:, t * P:(t + 1) * P], ch(S, a), start=True, stop=True)
                    if n >= CTX_TILES:
                        if n > CTX_TILES:
                            pe.wait_ge(q.o_done, i * LAT_TILES + (n - CTX_TILES))
                        for dr, v, a in chains:
                            t = step_tiles(n)[dr] - CTX_TILES
                            last = nc.tensor.matmul(ch(ps[:, 7], a), qT[:, t * P:(t + 1) * P], ch(S, a), start=True, stop=True)
                    if n >= 1:
                        last.then_inc(q.ks_done, 1)

                def state_y(n):
                    pair, s = divmod(n, 2)
                    if n >= 1:
                        pe.wait_ge(q.r_done, i * (STEPS - 1) + n)
                    for dr, v, a in chains:
                        rhs = ch(R, a) if n >= 1 else v_tok[:, step_tiles(n)[dr], v]
                        last = nc.tensor.matmul(ch(ps[:, 6], a), ch(TT[:, pair % 2, s], a), rhs, start=True, stop=True)
                    last.then_inc(q.y_done, 1)

                def state_kv(n):
                    pair, s = divmod(n, 2)
                    pe.wait_ge(q.v_scaled, i * STEPS + (n + 1))
                    for dr, v, a in chains:
                        last = nc.tensor.matmul(ch(ps[:, 6], a), k_tok[:, step_tiles(n)[dr]], ch(V2, a), start=True, stop=True)
                    if n >= CTX_TILES:
                        pe.wait_ge(q.oq_done, i * LAT_TILES + (n - CTX_TILES + 1))
                        for dr, v, a in chains:
                            last = nc.tensor.matmul(ch(ps[:, 7], a), ch(attn[:, pair % 2, s], a), ch(Vn, a), start=True, stop=True)
                    last.then_inc(q.kv_done, 1)

                def piece(pair, j):
                    (state_qk, state_y, state_kv)[j % 3](2 * pair + j // 3)

                pe.wait_ge(q.wz_in, i * 16 + 16)
                project_z(0)
                pe.wait_ge(q.squared, i + 1)
                pe.wait_ge(q.cin_copied, i * NCH + NCH)
                nc.tensor.matmul(ps[:, 0], g.ones[:], sq[0][:, 0:BANK], start=True, stop=True)
                nc.tensor.matmul(ps[:, 1, 0:TOKENS - BANK], g.ones[:], sq[0][:, BANK:TOKENS], start=True, stop=True)
                nc.tensor.matmul(ps[:, 2], g.ones[:], sq[1], start=True, stop=True).then_inc(q.ssq, 1)
                pe.wait_ge(q.gcol_set, i + 1)
                half = 2 * TILES
                for dr in range(2):
                    nc.tensor.matmul(ps[:, 3, dr * half:(dr + 1) * half], g.upper[:, 2 * dr],
                                     gsel[:, 0, dr * half:(dr + 1) * half], start=True, stop=True)
                nc.tensor.matmul(ps[:, 3, NC:2 * NC], g.ones[:], gsel[:, 0], start=True, stop=True).then_inc(q.gsum, 1)
                project_z(1)
                for v in range(2):
                    pe.wait_ge(q.silued, i * NCH + (v + 3))
                    if v:
                        pe.wait_ge(q.v_copied, i * 2 + 1)
                    turn_six(vx[v], q.v_turned)
                    project_z(2 + v)
                pe.wait_ge(q.gsum_read, i + 1)
                for s in range(2):
                    decays(0, s)
                pe.wait_ge(q.normed, i + 1)
                pe.wait_ge(q.v_copied, i * 2 + 2)
                turn_six(kT[:], q.k_turned)
                for lt in range(LAT_TILES):
                    t = lt + CTX_TILES
                    nc.tensor.matmul(ch(ps[:, 0], lt), kT[:, t * P:(t + 1) * P], qT[:, lt * P:(lt + 1) * P],
                                     start=True, stop=True)
                pe.wait_ge(q.z_copied, i * LAT_TILES + LAT_TILES)
                for t in range(TILES):
                    last = nc.tensor.matmul(ps[:, 4 + t // 4, (t % 4) * P:(t % 4 + 1) * P], kT[:, t * P:(t + 1) * P],
                                            kT[:, t * P:(t + 1) * P], start=True, stop=True)
                last.then_inc(q.kk_prod, 1)
                pe.wait_ge(q.kk_read, i + 1)
                pe.wait_ge(q.k_copied, i + 1)
                for pair in range(PAIRS):
                    for s in range(2):
                        pe.wait_ge(q.mt_done, i * STEPS + (2 * pair + s + 1))
                        turn_t(s, q.t_turned, pair)
                    for b in range(1, LEVELS):
                        at = (pair * (LEVELS - 1) + b - 1) * 2
                        for s in range(2):
                            pe.wait_ge(q.t_copied, i * (PAIRS * 12) + (at + s + 1))
                            for _, _, a in chains:
                                last = nc.tensor.matmul(ch(ps[:, 3 * s], a), ch(M[s], a), ch(T[s], a), start=True, stop=True)
                            last.then_inc(q.x_prod, 1)
                        if b == LEVELS - 1 and pair + 1 < PAIRS:
                            for s in range(2):
                                decays(pair + 1, s)
                        for s in range(2):
                            pe.wait_ge(q.x_masked, i * (PAIRS * 12) + (at + s + 1))
                            for _, _, a in chains:
                                last = nc.tensor.matmul(ch(ps[:, 3 * s + 1], a), ch(X[s], a), ch(TT[:, pair % 2, s], a),
                                                        start=True, stop=True)
                            last.then_inc(q.p_prod, 1)
                        for s in range(2):
                            if b < LEVELS - 1:
                                pe.wait_ge(q.tt_done, i * (PAIRS * 12) + (at + s + 1))
                                turn_t(s, q.t_turned, pair)
                            if pair and s == 0:
                                piece(pair - 1, b - 1)
                for s in range(2):
                    pe.wait_ge(q.tt_done, i * (PAIRS * 12) + (PAIRS * 12 - 1 + s))
                for j in range(6):
                    piece(PAIRS - 1, j)
                    if more and j in FRONT_AFTER:
                        project(i + 1, FRONT_AFTER.index(j))
                if more:
                    pe.wait_ge(q.s_done, i * STEPS + STEPS)
                    pe.wait_ge(q.o_done, i * LAT_TILES + LAT_TILES)

            for ct in range(NCH):
                project(0, ct)
            with pe.Fori(0, HK - 1) as i:
                back(i, True)
            back(HK - 1, False)

        @block.vector
        def _(dve):
            own = Own(dve, q.own_v)
            nc.vector.memset(cin[:], 0.0).then_inc(q.cin_zeroed, 1)
            dve.wait_ge(q.levels_in, 16)

            def set_taps(i):
                cw = conv[:].rearrange("p (j c) -> p j c", j=CONV_W)
                for at, first, size in ((0, GDN_KEY // P, 1), (1, 0, 1), (2, 2 * GDN_KEY // P, 2)):
                    own(nc.vector.tensor_copy(taps[:, :, at:at + size], cw[:, :, ds(i * size + first, size)]))

            def convolve(i, ct):
                dve.wait_ge(q.cin_copied, i * NCH + (ct + 1))
                if ct >= 2:
                    dve.wait_ge(q.silued, i * NCH + (ct - 1))
                lo = CTX_LEN + 2 if ct == 1 else 0
                n = CIN - 4
                src, dst = cin[:, ct % 2], cout[:, ct % 2, lo:n]
                own(nc.vector.tensor_scalar(dst, src[:, lo:n], taps[:, 0, ct:ct + 1], None, ALU.mult))
                for j in range(1, CONV_W):
                    ins = nc.vector.scalar_tensor_tensor(out=dst, in0=src[:, lo + j:n + j], scalar=taps[:, j, ct:ct + 1],
                                                         in1=dst, op0=ALU.mult, op1=ALU.add)
                    if j < CONV_W - 1:
                        own(ins)
                ins.then_inc(q.conved, 1)

            def back(i, more):
                def decay_args(pair, s):
                    n = 2 * pair + s
                    dve.wait_ge(q.g_prod, i * STEPS + (n + 1))
                    for dr, v, a in chains:
                        t = step_tiles(n)[dr]
                        ins = nc.vector.tensor_scalar(ch(Dm[s], a), ch(ps[:, g_bank(pair, s)], a), col(gc, dr, t, v), 0.0,
                                                      ALU.subtract, ALU.min)
                    ins.then_inc(q.d_arg, 1)

                for kind in range(2):
                    for dr in range(2):
                        src = gates[:, kind].rearrange("p t (d h) -> p t d h", d=2)[:, :, dr, ds(i * 2, 2)]
                        dst = gsel[:, kind, dr * 2 * TILES:(dr + 1) * 2 * TILES].rearrange("p (t v) -> p t v", v=2)
                        own(nc.vector.tensor_copy(dst, src))
                dve.sem_inc(q.gcol_set, 1)
                dve.wait_ge(q.ssq, i + 1)
                own.mark(nc.vector.tensor_scalar(sq[0], ps[:, 0:2].rearrange("p a b -> p (a b)")[:, 0:TOKENS], NORM_EPS, None, ALU.add))
                own(nc.vector.tensor_scalar(sq[1], ps[:, 2], NORM_EPS, None, ALU.add))
                dve.sem_inc(q.ss_read, 1)
                dve.wait_ge(q.gsum, i + 1)
                own.mark(nc.vector.tensor_copy(gc[:], ps[:, 3, 0:NC]))
                own(nc.vector.tensor_copy(gall[:, 2], ps[:, 3, NC:2 * NC]))
                own.mark(nc.vector.tensor_copy(gall[:, 0], gc[:]))
                own(nc.vector.tensor_tensor(gall[:, 1], gall[:, 2], gc[:], ALU.subtract))
                dve.sem_inc(q.gsum_read, 1)
                dve.wait_ge(q.rooted, i + 1)
                own.mark(nc.vector.reciprocal(sq[0], sq[0]))
                own(nc.vector.reciprocal(sq[1], sq[1]))
                own(nc.vector.tensor_tensor(kT[:], kT[:], sq[0], ALU.mult))
                nc.vector.scalar_tensor_tensor(out=qT[:], in0=qT[:], scalar=DH ** -0.5, in1=sq[1],
                                               op0=ALU.mult, op1=ALU.mult).then_inc(q.normed, 1)
                dve.wait_ge(q.gates_exp, i + 1)
                own.mark(nc.vector.tensor_scalar(neg_eg[:], gall[:, 0], -1.0, None, ALU.mult))
                own(nc.vector.tensor_tensor(beta_el[:], gall[:, 1], gsel[:, 1], ALU.mult))
                dve.sem_inc(q.gates_done, 1)
                for s in range(2):
                    decay_args(0, s)
                dve.wait_ge(q.kk_prod, i + 1)
                kk_ps = ps[:, 4:6].rearrange("p a b -> p (a b)")[:, 0:TILES * P].rearrange("p (t n) -> p t n", n=P)
                kq_ps = ps[:, 0].rearrange("p (t n) -> p t n", n=P)
                for dr in range(2):
                    own.mark(nc.vector.tensor_tensor(kk[:, dr], kk_ps, bc(g.upper[:, 2 * dr + 1:2 * dr + 2], [P, TILES, P]), ALU.mult))
                    own(nc.vector.tensor_tensor(kq[:, dr], kq_ps, bc(g.upper[:, 2 * dr:2 * dr + 1], [P, LAT_TILES, P]), ALU.mult))
                dve.sem_inc(q.kk_read, 1)

                def matrices(pair, s):
                    n = 2 * pair + s
                    tt = TT[:, pair % 2, s]
                    dve.wait_ge(q.d_exp, i * STEPS + (n + 1))
                    for dr, v, a in chains:
                        t = step_tiles(n)[dr]
                        ins = nc.vector.scalar_tensor_tensor(out=ch(M[s], a), in0=ch(Dm[s], a), scalar=col(gsel[:, 1], dr, t, v),
                                                             in1=kk[:, dr, t], op0=ALU.mult, op1=ALU.mult)
                        own.mark(ins)
                    own.wait()
                    own(nc.vector.tensor_tensor(four(tt), four(M[s]), perdir(levels[:, 0]), ALU.mult))
                    nc.vector.tensor_tensor(tt.rearrange("p (a n) -> p a n", n=P), bc(g.ident[:].unsqueeze(1), [P, 4, P]),
                                            tt.rearrange("p (a n) -> p a n", n=P), ALU.subtract).then_inc(q.mt_done, 1)

                def attention(pair, s):
                    n = 2 * pair + s
                    if n >= CTX_TILES:
                        for dr in range(2):
                            t = step_tiles(n)[dr] - CTX_TILES
                            half = slice(dr * 2 * P, (dr + 1) * 2 * P)
                            dst = attn[:, pair % 2, s, half].rearrange("p (v n) -> p v n", v=2)
                            own.mark(nc.vector.tensor_tensor(dst, Dm[s][:, half].rearrange("p (v n) -> p v n", v=2),
                                                             bc(kq[:, dr, t:t + 1], [P, 2, P]), ALU.mult))
                    own.wait()

                def state_r(n):
                    if n == 0:
                        return
                    dve.wait_ge(q.ks_done, i * (STEPS - 1) + n)
                    for dr, v, a in chains:
                        t = step_tiles(n)[dr]
                        ins = nc.vector.scalar_tensor_tensor(out=ch(R, a), in0=ch(ps[:, 6], a), scalar=col(neg_eg, dr, t, v),
                                                             in1=v_tok[:, t, v], op0=ALU.mult, op1=ALU.add)
                    ins.then_inc(q.r_done, 1)

                def state_s(n):
                    dve.wait_ge(q.kv_done, i * STEPS + (n + 1))
                    if n == 0:
                        nc.vector.tensor_copy(S[:], ps[:, 6]).then_inc(q.s_done, 1)
                        return
                    dve.wait_ge(q.s_done, i * STEPS + n)
                    for dr, v, a in chains:
                        t = step_tiles(n)[dr]
                        ins = nc.vector.scalar_tensor_tensor(out=ch(S, a), in0=ch(S, a), scalar=col(gall[:, 2], dr, t, v),
                                                             in1=ch(ps[:, 6], a), op0=ALU.mult, op1=ALU.add)
                    ins.then_inc(q.s_done, 1)

                def state_o(n):
                    if n < CTX_TILES:
                        return
                    for dr in range(2):
                        t = step_tiles(n)[dr] - CTX_TILES
                        half = slice(dr * 2 * P, (dr + 1) * 2 * P)
                        dst = o_tok[:, t, ds(i * (2 * P), 2 * P)]
                        again = n >= CTX_TILES + LAT_TILES // 2
                        if again:
                            own(nc.vector.tensor_tensor(dst, dst, oq[:, half], ALU.add))
                        ins = nc.vector.tensor_tensor(dst, ps[:, 7, half], dst if again else oq[:, half], ALU.add)
                        own.mark(ins)
                    own.wait()
                    dve.sem_inc(q.o_done, 1)

                def piece(pair, j):
                    n = 2 * pair + j // 3
                    if j % 3 == 0:
                        state_r(n)
                    if j % 3 == 2:
                        state_s(n)
                        state_o(n)

                for s in range(2):
                    matrices(0, s)
                for pair in range(PAIRS):
                    for b in range(1, LEVELS):
                        at = (pair * (LEVELS - 1) + b - 1) * 2
                        for s in range(2):
                            dve.wait_ge(q.x_prod, i * (PAIRS * 12) + (at + s + 1))
                            nc.vector.tensor_tensor(four(X[s]), four(ps[:, 3 * s]), perdir(levels[:, b]),
                                                    ALU.mult).then_inc(q.x_masked, 1)
                        if b == LEVELS - 1 and pair + 1 < PAIRS:
                            for s in range(2):
                                decay_args(pair + 1, s)
                        for s in range(2):
                            dve.wait_ge(q.p_prod, i * (PAIRS * 12) + (at + s + 1))
                            tt = TT[:, pair % 2, s]
                            nc.vector.tensor_tensor(tt, tt, ps[:, 3 * s + 1], ALU.subtract).then_inc(q.tt_done, 1)
                        if b == LEVELS - 1 and pair + 1 < PAIRS:
                            if pair:
                                dve.wait_ge(q.y_done, i * STEPS + 2 * pair)
                            for s in range(2):
                                matrices(pair + 1, s)
                        if pair:
                            piece(pair - 1, b - 1)
                        if b == LEVELS - 1 and pair + 1 < PAIRS:
                            for s in range(2):
                                attention(pair + 1, s)
                if more:
                    set_taps(i + 1)
                for j in range(6):
                    piece(PAIRS - 1, j)
                    if more and j in FRONT_AFTER:
                        convolve(i + 1, FRONT_AFTER.index(j))

            set_taps(0)
            for ct in range(NCH):
                convolve(0, ct)
            with dve.Fori(0, HK - 1) as i:
                own.enter(i, DVE_PER_HEAD)
                back(i, True)
            own.leave(HK - 1)
            back(HK - 1, False)

        @block.scalar
        def _(act):
            act.wait_ge(q.cin_zeroed, 1)
            act.dma_start(z[:, 0, 0:P], g.d.c_ident).then_inc(q.z_kept, 16)

            def copy_in(i, ct):
                act.wait_ge(q.projected, i * NCH + (ct + 1))
                if ct >= 2:
                    act.wait_ge(q.conved, i * NCH + (ct - 1))
                b = 2 * (ct % 2)
                if ct != 1:
                    nc.scalar.activation(cin[:, ct % 2, 2:2 + CTX_LEN], ps[:, b, 0:CTX_LEN], ACT.Copy)
                nc.scalar.activation(cin[:, ct % 2, CTX_LEN + 4:CTX_LEN + 4 + LAT], ps[:, b + 1],
                                     ACT.Copy).then_inc(q.cin_copied, 1)

            def silu(i, ct):
                act.wait_ge(q.conved, i * NCH + (ct + 1))
                dst = (kT, qT, vx[0], vx[1])[ct]
                src = cout[:, ct % 2]
                if ct != 1:
                    nc.scalar.activation(dst[:, 0:CTX_LEN], src[:, 0:CTX_LEN], ACT.Silu)
                    dst = dst[:, CTX_LEN:TOKENS]
                nc.scalar.activation(dst[:, 0:LAT], src[:, CTX_LEN + 2:CTX_LEN + 2 + LAT], ACT.Silu).then_inc(q.silued, 1)

            def square(i):
                act.wait_ge(q.silued, i * NCH + 2)
                nc.scalar.activation(sq[0], kT[:], ACT.Square)
                nc.scalar.activation(sq[1], qT[:], ACT.Square).then_inc(q.squared, 1)

            parts = {0: [(copy_in, 0)], 1: [(copy_in, 1)], 3: [(silu, 0), (copy_in, 2)],
                     4: [(silu, 1), (square,)], 5: [(copy_in, 3), (silu, 2), (silu, 3)]}

            def front(i, j):
                for part, *ct in parts.get(j, []):
                    part(i, *ct)

            def back(i, more):
                def silu_z(lt):
                    act.wait_ge(q.z_done, i * LAT_TILES + (lt + 1))
                    if lt == 0:
                        act.wait_ge(q.z_kept, i * 16 + 16)
                    nc.scalar.activation(z[:, lt], ps[:, 4 + lt % 2, 0:2 * P], ACT.Silu).then_inc(q.z_copied, 1)

                def copy_v(v):
                    act.wait_ge(q.v_turned, i * 2 + (v + 1))
                    nc.scalar.activation(v_tok[:, 0:4, v], ps[:, 6].rearrange("p (t n) -> p t n", n=P), ACT.Copy)
                    nc.scalar.activation(v_tok[:, 4:6, v], ps[:, 7, 0:2 * P].rearrange("p (t n) -> p t n", n=P),
                                         ACT.Copy).then_inc(q.v_copied, 1)

                silu_z(0)
                act.wait_ge(q.ss_read, i + 1)
                nc.scalar.activation(sq[0], sq[0], ACT.Sqrt)
                nc.scalar.activation(sq[1], sq[1], ACT.Sqrt).then_inc(q.rooted, 1)
                silu_z(1)
                copy_v(0)
                silu_z(2)
                act.wait_ge(q.gsum_read, i + 1)
                nc.scalar.activation(gall[:], gall[:], ACT.Exp).then_inc(q.gates_exp, 1)
                copy_v(1)
                silu_z(3)
                act.wait_ge(q.z_copied, i * LAT_TILES + LAT_TILES)
                act.dma_start(g.z_d[:, :, ds(i * (2 * P), 2 * P)], z[:]).then_inc(q.z_kept, 16)
                act.wait_ge(q.k_turned, i + 1)
                nc.scalar.activation(k_tok[:, 0:4], ps[:, 6].rearrange("p (t n) -> p t n", n=P), ACT.Copy)
                nc.scalar.activation(k_tok[:, 4:6], ps[:, 7, 0:2 * P].rearrange("p (t n) -> p t n", n=P),
                                     ACT.Copy).then_inc(q.k_copied, 1)
                act.wait_ge(q.gates_done, i + 1)

                def copy_t(s, at):
                    act.wait_ge(q.t_turned, i * (PAIRS * 12) + (at + s + 1))
                    nc.scalar.activation(T[s], ps[:, 3 * s + 2], ACT.Copy).then_inc(q.t_copied, 1)

                def state_oq(n):
                    if n < CTX_TILES:
                        return
                    act.wait_ge(q.ks_done, i * (STEPS - 1) + n)
                    if n > CTX_TILES:
                        act.wait_ge(q.o_done, i * LAT_TILES + (n - CTX_TILES))
                    for dr, v, a in chains:
                        t = step_tiles(n)[dr]
                        ins = nc.scalar.activation(ch(oq, a), ch(ps[:, 7], a), ACT.Copy, scale=col(gall[:, 0], dr, t, v))
                    ins.then_inc(q.oq_done, 1)

                def state_v(n):
                    act.wait_ge(q.y_done, i * STEPS + (n + 1))
                    for dr, v, a in chains:
                        t = step_tiles(n)[dr]
                        if n >= CTX_TILES:
                            nc.scalar.activation(ch(Vn, a), ch(ps[:, 6], a), ACT.Copy, scale=col(gsel[:, 1], dr, t, v))
                        ins = nc.scalar.activation(ch(V2, a), ch(ps[:, 6], a), ACT.Copy, scale=col(beta_el, dr, t, v))
                    ins.then_inc(q.v_scaled, 1)

                def piece(pair, j):
                    n = 2 * pair + j // 3
                    if j % 3 == 0:
                        state_oq(n)
                    if j % 3 == 1:
                        state_v(n)

                def exponentiate(pair):
                    for s in range(2):
                        act.wait_ge(q.d_arg, i * STEPS + (2 * pair + s + 1))
                        nc.scalar.activation(Dm[s], Dm[s], ACT.Exp).then_inc(q.d_exp, 1)

                exponentiate(0)
                for pair in range(PAIRS):
                    for b in range(0, LEVELS):
                        if b == LEVELS - 1 and pair + 1 < PAIRS:
                            exponentiate(pair + 1)
                        if b < LEVELS - 1:
                            for s in range(2):
                                copy_t(s, (pair * (LEVELS - 1) + b) * 2)
                        if pair and b:
                            piece(pair - 1, b - 1)
                for j in range(6):
                    piece(PAIRS - 1, j)
                    if more:
                        front(i + 1, j)

            for j in range(6):
                front(0, j)
            with act.Fori(0, HK - 1) as i:
                back(i, True)
            back(HK - 1, False)
            act.wait_ge(q.z_kept, 16 * HK + 16)


DVE_PER_HEAD = 88
@contextmanager
def semaphores(nc):
    taken = []

    def sem(name):
        taken.append(nc.alloc_semaphore(name=name))
        return taken[-1]

    yield sem
    nc.clear_and_free_semaphores(taken)
    nc.all_engine_barrier()


def build_program(nc, d, out, stages=None):
    on = lambda s: stages is None or s in stages
    with ExitStack() as c:
        sb = lambda name, shape: c.enter_context(nc.sbuf_tensor(name, shape, F32))
        dram = lambda name, shape, dt: nc.dram_tensor(name, shape, dt, kind="Internal").ap()
        g = Core()
        g.d = d
        g.mod_d = dram("mod_d", (2, DEPTH * ADA * D), F32)
        g.h_d = dram("h_d", (TOKENS + P, D), F32)
        g.acc_d = dram("acc_d", (TOKENS + P, D), F32)
        g.z_d = dram("z_d", (P, LAT_TILES, GDN_VAL), F32)
        g.x = sb("x_res", [P, TILES, D])
        g.ident, g.ones, g.upper = sb("ident", [P, P]), sb("ones", [P, P]), sb("upper", [P, 4, P])
        g.subln, g.gdn_gain, g.neg_lam = sb("subln", [P, P]), sb("gdn_gain", [P, P]), sb("neg_lam", [P, 1])
        with semaphores(nc) as sem:
            first_stage(nc, g, sem)
        if on("attn"):
            with semaphores(nc) as sem, nc.sbuf_tensor("da_o", [P, TILES, D], F32) as o_tok:
                with nc.sbuf_tensor("hT_a", [P, KD, TOKENS], F32) as g.hT:
                    diff_attention(nc, g, sem, o_tok)
                project_out(nc, g, sem, 0, d.da_w_o[0], DA_HEADS, o_tok, None, g.subln[:], range(TILES))
        if on("moe0"):
            with semaphores(nc) as sem:
                moe(nc, g, sem, 0, range(TILES))
        if on("gdn"):
            with semaphores(nc) as sem, nc.sbuf_tensor("gdn_o", [P, LAT_TILES, GDN_VAL], F32) as o_tok:
                with nc.sbuf_tensor("hT_b", [P, KD, TOKENS], F32) as g.hT:
                    gated_deltanet(nc, g, sem, o_tok)
                project_out(nc, g, sem, 1, d.gdn_w_o[0], HV, o_tok, g.z_d, g.gdn_gain[:], range(CTX_TILES, TILES))
        if on("moe1"):
            with semaphores(nc) as sem:
                moe(nc, g, sem, 1, range(CTX_TILES, TILES))
        with nc.semaphore("out_stored") as stored, nc.Block() as block:
            @block.sync
            def _(sp):
                sp.dma_start(out[0].rearrange("(t p) n -> p t n", p=P), g.x[:, CTX_TILES:]).then_inc(stored, 16)
                sp.wait_ge(stored, 16)


def empty_slots():
    n = slots(range(TILES)) * P
    return np.stack([TOKENS + np.arange(n) % P, np.zeros(n)], 1).astype(np.int32)


def constants():
    i = np.arange(P)
    n_freq = DA_DIM // 4
    inv = 1.0 / (10000.0 ** (np.arange(n_freq, dtype=np.float32) / n_freq))
    tok = np.arange(SEQ)
    ang = np.concatenate([(tok // 64)[:, None] * inv, (tok % 64)[:, None] * inv], -1).astype(np.float32)
    cos, sin = np.cos(ang), np.sin(ang)
    tiled = lambda a: np.ascontiguousarray(a.reshape(LAT_TILES, P, -1).transpose(1, 0, 2)).astype(np.float32)
    upper = np.stack([i[:, None] <= i, i[:, None] < i, i[:, None] >= i, i[:, None] > i], 1)
    def level(b):
        pair, half = i // (2 * b), (i // b) % 2
        same = pair[:, None] == pair
        fwd = same & (half[:, None] == 1) & (half == 0)
        return np.stack([fwd, fwd.T], 0)
    levels = np.stack([level(2 ** n) for n in range(7)], 0)
    levels[0] = levels[0].transpose(0, 2, 1)
    return {
        "c_ident": np.eye(P, dtype=np.float32), "c_ones": np.ones((P, P), np.float32),
        "c_upper": upper.astype(np.float32),
        "c_cos": tiled(np.concatenate([cos, cos], -1)), "c_sin": tiled(np.concatenate([-sin, sin], -1)),
        "c_levels": np.ascontiguousarray(levels.transpose(2, 0, 1, 3)).astype(np.float32),
        "c_ranks": np.broadcast_to(np.arange(1, TOP_K + 1, dtype=np.float32)[None, :, None], (P, TOP_K, E)).copy(),
        "c_index": i[:, None].astype(np.float32),
        "c_empty": empty_slots(),
        "c_tokens": (i[:, None] + P * np.arange(TILES)[None]).astype(np.int32),
    }


INS = ["x", "c", "ctx", "c_ctx", "ada_w", "ada_b", "ln_g", "ln_b", "da_w_in", "da_w_o", "da_lambda", "da_subln",
       "gdn_w_in", "gdn_conv", "gdn_a_log", "gdn_dt_bias", "gdn_norm", "gdn_w_o",
       "moe_router", "moe_router_b", "moe_w_gu", "moe_w_dn", "moe_ws_gu", "moe_ws_dn"]


def kernel(**inputs):
    import concourse.bacc as bacc
    from concourse.bass_utils import run_bass_kernel_spmd as run

    nc = bacc.Bacc("TRN2", target_bir_lowering=False, num_devices=1)
    arrays, aps = {}, {}
    given = {name: inputs[name] for name in INS}
    given.update(constants())
    for name, a in given.items():
        a = np.ascontiguousarray(a)
        arrays[f"in_{name}"] = a
        aps[name] = nc.dram_tensor(f"in_{name}", a.shape, mybir.dt.from_np(a.dtype), kind="ExternalInput").ap()
    out = nc.dram_tensor("out_0", (1, SEQ, D), F32, kind="ExternalOutput").ap()
    build_program(nc, named("Inputs", **aps), out)
    r = run(nc, [arrays], core_ids=[0])
    return r.results[0]["out_0"]
```
